# Optimizing a Trainium2 kernel written in Bass

```python
import math, functools
import jax, jax.numpy as jnp
from jax import lax
import numpy as np

'''One inference step of a hybrid streaming encoder layer stack (Hymba-style parallel head groups:
mLSTM matrix memory + differential attention), macaron SwiGLU FFNs, sandwich RMSNorm, adaLN conditioning.
All token mixing is chunk-causal (CHUNK = 64); the mLSTM is per-token causal.

Inputs:
  x_prompt (BATCH, SEQ, D_MODEL), x_sample (DEC_BATCH, DEC_SEQ, D_MODEL)
  cache_k  (DEPTH, DEC_BATCH, PAST_LEN, N_DIFF_HEADS, 2*DIFF_QK_DIM)  rotated keys [k1 | k2]
  cache_v  (DEPTH, DEC_BATCH, PAST_LEN, N_DIFF_HEADS, DIFF_V_DIM)
  state_C  (DEPTH, DEC_BATCH, N_MLSTM_HEADS, MLSTM_V_DIM, MLSTM_QK_DIM)  stabilised matrix memory
  state_n  (DEPTH, DEC_BATCH, N_MLSTM_HEADS, MLSTM_QK_DIM)               stabilised normaliser
  state_m  (DEPTH, DEC_BATCH, N_MLSTM_HEADS)                             running-max stabiliser
  c_prompt (BATCH, D_MODEL), c_sample (DEC_BATCH, D_MODEL)
  then per-layer weights with leading DEPTH axis.
Output tuple:
  (y_prompt (BATCH,SEQ,D), y_sample (DEC_BATCH,DEC_SEQ,D),
   k_prompt (DEPTH,BATCH,SEQ,HD,2*DQK), v_prompt (DEPTH,BATCH,SEQ,HD,DV),
   C_prompt (DEPTH,BATCH,HM,MV,MQK), n_prompt (DEPTH,BATCH,HM,MQK), m_prompt (DEPTH,BATCH,HM),
   k_sample (DEPTH,DEC_BATCH,DEC_SEQ,HD,2*DQK), v_sample (DEPTH,DEC_BATCH,DEC_SEQ,HD,DV),
   C_sample (DEPTH,DEC_BATCH,HM,MV,MQK), n_sample (DEPTH,DEC_BATCH,HM,MQK), m_sample (DEPTH,DEC_BATCH,HM))
'''

D_MODEL = 1024
BATCH = 1
SEQ = 512
DEPTH = 1
DEC_BATCH = 8
DEC_SEQ = 16
PAST_LEN = 256

CHUNK = 64
Q_BLOCK = 128
MLSTM_WIDTH = D_MODEL // 2
DIFF_WIDTH = D_MODEL - MLSTM_WIDTH
MLSTM_V_DIM = 128
MLSTM_QK_DIM = MLSTM_V_DIM // 2
N_MLSTM_HEADS = MLSTM_WIDTH // MLSTM_V_DIM
DIFF_V_DIM = 128
DIFF_QK_DIM = DIFF_V_DIM // 2
N_DIFF_HEADS = DIFF_WIDTH // DIFF_V_DIM
ROPE_DIM = DIFF_QK_DIM // 4
ROPE_THETA = 500000.0
D_FF = 2816
N_ADA = 9
NORM_EPS = 1e-6
PROJ_SIZES = (N_MLSTM_HEADS * MLSTM_QK_DIM, N_MLSTM_HEADS * MLSTM_QK_DIM, N_MLSTM_HEADS * MLSTM_V_DIM,
              MLSTM_WIDTH, N_MLSTM_HEADS, N_MLSTM_HEADS,
              N_DIFF_HEADS * 2 * DIFF_QK_DIM, N_DIFF_HEADS * 2 * DIFF_QK_DIM, N_DIFF_HEADS * DIFF_V_DIM)
PROJ_WIDTH = (3 * N_MLSTM_HEADS * MLSTM_QK_DIM + N_MLSTM_HEADS * MLSTM_V_DIM + MLSTM_WIDTH + 2 * N_MLSTM_HEADS
              + 4 * N_DIFF_HEADS * DIFF_QK_DIM + N_DIFF_HEADS * DIFF_V_DIM) - N_MLSTM_HEADS * MLSTM_QK_DIM

kernel_name = 'hybrid_mlstm_diffattn_streaming_step'

def rms_norm(x, g):
    xf = x.astype(jnp.float32)
    y = xf * lax.rsqrt(jnp.mean(xf * xf, axis=-1, keepdims=True) + NORM_EPS)
    return (y * g.astype(jnp.float32)).astype(x.dtype)

def modulate(x, g, shift, scale):
    return rms_norm(x, g) * (1 + scale[:, None, :]) + shift[:, None, :]

def residual(x, out, g, gate, weight):
    return x + weight * gate[:, None, :] * rms_norm(out, g)

def swiglu(h, w_in, w_out):
    gate, up = jnp.split(h @ w_in, 2, axis=-1)
    return (jax.nn.silu(gate) * up) @ w_out

def ada_params(c, w_ada, b_ada):
    mod = jax.nn.silu(c) @ w_ada + b_ada
    return mod.reshape(c.shape[0], N_ADA, D_MODEL)

def partial_rope(x, pos):
    half = ROPE_DIM // 2
    inv_freq = ROPE_THETA ** (-jnp.arange(half, dtype=jnp.float32) * (2.0 / ROPE_DIM))
    ang = pos.astype(jnp.float32)[:, None] * inv_freq[None, :]
    cos = jnp.cos(ang)[None, :, None, None, :]
    sin = jnp.sin(ang)[None, :, None, None, :]
    xr = x[..., :ROPE_DIM].astype(jnp.float32)
    x1, x2 = xr[..., :half], xr[..., half:]
    rot = jnp.concatenate([x1 * cos - x2 * sin, x2 * cos + x1 * sin], axis=-1).astype(x.dtype)
    return jnp.concatenate([rot, x[..., ROPE_DIM:]], axis=-1)

def project(h, w_in, b_igate, b_fgate, pos):
    B, T, _ = h.shape
    f32 = jnp.float32
    idx = [int(i) for i in np.cumsum(PROJ_SIZES)[:-1]]
    mq, mk, mv, mo, mi, mf, dq, dk, dv = jnp.split(h @ w_in, idx, axis=-1)
    mq = mq.reshape(B, T, N_MLSTM_HEADS, MLSTM_QK_DIM).astype(f32)
    mk = mk.reshape(B, T, N_MLSTM_HEADS, MLSTM_QK_DIM).astype(f32) * (MLSTM_QK_DIM ** -0.5)
    mv = mv.reshape(B, T, N_MLSTM_HEADS, MLSTM_V_DIM).astype(f32)
    o_gate = jax.nn.sigmoid(mo)
    i_pre = (mi + b_igate).astype(f32)
    log_f = jax.nn.log_sigmoid((mf + b_fgate).astype(f32))
    dq = partial_rope(dq.reshape(B, T, N_DIFF_HEADS, 2, DIFF_QK_DIM), pos)
    dk = partial_rope(dk.reshape(B, T, N_DIFF_HEADS, 2, DIFF_QK_DIM), pos)
    dv = dv.reshape(B, T, N_DIFF_HEADS, DIFF_V_DIM)
    return (mq, mk, mv, i_pre, log_f), o_gate, (dq, dk, dv)

def mlstm_chunk(carry, inp):
    C, n, m = carry
    q, k, v, i_pre, log_f = inp
    L = q.shape[1]
    b = jnp.moveaxis(jnp.cumsum(log_f, axis=1), 1, 2)
    ig = jnp.moveaxis(i_pre, 1, 2)
    dmat = b[..., :, None] - b[..., None, :] + ig[..., None, :]
    causal = jnp.tril(jnp.ones((L, L), dtype=bool))
    dmat = jnp.where(causal, dmat, -jnp.inf)
    inter = b + m[..., None]
    m_t = jnp.maximum(inter, jnp.max(dmat, axis=-1))
    w_intra = jnp.exp(dmat - m_t[..., None])
    w_inter = jnp.exp(inter - m_t)
    s = jnp.einsum('blhd,bshd->bhls', q, k) * w_intra
    num = (jnp.einsum('bhls,bshv->blhv', s, v)
           + jnp.einsum('bhvd,blhd->blhv', C, q) * jnp.moveaxis(w_inter, 1, 2)[..., None])
    den = jnp.sum(s, axis=-1) + w_inter * jnp.einsum('bhd,blhd->bhl', n, q)
    den = jnp.maximum(jnp.abs(den), jnp.exp(-m_t))
    h = num / jnp.moveaxis(den, 1, 2)[..., None]
    m_last = m_t[..., -1]
    w_state = jnp.exp(b[..., -1] + m - m_last)
    w_rows = jnp.exp(b[..., -1:] - b + ig - m_last[..., None])
    C_new = w_state[..., None, None] * C + jnp.einsum('bhs,bshv,bshd->bhvd', w_rows, v, k)
    n_new = w_state[..., None] * n + jnp.einsum('bhs,bshd->bhd', w_rows, k)
    return (C_new, n_new, m_last), h

def mlstm_readout(h, o_gate, g):
    B, T = h.shape[:2]
    return rms_norm(h, g).reshape(B, T, MLSTM_WIDTH).astype(o_gate.dtype) * o_gate

def diff_lambda(lam_qk, layer):
    lam_init = 0.8 - 0.6 * math.exp(-0.3 * layer)
    lf = lam_qk.astype(jnp.float32)
    lam = jnp.exp(jnp.sum(lf[0] * lf[1])) - jnp.exp(jnp.sum(lf[2] * lf[3])) + lam_init
    return lam, lam_init

def diff_weights(scores, lam):
    p = jax.nn.softmax(scores, axis=-1)
    return p[:, :, 0] - lam * p[:, :, 1]

def diff_attn_prompt(q, k, v, lam):
    B, S = q.shape[:2]
    nb = S // Q_BLOCK
    q_blocks = jnp.moveaxis(q.reshape(B, nb, Q_BLOCK, N_DIFF_HEADS, 2, DIFF_QK_DIM), 1, 0)
    key_chunk = jnp.arange(S) // CHUNK
    vf = v.astype(jnp.float32)
    scale = DIFF_QK_DIM ** -0.5

    def one_block(args):
        qb, blk = args
        q_chunk = (blk * Q_BLOCK + jnp.arange(Q_BLOCK)) // CHUNK
        s = jnp.einsum('bqhcd,bkhcd->bhcqk', qb, k).astype(jnp.float32) * scale
        visible = key_chunk[None, :] <= q_chunk[:, None]
        s = jnp.where(visible, s, -jnp.inf)
        return jnp.einsum('bhqk,bkhd->bqhd', diff_weights(s, lam), vf)

    out = lax.map(one_block, (q_blocks, jnp.arange(nb)))
    return jnp.moveaxis(out, 0, 1).reshape(B, S, N_DIFF_HEADS, DIFF_V_DIM)

def diff_readout(o, g, lam_init):
    B, T = o.shape[:2]
    return (rms_norm(o, g) * (1 - lam_init)).reshape(B, T, DIFF_WIDTH)

def mixer_prompt(h, w_in, b_igate, b_fgate, g_mlstm, g_diff, lam, lam_init):
    B, S, _ = h.shape
    pos = jnp.arange(S)
    m_inputs, o_gate, (dq, dk, dv) = project(h, w_in, b_igate, b_fgate, pos)
    n_chunks = S // CHUNK
    chunked = tuple(jnp.moveaxis(a.reshape(B, n_chunks, CHUNK, *a.shape[2:]), 1, 0) for a in m_inputs)
    f32 = jnp.float32
    carry0 = (jnp.zeros((B, N_MLSTM_HEADS, MLSTM_V_DIM, MLSTM_QK_DIM), f32),
              jnp.zeros((B, N_MLSTM_HEADS, MLSTM_QK_DIM), f32),
              jnp.zeros((B, N_MLSTM_HEADS), f32))
    (C, n, m), hm = lax.scan(mlstm_chunk, carry0, chunked)
    hm = jnp.moveaxis(hm, 0, 1).reshape(B, S, N_MLSTM_HEADS, MLSTM_V_DIM)
    y_m = mlstm_readout(hm, o_gate, g_mlstm)
    y_d = diff_readout(diff_attn_prompt(dq, dk, dv, lam), g_diff, lam_init)
    heads = jnp.concatenate([y_m.astype(h.dtype), y_d.astype(h.dtype)], axis=-1)
    new_state = (dk.reshape(B, S, N_DIFF_HEADS, 2 * DIFF_QK_DIM), dv,
                 C.astype(h.dtype), n.astype(h.dtype), m.astype(h.dtype))
    return heads, new_state

def mixer_sample(h, cache_k, cache_v, state_C, state_n, state_m, w_in, b_igate, b_fgate,
                 g_mlstm, g_diff, lam, lam_init):
    B, T, _ = h.shape
    P = cache_k.shape[1]
    pos = P + jnp.arange(T)
    m_inputs, o_gate, (dq, dk, dv) = project(h, w_in, b_igate, b_fgate, pos)
    f32 = jnp.float32
    carry = (state_C.astype(f32), state_n.astype(f32), state_m.astype(f32))
    (C, n, m), hm = mlstm_chunk(carry, m_inputs)
    y_m = mlstm_readout(hm, o_gate, g_mlstm)
    k_all = jnp.concatenate([cache_k.reshape(B, P, N_DIFF_HEADS, 2, DIFF_QK_DIM), dk], axis=1)
    v_all = jnp.concatenate([cache_v, dv], axis=1)
    s = jnp.einsum('bqhcd,bkhcd->bhcqk', dq, k_all).astype(f32) * (DIFF_QK_DIM ** -0.5)
    o = jnp.einsum('bhqk,bkhd->bqhd', diff_weights(s, lam), v_all.astype(f32))
    y_d = diff_readout(o, g_diff, lam_init)
    heads = jnp.concatenate([y_m.astype(h.dtype), y_d.astype(h.dtype)], axis=-1)
    new_state = (dk.reshape(B, T, N_DIFF_HEADS, 2 * DIFF_QK_DIM), dv,
                 C.astype(h.dtype), n.astype(h.dtype), m.astype(h.dtype))
    return heads, new_state

def trunk_layer(x, c, mixer, w_ada, b_ada, g_norm, w_ffn1_in, w_ffn1_out, w_out, w_ffn2_in, w_ffn2_out):
    mod = ada_params(c, w_ada, b_ada)
    x = residual(x, swiglu(modulate(x, g_norm[0], mod[:, 0], mod[:, 1]), w_ffn1_in, w_ffn1_out),
                 g_norm[1], mod[:, 2], 0.5)
    heads, new_state = mixer(modulate(x, g_norm[2], mod[:, 3], mod[:, 4]))
    x = residual(x, heads @ w_out, g_norm[3], mod[:, 5], 1.0)
    x = residual(x, swiglu(modulate(x, g_norm[4], mod[:, 6], mod[:, 7]), w_ffn2_in, w_ffn2_out),
                 g_norm[5], mod[:, 8], 0.5)
    return x, new_state

def setup_inputs(seed: int = 0) -> dict:
    key = jax.random.key(seed)
    ks = jax.random.split(key, 24)
    f32 = jnp.float32

    def nrm(k, shape, s):
        return jax.random.normal(k, shape, f32) * s

    return {
        'x_prompt': nrm(ks[0], (BATCH, SEQ, D_MODEL), 1.0),
        'x_sample': nrm(ks[1], (DEC_BATCH, DEC_SEQ, D_MODEL), 1.0),
        'cache_k': nrm(ks[2], (DEPTH, DEC_BATCH, PAST_LEN, N_DIFF_HEADS, 2 * DIFF_QK_DIM), 1.0),
        'cache_v': nrm(ks[3], (DEPTH, DEC_BATCH, PAST_LEN, N_DIFF_HEADS, DIFF_V_DIM), 1.0),
        'state_C': nrm(ks[4], (DEPTH, DEC_BATCH, N_MLSTM_HEADS, MLSTM_V_DIM, MLSTM_QK_DIM), 0.3),
        'state_n': nrm(ks[5], (DEPTH, DEC_BATCH, N_MLSTM_HEADS, MLSTM_QK_DIM), 1.0),
        'state_m': nrm(ks[6], (DEPTH, DEC_BATCH, N_MLSTM_HEADS), 0.5),
        'c_prompt': nrm(ks[7], (BATCH, D_MODEL), 1.0),
        'c_sample': nrm(ks[8], (DEC_BATCH, D_MODEL), 1.0),
        'w_ada': nrm(ks[9], (DEPTH, D_MODEL, N_ADA * D_MODEL), D_MODEL ** -0.5),
        'b_ada': nrm(ks[10], (DEPTH, N_ADA * D_MODEL), 0.01),
        'g_norm': 1.0 + nrm(ks[11], (DEPTH, 6, D_MODEL), 0.05),
        'w_ffn1_in': nrm(ks[12], (DEPTH, D_MODEL, 2 * D_FF), D_MODEL ** -0.5),
        'w_ffn1_out': nrm(ks[13], (DEPTH, D_FF, D_MODEL), D_FF ** -0.5),
        'w_in': nrm(ks[14], (DEPTH, D_MODEL, PROJ_WIDTH), D_MODEL ** -0.5),
        'b_igate': nrm(ks[15], (DEPTH, N_MLSTM_HEADS), 0.1),
        'b_fgate': jnp.linspace(3.0, 6.0, N_MLSTM_HEADS, dtype=f32)[None, :] + nrm(ks[16], (DEPTH, N_MLSTM_HEADS), 0.1),
        'g_mlstm': 1.0 + nrm(ks[17], (DEPTH, N_MLSTM_HEADS, MLSTM_V_DIM), 0.05),
        'g_diff': 1.0 + nrm(ks[18], (DEPTH, N_DIFF_HEADS, DIFF_V_DIM), 0.05),
        'lambda_qk': nrm(ks[19], (DEPTH, 4, DIFF_QK_DIM), 0.1),
        'w_out': nrm(ks[20], (DEPTH, D_MODEL, D_MODEL), D_MODEL ** -0.5),
        'w_ffn2_in': nrm(ks[21], (DEPTH, D_MODEL, 2 * D_FF), D_MODEL ** -0.5),
        'w_ffn2_out': nrm(ks[22], (DEPTH, D_FF, D_MODEL), D_FF ** -0.5),
    }

def reference(x_prompt, x_sample, cache_k, cache_v, state_C, state_n, state_m, c_prompt, c_sample,
              w_ada, b_ada, g_norm, w_ffn1_in, w_ffn1_out, w_in, b_igate, b_fgate, g_mlstm, g_diff,
              lambda_qk, w_out, w_ffn2_in, w_ffn2_out):
    y_p, y_s = x_prompt, x_sample
    states_p, states_s = [], []
    for l in range(DEPTH):
        lam, lam_init = diff_lambda(lambda_qk[l], l)
        mix_p = functools.partial(mixer_prompt, w_in=w_in[l], b_igate=b_igate[l], b_fgate=b_fgate[l],
                                  g_mlstm=g_mlstm[l], g_diff=g_diff[l], lam=lam, lam_init=lam_init)
        mix_s = functools.partial(mixer_sample, cache_k=cache_k[l], cache_v=cache_v[l], state_C=state_C[l],
                                  state_n=state_n[l], state_m=state_m[l], w_in=w_in[l], b_igate=b_igate[l],
                                  b_fgate=b_fgate[l], g_mlstm=g_mlstm[l], g_diff=g_diff[l],
                                  lam=lam, lam_init=lam_init)
        y_p, st_p = trunk_layer(y_p, c_prompt, mix_p, w_ada[l], b_ada[l], g_norm[l], w_ffn1_in[l],
                                w_ffn1_out[l], w_out[l], w_ffn2_in[l], w_ffn2_out[l])
        y_s, st_s = trunk_layer(y_s, c_sample, mix_s, w_ada[l], b_ada[l], g_norm[l], w_ffn1_in[l],
                                w_ffn1_out[l], w_out[l], w_ffn2_in[l], w_ffn2_out[l])
        states_p.append(st_p)
        states_s.append(st_s)
    k_p, v_p, C_p, n_p, m_p = [jnp.stack(a, axis=0) for a in zip(*states_p)]
    k_s, v_s, C_s, n_s, m_s = [jnp.stack(a, axis=0) for a in zip(*states_s)]
    return (y_p, y_s, k_p, v_p, C_p, n_p, m_p, k_s, v_s, C_s, n_s, m_s)


_drawn_inputs = setup_inputs


def setup_inputs(seed=0):
    import zlib

    import numpy as np

    out = dict(_drawn_inputs(seed))
    spreads = {}
    factors = {'b_igate': 8.0, 'g_mlstm': 4.234, 'g_diff': 2.87}
    for name, (base, spread) in spreads.items():
        noise = np.random.default_rng([zlib.crc32(name.encode()), seed]).standard_normal(out[name].shape)
        drawn = base * np.exp(spread * noise) if base else spread * noise
        out[name] = __import__('jax').numpy.asarray(drawn.astype(out[name].dtype))
    for name, factor in factors.items():
        out[name] = (out[name] * factor).astype(out[name].dtype)
    return out
```

```python
from contextlib import ExitStack

import concourse.bass as bass
from concourse import mybir

P = 128
D = 1024
KT = D // P
SEQ, DB, DS, PAST = 512, 8, 16, 256
TOK = SEQ + DB * DS
NT = TOK // P
NTP = SEQ // P
HALF = TOK // 2
DFF = 2816
FT = DFF // P
NADA = 9
NB = 1 + DB
HM = HD = 4
DQ, DV = 64, 128
EPS = 1e-6
LAM_INIT = 0.8 - 0.6
SCALE = float(DQ) ** -0.5
BIG = -1.0e30

UNIT = 2048
ADA_COLS = UNIT // KT
ADA_UNITS = NADA * D // ADA_COLS
ADA_FIRST = 2 * D // ADA_COLS // 2
ADA_REST = (ADA_UNITS - 2 * ADA_FIRST - FT) // 2
OUT_TURNS = FT // 2
C_MK, C_MV, C_MO, C_G, C_DQ, C_DK, C_DV = 256, 512, 1024, 1536, 1544, 2056, 2568
GROUPS = [("mq", 0, 256 + 2 * HM), ("mk", C_MK, 256), ("mv", C_MV, 512), ("mo", C_MO, 512),
          ("dq", C_DQ, 512), ("dk", C_DK, 512), ("dv", C_DV, 512), ("o0", 0, 512), ("o1", 512, 512)]

_c = 0
def _col(n):
    global _c
    _c += n
    return _c - n
CI, CMP, CMS, CBM = _col(P), _col(P), _col(P), _col(DB)
CSEL, CS18, CROPE = _col(HD * DS), _col(NB), _col(NT * 24)
CHEAD, CPAIR, CONE, CDELTA, CSIGN = _col(HM * P), _col(2 * P), _col(P), _col(HM * DB), _col(2)
CW = _c


def constants():
    import numpy as np
    c = np.zeros((P, CW), np.float32)
    i = np.arange(P)
    c[:, CI:CI + P] = np.eye(P)
    causal = i[:, None] <= i[None, :]
    c[:, CMP:CMP + P] = np.where(causal, 0, BIG)
    same = i[:, None] // DS == i[None, :] // DS
    c[:, CMS:CMS + P] = np.where(causal & same, 0, BIG)
    c[:, CBM:CBM + DB] = i[:, None] // DS == np.arange(DB)
    row_head, row_q = i // 32, i % DS
    c[:, CSEL:CSEL + 64] = (row_head[:, None] == np.arange(64) // DS) & (row_q[:, None] == np.arange(64) % DS)
    for r in range(NB):
        c[r, CS18 + r] = c[NB + r, CS18 + r] = 1
    f = np.float32
    inv = f(500000.0) ** (-np.arange(8, dtype=f) * f(2.0 / 16))
    pos = np.concatenate([np.arange(SEQ), np.tile(PAST + np.arange(DS), DB)]).astype(f)
    ang = pos[:, None] * inv[None, :]
    rope = np.concatenate([np.cos(ang), -np.sin(ang), np.sin(ang)], axis=1)
    c[:, CROPE:CROPE + NT * 24] = rope.reshape(NT, P, 24).transpose(1, 0, 2).reshape(P, NT * 24)
    for h in range(HM):
        c[h, CHEAD + h * P:CHEAD + (h + 1) * P] = -1
        c[h, CDELTA + h * DB:CDELTA + (h + 1) * DB] = 1
        c[h, CPAIR + (h // 2) * P + 64 * (h % 2):CPAIR + (h // 2) * P + 64 * (h % 2) + 64] = 1
    c[:, CONE:CONE + P] = 1
    c[:, CSIGN] = i // DS % 2 == 0
    c[:, CSIGN + 1] = i // DS % 2 == 1
    return c


def chain(eng, done):
    count = [0]

    def link(ins):
        count[0] += 1
        ins.then_inc(done, 1)
        eng.wait_ge(done, count[0])
        return ins
    return link


def from_zero(eng, turns, body):
    body(0)
    with eng.Fori(1, turns) as t:
        body(t)


ALU = mybir.AluOpType
ACT = mybir.ActivationFunctionType
AXX = mybir.AxisListType.X
F32 = mybir.dt.float32
F32R = mybir.dt.float32r
KB = 1024


def build(nc, i, o):
    with ExitStack() as ctx:
        base = (nc.sbuf_base + 31) // 32 * 32

        def at(name, off, shape, dt=F32):
            return nc.alloc_sbuf_tensor_at(name, shape, dt, offset=base + off)

        def sem(name):
            return ctx.enter_context(nc.semaphore(name))

        X = at("resid", 0, [P, NT, D])
        HTH = at("h_t_hi", 20 * KB, [P, KT, TOK], F32R)
        HTL = at("h_t_lo", 40 * KB, [P, KT, TOK], F32R)
        RAW = at("w_raw", 60 * KB, [P, 2, UNIT])
        WH = at("w_hi", 76 * KB, [P, 2, UNIT], F32R)
        WL = at("w_lo", 92 * KB, [P, 2, UNIT], F32R)
        FIX = 193 * KB
        CON = at("const", FIX, [P, CW])
        off = FIX + CW * 4
        def fixed(name, shape, dt=F32):
            nonlocal off
            n = 4
            for s in shape[1:]:
                n *= s
            off += -off % 32
            t = at(name, off, shape, dt)
            off += n
            return t
        MODT = fixed("mod_t", [P, NADA * KT, NB])
        BT = fixed("b_ada_t", [P, NADA * KT])
        GT = fixed("g_norm_t", [P, 6 * KT])
        CT = fixed("c_t", [P, KT, 2 * NB], F32R)
        SCA = fixed("scale_t", [P, KT, NB])
        GATE = fixed("gate_t", [P, KT, NB])
        AROW = fixed("mod_rows", [2 * NB, 2, ADA_COLS])
        SS = fixed("sum_squares", [P, 2, NT])
        RS = fixed("rstd", [P, 2, NT])
        NNAT = fixed("state_n", [DB, HM, DQ])
        ASTH = at("act_hi", 108 * KB, [P, 2, TOK], F32R)
        ASTL = at("act_lo", 113 * KB, [P, 2, TOK], F32R)
        SIL = at("silu_gate", 108 * KB, [P, TOK])
        Y = at("y", 118 * KB, [P, NT, D])
        ACTT = at("act_t", 138 * KB, [P, FT, TOK])
        XN = at("x_norm", 138 * KB, [P, NT, D])
        V = at("modulated", 158 * KB, [P, 2, TOK])
        CALL = at("c_all", 138 * KB, [NB, D])
        CSI = at("c_silu", 142 * KB, [NB, D])
        BG = at("b_g_rows", 146 * KB, [P, 2, P])
        GSP = at("gate_bc_prompt", 28 * KB, [P, KT, P])
        GSS = at("gate_bc_sample", 32 * KB, [P, KT, P])
        GB = at("gate_rows", 20 * KB, [P, 2, D])
        GATE_BUF = [(GSP, GSS, GB),
                    (at("gate_bc_prompt1", 164 * KB, [P, KT, P]), at("gate_bc_sample1", 168 * KB, [P, KT, P]),
                     at("gate_rows1", 172 * KB, [P, 2, D])),
                    (GSP, GSS, GB)]
        M0 = 108 * KB
        MQG = at("mq_gates", M0, [P, NT, 264]); M0 += 264 * NT * 4
        MK = at("mk", M0, [P, NT, 256]); M0 += 5 * KB
        MQT = at("mq_t", M0, [P, 2, TOK]); M0 += 5 * KB
        MKT = at("mk_t", M0, [P, 2, TOK]); M0 += 5 * KB
        QST = at("mq_scaled_t", M0, [P, 2, SEQ]); M0 += 4 * KB
        MVX = at("mv_ones", M0, [P, NT, HM, DV + 1]); M0 += NT * HM * (DV + 1) * 4 + 16
        OG = at("o_gate", M0, [P, NT, 512]); M0 += 10 * KB
        DVT = at("dv", M0, [P, NT, 512]); M0 += 10 * KB
        DQT = at("dq_t", M0, [P, HD, TOK]); M0 += 10 * KB
        DKT = at("dk_t", M0, [P, HD, TOK]); M0 += 10 * KB
        DQK = at("rope_in", M0, [P, 2, 512])
        R1 = at("rope_cos", M0 + 4 * KB, [P, 2, 2 * HD, 2, 8])
        R2 = at("rope_sin", M0 + 5 * KB, [P, 2, 2 * HD, 2, 8])
        HHM = at("mlstm_heads", M0, [P, NT, 512]); M0 += 10 * KB
        assert M0 <= FIX
        HDF = at("diff_heads", 108 * KB + 264 * NT * 4 + 19 * KB, [P, NT, 512])
        N0 = 20 * KB
        ROWA = at("row_a", N0, [HM, TOK]); N0 += 2560
        ROWB = at("row_b", N0, [HM, TOK]); N0 += 2560
        ROWM = at("row_m", N0, [HM, TOK]); N0 += 2560
        ROWI = at("row_inter", N0, [HM, TOK]); N0 += 2560
        ROWR = at("row_rows", N0, [HM, TOK]); N0 += 2560
        ARG = at("w_arg", N0, [P, HM, P]); N0 += 2 * KB
        KBM = at("k_by_batch", N0 - 2 * KB, [P, DB, DQ])
        ST = at("s_t", N0, [P, HM, P]); N0 += 2 * KB
        KW = at("k_weighted", N0, [P, HM, DQ]); N0 += KB
        CTX = at("state_t", N0, [P, 2, DV + 1]); N0 += 1056
        SC = at("state_c", N0, [P, HM, DB, DQ]); N0 += 8 * KB
        SCT = at("state_ct", N0, [P, DB // 2, HM, DV + 1]); N0 += 8256
        QB = at("q_by_batch", N0, [P, DB, DQ]); N0 += 2 * KB
        NROW = at("state_n_rows", N0 - 2 * KB, [32, P])
        QBT = at("q_by_batch_t", N0, [P, DB // 2, P]); N0 += 2 * KB
        COLA = at("col_a", N0, [P, NT, HM]); N0 += 96
        COLE = at("col_exp", N0, [P, 3, NT, HM]); N0 += 256
        WSR = at("seg_rows", N0, [HM, 96]); N0 += 384
        WSB = at("seg_bc", N0, [P, 40]); N0 += 160
        WS8 = at("seg_by_batch", N0, [DB, HM]); N0 += 32
        DEN = at("denominators", N0, [P, NT, HM]); N0 += 96
        WB = at("rows_by_batch", N0, [P, HM, DB]); N0 += 128
        assert N0 <= 60 * KB, N0
        A0 = 20 * KB
        PR = at("probs", A0, [P, 2, 2, 512]); A0 += 8 * KB
        PTT = at("probs_t", A0, [P, 2, 512]); A0 += 4 * KB
        KC = at("k_cache", A0, [P, 2, 2, 512]); A0 += 8 * KB
        VC = at("v_cache", A0, [P, 2, 2, 512]); A0 += 8 * KB
        KCT = at("k_cache_t", A0, [P, HD, PAST]); A0 += 4 * KB
        QBD = at("q_blocks", A0, [P, DB, HD, 32]); A0 += 4 * KB
        VN = at("v_new", A0, [DS, 2, 512]); A0 += 4 * KB
        assert A0 <= 60 * KB
        B0 = 108 * KB
        GH = at("g_heads", B0, [P, D]); B0 += 4 * KB
        OB = at("out_b", B0, [DS, 2, 512]); B0 += 4 * KB
        PS_ = at("probs_s", B0, [P, 2, PAST + DS]); B0 += 2 * KB + 192
        B0 = 108 * KB + 264 * NT * 4 + 5 * KB
        PTS = at("probs_s_t", B0, [P, 3, 64]); B0 += KB
        LAM = at("lambda", B0, [P, 4, DQ]); B0 += KB
        LS = at("lambda_s", B0, [P, 16]); B0 += 64
        MX = at("max_den", B0, [P, 32]); B0 += 128
        MR = at("combine", B0, [P, 64]); B0 += 256
        HR = at("head_rstd", B0, [P, 2, NT, HM]); B0 += 160
        SQ = at("squares", 20 * KB, [P, NT, 512])

        PS = ctx.enter_context(nc.psum_tensor("ps", [P, 8, 512], F32))
        ident = CON[:, CI:CI + P]

        small_landed = sem("small_landed")
        x_landed = sem("x_landed")
        c_silu = sem("c_silu")
        c_tr = sem("c_tr")
        c_hi = sem("c_hi")
        c_ready = sem("c_ready")
        a_landed = [sem(f"a_landed{s}") for s in range(2)]
        a_hi = [sem(f"a_hi{s}") for s in range(2)]
        a_lo = [sem(f"a_lo{s}") for s in range(2)]
        a_mm = [sem(f"a_mm{s}") for s in range(2)]
        a_row = [sem(f"a_row{s}") for s in range(2)]
        a_tr = [sem(f"a_tr{s}") for s in range(2)]
        a_mod = [sem(f"a_mod{s}") for s in range(2)]
        f_landed = [sem(f"f_landed{s}") for s in range(2)]
        f_hi = [sem(f"f_hi{s}") for s in range(2)]
        f_lo = [sem(f"f_lo{s}") for s in range(2)]
        f_mm = [sem(f"f_mm{s}") for s in range(2)]
        f_silu = sem("f_silu")
        f_act = sem("f_act")
        k_landed = [sem(f"k_landed{s}") for s in range(2)]
        k_hi = [sem(f"k_hi{s}") for s in range(2)]
        k_lo = [sem(f"k_lo{s}") for s in range(2)]
        k_mm = [sem(f"k_mm{s}") for s in range(2)]
        out_done = sem("out_done")
        y_copied = sem("y_copied")
        gate_t = sem("gate_t")
        gate_bc = sem("gate_bc")
        gate_mm = sem("gate_mm")
        gate_rows = sem("gate_rows")
        y_sq = sem("y_sq")
        y_ms = sem("y_ms")
        y_rstd = sem("y_rstd")
        x_new = sem("x_new")
        x_sq = sem("x_sq")
        x_ms = sem("x_ms")
        x_rstd = sem("x_rstd")
        x_norm = sem("x_norm")
        x_tr = sem("x_tr")
        sca_ready = sem("sca_ready")
        v_p = sem("v_p")
        v_s = sem("v_s")
        h_hi = sem("h_hi")
        h_lo = sem("h_lo")
        g_landed = [sem(f"g_landed{s}") for s in range(2)]
        g_hi = [sem(f"g_hi{s}") for s in range(2)]
        g_lo = [sem(f"g_lo{s}") for s in range(2)]
        g_half = sem("g_half")
        g_free = sem("g_free")
        k_sent = [sem(f"k_sent{s}") for s in range(2)]
        y_scaled = sem("y_scaled")
        g_bank = sem("g_bank")
        rope_done = sem("rope_done")
        rope_tr = sem("rope_tr")
        rope_t = sem("rope_t")
        kv_out = sem("kv_out")
        dvec = sem("dve_chain")
        actc = sem("act_chain")
        q_tr = sem("q_tr")
        q_t = sem("q_t")
        gates_tr = sem("gates_tr")
        gates_row = sem("gates_row")
        ln_f = sem("ln_f")
        mst_landed = sem("mst_landed")
        rows_ready = sem("rows_ready")
        cols_tr = sem("cols_tr")
        cols_exp = sem("cols_exp")
        seg_exp = sem("seg_exp")
        seg_d = sem("seg_d")
        seg_mm = sem("seg_mm")
        seg_bc = sem("seg_bc")
        qs_ready = sem("qs_ready")
        qs_tr = sem("qs_tr")
        qs_t = sem("qs_t")
        st_tr = sem("st_tr")
        st_t = sem("st_t")
        m_even = sem("m_even")
        m_scores = sem("m_scores")
        m_arg = sem("m_arg")
        m_exp = sem("m_exp")
        m_s = sem("m_s")
        m_kw = sem("m_kw")
        m_cu = sem("m_cu")
        m_state = sem("m_state")
        m_hn = sem("m_hn")
        m_head = sem("m_head")
        qb_ready = sem("qb_ready")
        qb_tr = sem("qb_tr")
        qb_t = sem("qb_t")
        kb_ready = sem("kb_ready")
        cu_s = sem("cu_s")
        c_new = sem("c_new")
        n_mm = sem("n_mm")
        fin_tr = sem("fin_tr")
        fin_c = sem("fin_c")
        st_out = sem("st_out")
        g_lam_landed = sem("g_lam_landed")
        lam_e = sem("lam_e")
        p_scores = sem("p_scores")
        p_max = sem("p_max")
        p_exp = sem("p_exp")
        p_comb = sem("p_comb")
        p_tr = sem("p_tr")
        p_t = sem("p_t")
        p_o = sem("p_o")
        p_copied = sem("p_copied")
        cache_landed = [sem(f"cache_landed{s}") for s in range(2)]
        qbd_ready = sem("qbd_ready")
        s_ktr = sem("s_ktr")
        s_scores = sem("s_scores")
        s_max = sem("s_max")
        s_exp = sem("s_exp")
        s_mr = sem("s_mr")
        s_ptr = sem("s_ptr")
        s_pt = sem("s_pt")
        s_o = sem("s_o")
        s_ob = sem("s_ob")
        ob_moved = [sem(f"ob_moved{s}") for s in range(2)]
        hd_ms = sem("hd_ms")
        hd_rstd = sem("hd_rstd")
        heads = sem("heads")
        hh_tr = sem("hh_tr")
        seg_arg = sem("seg_arg")
        st_n = sem("st_n")
        wb_ready = sem("wb_ready")
        qb_mm = sem("qb_mm")
        lam_s = sem("lam_s")
        s_kta = sem("s_kta")
        s_ktd = sem("s_ktd")
        hh_hi = sem("hh_hi")
        hh_lo = sem("hh_lo")
        n_new = sem("n_new")
        y_out = sem("y_out")

        w_ada = i["w_ada"].rearrange("l (k p) n -> p (l k) n", p=P)
        ffn_in = [i[n].rearrange("l (k p) n -> p (l k) n", p=P) for n in ("w_ffn1_in", "w_ffn2_in")]
        ffn_out = [i[n].rearrange("l f n -> (l f) n") for n in ("w_ffn1_out", "w_ffn2_out")]
        w_in = i["w_in"].rearrange("l (k p) n -> p (l k) n", p=P)
        w_o = i["w_out"].rearrange("l (k p) n -> p (l k) n", p=P)
        x_p = i["x_prompt"].rearrange("b (t p) d -> p (b t) d", p=P)
        x_s = i["x_sample"].rearrange("b s d -> (b s) d")
        k_cache = i["cache_k"].rearrange("l b (k p) h d -> p (l b) k (h d)", p=P)
        v_cache = i["cache_v"].rearrange("l b (k p) h d -> p (l b) k (h d)", p=P)

        def ada_view(T, s):
            return T[:, s, :].rearrange("p (k n) -> p k n", k=KT)

        def ffn_view(T, s):
            return T[:, 0, s * 1024:(s + 1) * 1024].rearrange("p (k n) -> p k n", k=KT)

        def out_view(T, s):
            return T[:, 0, s * 1024:s * 1024 + 512]

        def grp_view(T, s, n):
            return T[:, s, 0:4 * n].rearrange("p (k n) -> p k n", k=4)

        block = ctx.enter_context(nc.Block())

        @block.sync
        def _(sp):
            sp.dma_start(CON[:, :], i["const"]).then_inc(small_landed, 16)
            sp.dma_start(CALL[0:1, :], i["c_prompt"]).then_inc(small_landed, 16)
            sp.dma_start(CALL[1:NB, :], i["c_sample"]).then_inc(small_landed, 16)
            sp.dma_start(BG[0:NADA * KT, 0, :], i["b_ada"].rearrange("l (r p) -> (l r) p", p=P)).then_inc(small_landed, 16)
            sp.dma_start(BG[0:6 * KT, 1, :], i["g_norm"].rearrange("l g (k p) -> (l g k) p", p=P)).then_inc(small_landed, 16)

            def ada_load(s, unit, n):
                sp.wait_ge(a_hi[s], n)
                sp.wait_ge(a_lo[s], n)
                sp.dma_start(ada_view(RAW, s), w_ada[:, :, bass.ds(unit * ADA_COLS, ADA_COLS)]).then_inc(a_landed[s], 16)

            def turn(t):
                for s in range(2):
                    ada_load(s, 2 * t + s, t)
            from_zero(sp, ADA_FIRST, turn)

            sp.dma_start(X[:, 0:NTP, :], x_p).then_inc(x_landed, 16)
            sp.dma_start(X[:, NTP, :], x_s).then_inc(x_landed, 16)

            def ffn_in_loads(f, m, n):
                for s in range(2):
                    sp.wait_ge(f_hi[s], n)
                    sp.wait_ge(f_lo[s], n)
                    sp.dma_start(ffn_view(RAW, s), ffn_in[f][:, :, bass.ds(m * P + s * DFF, P)]).then_inc(f_landed[s], 16)

            def ffn_out_loads(f):
                for half in range(2):
                    def turn(t):
                        for s in range(2):
                            n = (2 * f + half) * OUT_TURNS + t
                            sp.wait_ge(k_hi[s], 2 * n)
                            sp.wait_ge(k_lo[s], 2 * n)
                            sp.dma_start(out_view(RAW, s), ffn_out[f][bass.ds((2 * t + s) * P, P), half * 512:(half + 1) * 512]).then_inc(k_landed[s], 16)

                    from_zero(sp, OUT_TURNS, turn)

            sp.wait_ge(a_hi[0], ADA_FIRST)
            sp.wait_ge(a_lo[0], ADA_FIRST)
            def turn(m):
                ffn_in_loads(0, m, m)
                ada_load(1, 2 * ADA_FIRST + m, ADA_FIRST + m)
            from_zero(sp, FT, turn)

            for s in range(2):
                sp.wait_ge(f_hi[s], FT)
                sp.wait_ge(f_lo[s], FT)
            ffn_out_loads(0)
            for s in range(2):
                sp.wait_ge(k_hi[s], 4 * OUT_TURNS)
                sp.wait_ge(k_lo[s], 4 * OUT_TURNS)
            with sp.Fori(0, ADA_REST) as t:
                ada_load(0, 2 * ADA_FIRST + FT + 2 * t, ADA_FIRST + t)
                ada_load(1, 2 * ADA_FIRST + FT + 1 + 2 * t, ADA_FIRST + FT + t)
            sp.wait_ge(a_hi[0], ADA_FIRST + ADA_REST)
            sp.wait_ge(a_lo[0], ADA_FIRST + ADA_REST)
            sp.wait_ge(a_hi[1], ADA_FIRST + FT + ADA_REST)
            sp.wait_ge(a_lo[1], ADA_FIRST + FT + ADA_REST)
            for g, (name, c0, n) in enumerate(GROUPS):
                w = w_in if g < 7 else w_o
                for s in range(2):
                    sp.wait_ge(g_hi[s], g)
                    sp.wait_ge(g_lo[s], g)
                    v = grp_view(RAW, s, n)
                    if g == 0:
                        sp.dma_start(v[:, :, 0:256], w[:, 4 * s:4 * s + 4, 0:256]).then_inc(g_landed[s], 16)
                        with nc.allow_non_contiguous_dma(reason="the gates' few columns"):
                            sp.dma_start(v[:, :, 256:264], w[:, 4 * s:4 * s + 4, C_G:C_G + 8]).then_inc(g_landed[s], 16)
                    else:
                        sp.dma_start(v, w[:, 4 * s:4 * s + 4, c0:c0 + n]).then_inc(g_landed[s], 16)
            for s in range(2):
                sp.wait_ge(g_hi[s], len(GROUPS))
                sp.wait_ge(g_lo[s], len(GROUPS))
            with sp.Fori(0, FT) as m:
                ffn_in_loads(1, m, FT + m)
            for s in range(2):
                sp.wait_ge(f_hi[s], 2 * FT)
                sp.wait_ge(f_lo[s], 2 * FT)
            ffn_out_loads(1)
            for t in range(NT):
                sp.wait_ge(x_new, 2 * NT + t + 1)
                dst = o["y_prompt"].rearrange("b (t p) d -> (b t) p d", p=P)[t] if t < NTP else o["y_sample"].rearrange("b s d -> (b s) d")
                sp.dma_start(dst, X[:, t, :]).then_inc(y_out, 16)
            sp.wait_ge(y_out, 16 * NT)

        @block.scalar
        def _(act):
            link = chain(act, actc)
            act.wait_ge(small_landed, 16 * 5)
            act.activation(CSI[:, :], CALL[:, :], ACT.Silu).then_inc(c_silu, 1)
            act.wait_ge(c_tr, 1)
            act.activation(CT[:, :, 0:NB], PS[:, 7, 0:KT * NB].rearrange("p (k b) -> p k b", k=KT), ACT.Copy).then_inc(c_hi, 1)

            def ada_hi(s, n):
                act.wait_ge(a_landed[s], 16 * (n + 1))
                act.wait_ge(a_mm[s], n)
                act.activation(WH[:, s, :], RAW[:, s, :], ACT.Copy).then_inc(a_hi[s], 1)

            def ada_row(s, n):
                act.wait_ge(a_mm[s], n + 1)
                act.wait_ge(a_tr[s], n)
                act.activation(AROW[:, s, :], PS[0:2 * NB, 4 + s, 0:ADA_COLS], ACT.Copy).then_inc(a_row[s], 1)

            def turn(t):
                for s in range(2):
                    ada_hi(s, t)
                for s in range(2):
                    ada_row(s, t)

            from_zero(act, ADA_FIRST, turn)

            def norm(p):
                for t in range(NT):
                    if p == 0:
                        act.wait_ge(x_landed, 32)
                    else:
                        act.wait_ge(x_new, (p - 1) * NT + t + 1)
                    act.activation(XN[:, t, :], X[:, t, :], ACT.Square, accum_out=SS[:, 0, t:t + 1]).then_inc(x_sq, 1)
                act.wait_ge(x_ms, p + 1)
                act.activation(RS[:, 0, :], SS[:, 0, :], ACT.Sqrt).then_inc(x_rstd, 1)
                act.wait_ge(sca_ready, p + 1)

                def hi(k):
                    act.wait_ge(v_s, KT * p + k + 1)
                    act.wait_ge(v_p, KT * p + k + 1)
                    act.activation(HTH[:, k, :], V[:, k % 2, :], ACT.Copy).then_inc(h_hi, 1)

                shift = MODT[:, 3 * p * KT:(3 * p + 1) * KT, 0:1]
                for k in range(KT):
                    act.wait_ge(x_tr, KT * p + k + 1)
                    if k >= 2:
                        act.wait_ge(h_lo, KT * p + k - 1)
                    act.activation(V[:, k % 2, 0:SEQ], PS[:, 4 + k % 2, :], ACT.Identity, bias=shift[:, k, :],
                                   scale=SCA[:, k, 0:1]).then_inc(v_p, 1)
                    if k >= 1:
                        hi(k - 1)
                hi(KT - 1)

            def ffn_hi(s, n):
                act.wait_ge(f_landed[s], 16 * (n + 1))
                act.wait_ge(f_mm[s], n)
                act.activation(WH[:, 0, s * 1024:(s + 1) * 1024], RAW[:, 0, s * 1024:(s + 1) * 1024], ACT.Copy).then_inc(f_hi[s], 1)

            def ffn_silu(n):
                act.wait_ge(f_mm[0], n + 1)
                act.wait_ge(f_act, n)
                act.activation(SIL[:, :].rearrange("p (a n) -> p a n", a=2), PS[:, 0:2, 0:HALF], ACT.Silu).then_inc(f_silu, 1)

            def out_hi(s, t, n):
                act.wait_ge(k_landed[s], 16 * (n + 1))
                act.wait_ge(k_mm[s], n)
                act.activation(WH[:, 0, s * 1024:s * 1024 + 512], RAW[:, 0, s * 1024:s * 1024 + 512], ACT.Copy).then_inc(k_hi[s], 1)
                act.activation(ASTH[:, s, :], ACTT[:, bass.ds(2 * t + s, 1), :].rearrange("p a n -> p (a n)"), ACT.Copy).then_inc(k_hi[s], 1)

            def gate_evac(r):
                for j in range(4):
                    act.wait_ge(gate_mm, 4 * r + j + 1)
                    act.activation(GATE_BUF[r][2][:, j // 2, 512 * (j % 2):512 * (j % 2) + 512], PS[:, 4 + j, :], ACT.Copy).then_inc(gate_rows, 1)

            def ffn_out(f):
                act.wait_ge(f_act, (f + 1) * FT)
                n0 = 2 * f * OUT_TURNS
                def turn(t):
                    for s in range(2):
                        out_hi(s, t, n0 + t)
                from_zero(act, OUT_TURNS, turn)

                n0 += OUT_TURNS
                for s in range(2):
                    out_hi(s, 0, n0)
                gate_evac(2 * f)
                with act.Fori(1, OUT_TURNS) as t:
                    for s in range(2):
                        out_hi(s, t, n0 + t)

            def residual(r):
                for t in range(NT):
                    act.wait_ge(y_copied, 2 * NT * r + NT + t + 1)
                    act.activation(XN[:, t, :], Y[:, t, :], ACT.Square, accum_out=SS[:, 1, t:t + 1]).then_inc(y_sq, 1)
                act.wait_ge(y_ms, r + 1)
                act.activation(RS[:, 1, :], SS[:, 1, :], ACT.Sqrt).then_inc(y_rstd, 1)

            norm(0)
            def turn(m):
                for s in range(2):
                    ffn_hi(s, m)
                ada_hi(1, ADA_FIRST + m)
                ffn_silu(m)
                ada_row(1, ADA_FIRST + m)
            from_zero(act, FT, turn)

            ffn_out(0)
            for s in range(2):
                act.wait_ge(k_mm[s], 2 * OUT_TURNS)
            with act.Fori(0, ADA_REST) as t:
                ada_hi(0, ADA_FIRST + t)
                ada_hi(1, ADA_FIRST + FT + t)
                ada_row(0, ADA_FIRST + t)
                ada_row(1, ADA_FIRST + FT + t)
            residual(0)
            norm(1)

            def grp_hi(g):
                n = 4 * GROUPS[g][2]
                for s in range(2):
                    act.wait_ge(g_landed[s], 16 * (g + 2))
                    act.activation(WH[:, s, 0:n], RAW[:, s, 0:n], ACT.Copy).then_inc(g_hi[s], 1)

            def evac(g, t, out, cols, func=ACT.Copy, scale=1.0):
                act.wait_ge(g_bank, NT * g + t + 1)
                act.activation(out, cols, func, scale=scale).then_inc(g_free, 1)

            act.wait_ge(a_mm[0], ADA_FIRST + ADA_REST)
            act.wait_ge(a_mm[1], ADA_FIRST + FT + ADA_REST)
            grp_hi(0)
            for g in range(7):
                if g < 6:
                    n = 4 * GROUPS[g + 1][2]
                    act.wait_ge(g_landed[0], 16 * (g + 3))
                    act.wait_ge(g_half, g + 1)
                    act.activation(WH[:, 0, 0:n], RAW[:, 0, 0:n], ACT.Copy).then_inc(g_hi[0], 1)
                for t in range(NT):
                    ps = PS[:, t, :]
                    if g == 0:
                        evac(g, t, MQG[:, t, :], ps[:, 0:264])
                    elif g == 1:
                        evac(g, t, MK[:, t, :], ps[:, 0:256], scale=DQ ** -0.5)
                    elif g == 2:
                        evac(g, t, MVX[:, t, :, 0:DV], ps.rearrange("p (h v) -> p h v", h=HM))
                    elif g == 3:
                        evac(g, t, OG[:, t, :], ps, ACT.Sigmoid)
                    elif g in (4, 5):
                        r = NT * (g - 4) + t
                        if r >= 2:
                            act.wait_ge(rope_tr, r - 1)
                            if r - 2 >= NT:
                                act.wait_ge(k_sent[r % 2], 16 * ((r - 2 - NT) // 2 + 1))
                        evac(g, t, DQK[:, r % 2, :], ps)
                    else:
                        evac(g, t, DVT[:, t, :], ps)
                if g < 6:
                    act.wait_ge(g_landed[1], 16 * (g + 3))
                    act.wait_ge(g_bank, NT * (g + 1))
                    act.activation(WH[:, 1, 0:n], RAW[:, 1, 0:n], ACT.Copy).then_inc(g_hi[1], 1)
            for s in range(2):
                n = 4 * GROUPS[7][2]
                act.wait_ge(g_landed[s], 16 * (7 + 2))
                act.activation(WH[:, s, 0:n], RAW[:, s, 0:n], ACT.Copy).then_inc(g_hi[s], 1)

            act.wait_ge(gates_row, 4)
            link(act.activation(ROWI[:, :], ROWB[:, :], ACT.Abs))
            link(act.activation(ROWI[:, :], ROWI[:, :], ACT.Exp, scale=-1.0))
            act.activation(ROWR[:, :], ROWI[:, :], ACT.Ln, bias=1.0).then_inc(ln_f, 1)
            for pr in range(DB // 2):
                act.wait_ge(st_tr, pr + 1)
                act.activation(SCT[:, pr, :, 0:DV], PS[:, pr, :].rearrange("p (h v) -> p h v", h=HM), ACT.Copy).then_inc(st_t, 1)
            act.wait_ge(seg_arg, 1)
            act.activation(WSR[:, 36:48], WSR[:, 24:36], ACT.Exp).then_inc(seg_exp, 1)
            act.wait_ge(cols_tr, 1)
            act.activation(COLA[:, :, :], PS[:, 5, 0:NT * HM].rearrange("p (t h) -> p t h", t=NT), ACT.Copy).then_inc(cols_exp, 1)
            act.activation(COLE[:, :, :, :].rearrange("p a t h -> p (a t h)"), PS[:, 5, NT * HM:4 * NT * HM], ACT.Exp).then_inc(cols_exp, 1)
            for c in range(NT):
                act.wait_ge(m_arg, c + 1)
                act.activation(ARG[:, :, :], ARG[:, :, :], ACT.Exp).then_inc(m_exp, 1)
            for h in range(HM):
                act.wait_ge(qb_tr, h + 1)
                if h in (1, 2):
                    act.wait_ge(qb_mm, h)
                elif h == 3:
                    act.wait_ge(m_hn, 2 * NTP + 1)
                act.activation(QBT[:, :, :], PS[:, 7, :].rearrange("p (r t) -> p r t", r=DB // 2), ACT.Copy).then_inc(qb_t, 1)
            act.wait_ge(fin_tr, 1)
            act.activation(ST[:, 0:2, :], PS[:, 2, 0:2 * P].rearrange("p (j v) -> p j v", j=2), ACT.Copy).then_inc(fin_c, 1)

            act.wait_ge(lam_s, 1)
            act.activation(LS[:, 2:4], LS[:, 0:2], ACT.Exp).then_inc(lam_e, 1)

            def p_evac(n):
                nk = P * (n // HD + 1)
                act.wait_ge(p_tr, n + 1)
                if n >= 2:
                    act.wait_ge(p_o, n - 1)
                act.activation(PTT[:, n % 2, 0:nk], PS[:, 4 + n % 2, 0:nk], ACT.Copy).then_inc(p_t, 1)

            def o_evac(n):
                if n % HD == HD - 1:
                    act.wait_ge(p_o, n + 1)
                    act.activation(HDF[:, n // HD, :], PS[:, 6 + n // HD % 2, :], ACT.Copy).then_inc(p_copied, 1)

            for n in range(NTP * HD):
                nk = P * (n // HD + 1)
                act.wait_ge(p_max, n + 1)
                if n >= 2:
                    act.wait_ge(p_tr, n - 1)
                m = 8 * (n % 2)
                for c in range(2):
                    act.activation(PR[:, n % 2, c, 0:nk], PS[:, 2 * (n % 2) + c, 0:nk], ACT.Exp, bias=MX[:, m + 2 + c:m + 3 + c],
                                   scale=SCALE, accum_out=MX[:, m + 4 + c:m + 5 + c]).then_inc(p_exp, 1)
                if n:
                    p_evac(n - 1)
                if n > 1:
                    o_evac(n - 2)
            p_evac(NTP * HD - 1)
            o_evac(NTP * HD - 2)
            o_evac(NTP * HD - 1)

            for b in range(DB):
                act.wait_ge(s_ktr, 2 * b + 1)
                if b:
                    act.wait_ge(s_scores, b)
                act.activation(KCT[:, :, 0:P], PS[:, 6 * (b % 2), :].rearrange("p (h t) -> p h t", h=HD), ACT.Copy).then_inc(s_kta, 1)
                act.wait_ge(s_max, b + 1)
                if b >= 2:
                    act.wait_ge(s_ptr, b - 1)
                m = 16 + 4 * (b % 2)
                act.activation(PS_[:, b % 2, :], PS[:, 2 + b % 2, 0:PAST + DS], ACT.Exp, bias=MX[:, m + 1:m + 2], scale=SCALE,
                               accum_out=MX[:, m + 2:m + 3]).then_inc(s_exp, 1)
                act.wait_ge(s_ptr, b + 1)
                act.activation(PTS[:, 0:2, :], PS[:, 4, 0:128].rearrange("p (k n) -> p k n", k=2), ACT.Copy).then_inc(s_pt, 1)
                act.activation(PTS[0:DS, 2, :], PS[0:DS, 4, 128:192], ACT.Copy).then_inc(s_pt, 1)
                act.wait_ge(s_o, b + 1)
                if b >= 2:
                    act.wait_ge(ob_moved[b % 2], 16 * (b // 2))
                act.activation(OB[:, b % 2, :], PS[0:DS, 5, :], ACT.Copy).then_inc(s_ob, 1)
            for a in range(2):
                act.wait_ge(hd_ms, a + 1)
                act.activation(HR[:, a, :, :], HR[:, a, :, :], ACT.Sqrt).then_inc(hd_rstd, 1)
            for k in range(KT):
                act.wait_ge(hh_tr, k + 1)
                act.activation(HTH[:, k, 0:SEQ], PS[:, 4 + k % 2, :], ACT.Copy)
                act.activation(HTH[:, k, SEQ:TOK], PS[:, 6 + k % 2, 0:P], ACT.Copy).then_inc(hh_hi, 1)
            gate_evac(1)
            for s in range(2):
                act.wait_ge(g_landed[s], 16 * (8 + 2))
                if s:
                    act.wait_ge(g_bank, 8 * NT)
                else:
                    act.wait_ge(g_half, 8)
                act.activation(WH[:, s, :], RAW[:, s, :], ACT.Copy).then_inc(g_hi[s], 1)
            residual(1)
            norm(2)
            def turn_2(m):
                for s in range(2):
                    ffn_hi(s, m)
                ffn_silu(m)
            act.wait_ge(g_half, 9)
            act.wait_ge(g_bank, 9 * NT)
            with act.Fori(FT, 2 * FT) as n:
                turn_2(n)
            ffn_out(1)
            residual(2)
        @block.tensor
        def _(pe):
            def mm(out, lhsT, rhs, start=True, stop=True):
                return pe.matmul(out, lhsT, rhs, start=start, stop=stop)

            pe.wait_ge(small_landed, 16 * 5)
            pe.wait_ge(c_silu, 1)
            for k in range(KT):
                q = pe.transpose(PS[:, 7, k * NB:(k + 1) * NB], CSI[:, k * P:(k + 1) * P], ident[0:NB, 0:NB])
            q.then_inc(c_tr, 1)
            pe.transpose(PS[:, 6, 0:NADA * KT], BG[0:NADA * KT, 0, :], ident[0:NADA * KT, 0:NADA * KT])
            pe.transpose(PS[:, 6, P:P + 6 * KT], BG[0:6 * KT, 1, :], ident[0:6 * KT, 0:6 * KT]).then_inc(c_tr, 1)
            pe.wait_ge(c_ready, 3)

            def ada_mm(s, n):
                pe.wait_ge(a_hi[s], n + 1)
                pe.wait_ge(a_lo[s], n + 1)
                pe.wait_ge(a_row[s], n)
                wh, wl = ada_view(WH, s), ada_view(WL, s)
                for k in range(KT):
                    mm(PS[0:2 * NB, 4 + s, 0:ADA_COLS], CT[:, k, :], wh[:, k, :], k == 0, False)
                    q = mm(PS[0:NB, 4 + s, 0:ADA_COLS], CT[:, k, 0:NB], wl[:, k, :], False, k == KT - 1)
                q.then_inc(a_mm[s], 1)

            def ada_tr(s, n):
                pe.wait_ge(a_row[s], n + 1)
                pe.wait_ge(a_mod[s], n)
                for j in range(2):
                    q = mm(PS[:, 6 + s, j * NB:(j + 1) * NB], AROW[:, s, j * P:(j + 1) * P], CON[0:2 * NB, CS18:CS18 + NB])
                q.then_inc(a_tr[s], 1)

            def turn(t):
                for s in range(2):
                    ada_mm(s, t)
                for s in range(2):
                    ada_tr(s, t)
            from_zero(pe, ADA_FIRST, turn)

            for s in range(2):
                pe.wait_ge(a_row[s], ADA_FIRST)
                pe.wait_ge(a_mod[s], ADA_FIRST)

            def norm(p):
                pe.wait_ge(x_norm, NT * (p + 1))
                for k in range(KT):
                    if k >= 2:
                        pe.wait_ge(v_p, KT * p + k - 1)
                        pe.wait_ge(v_s, KT * p + k - 1)
                    for t in range(NT):
                        dst = PS[:, 4 + k % 2, t * P:(t + 1) * P] if t < NTP else PS[:, 6 + k % 2, 0:P]
                        q = pe.transpose(dst, XN[:, t, k * P:(k + 1) * P], ident)
                    q.then_inc(x_tr, 1)

            def ffn_mm(s, n, h0=None):
                pe.wait_ge(f_hi[s], n + 1)
                pe.wait_ge(f_lo[s], n + 1)
                pe.wait_ge(f_act if s else f_silu, n)
                wh, wl = ffn_view(WH, s), ffn_view(WL, s)
                for k in range(KT):
                    for w, h, first, last in ((wh, HTH, True, False), (wh, HTL, False, False), (wl, HTH, False, True)):
                        for a in range(2):
                            q = mm(PS[:, 2 * s + a, 0:HALF], w[:, k, :], h[:, k, a * HALF:(a + 1) * HALF],
                                   k == 0 and first, k == KT - 1 and last)
                q.then_inc(f_mm[s], 1)

            def out_mm(s, n, start=False, stop=False, before=None):
                pe.wait_ge(k_hi[s], 2 * (n + 1))
                pe.wait_ge(k_lo[s], 2 * (n + 1))
                for t in range(NT):
                    if before:
                        before(t)
                    th, tl = ASTH[:, s, t * P:(t + 1) * P], ASTL[:, s, t * P:(t + 1) * P]
                    mm(PS[:, t, :], th, out_view(WH, s), start, False)
                    mm(PS[:, t, :], th, out_view(WL, s), False, False)
                    q = mm(PS[:, t, :], tl, out_view(WH, s), False, stop)
                    if stop and t < NT - 1:
                        q.then_inc(out_done, 1)
                return q

            def ffn_out(f):
                for half in range(2):
                    n0 = (2 * f + half) * OUT_TURNS
                    if half:
                        gate_mms(2 * f)

                    def free(t):
                        if half:
                            pe.wait_ge(y_copied, 4 * NT * f + t + 1)
                            if t == 4:
                                pe.wait_ge(gate_rows, 4 * (2 * f + 1))

                    out_mm(0, n0, start=True, before=free).then_inc(k_mm[0], 1)
                    out_mm(1, n0).then_inc(k_mm[1], 1)
                    with pe.Fori(n0 + 1, n0 + OUT_TURNS - 1) as n:
                        for s in range(2):
                            out_mm(s, n).then_inc(k_mm[s], 1)
                    out_mm(0, n0 + OUT_TURNS - 1).then_inc(k_mm[0], 1)
                    out_mm(1, n0 + OUT_TURNS - 1, stop=True).then_inc(k_mm[1], 1)

            def gate_mms(r):
                pe.wait_ge(gate_bc, 2 * (r + 1))
                for j in range(4):
                    if j == 0 and r != 1:
                        pe.wait_ge(y_copied, 2 * NT * r + NT)
                    for k in range(4):
                        q = mm(PS[:, 4 + j, k * P:(k + 1) * P], GATE_BUF[r][j // 2][:, 4 * (j % 2) + k, :], ident)
                    q.then_inc(gate_mm, 1)

            norm(0)
            pe.wait_ge(h_hi, KT)
            pe.wait_ge(h_lo, KT)
            def turn(m):
                ffn_mm(0, m)
                ada_mm(1, ADA_FIRST + m)
                ffn_mm(1, m)
                ada_tr(1, ADA_FIRST + m)
            from_zero(pe, FT, turn)

            ffn_out(0)
            pe.wait_ge(gate_rows, 4)
            pe.wait_ge(y_copied, 2 * NT)
            with pe.Fori(0, ADA_REST) as t:
                ada_mm(0, ADA_FIRST + t)
                ada_mm(1, ADA_FIRST + FT + t)
                ada_tr(0, ADA_FIRST + t)
                ada_tr(1, ADA_FIRST + FT + t)
            for s, n in ((0, ADA_FIRST + ADA_REST), (1, ADA_FIRST + FT + ADA_REST)):
                pe.wait_ge(a_row[s], n)
                pe.wait_ge(a_mod[s], n)
            norm(1)

            def project(g, s, t):
                n = GROUPS[g][2]
                if t == 0:
                    pe.wait_ge(g_hi[s], g + 1)
                    pe.wait_ge(g_lo[s], g + 1)
                if s == 0 and 1 <= g <= 7:
                    pe.wait_ge(g_free, NT * (g - 1) + t + 1)
                wh, wl = grp_view(WH, s, n), grp_view(WL, s, n)
                for k in range(4):
                    th, tl = (T[:, 4 * s + k, t * P:(t + 1) * P] for T in (HTH, HTL))
                    mm(PS[:, t, 0:n], th, wh[:, k, :], s == 0 and k == 0, False)
                    mm(PS[:, t, 0:n], th, wl[:, k, :], False, False)
                    q = mm(PS[:, t, 0:n], tl, wh[:, k, :], False, s == 1 and k == 3)
                return q

            def rope_transposes(n):
                pe.wait_ge(rope_done, n + 1)
                if n >= 2:
                    pe.wait_ge(rope_t, n - 1)
                for h in range(HD):
                    q = pe.transpose(PS[:, 5 + n % 2, h * P:(h + 1) * P], DQK[:, n % 2, h * P:(h + 1) * P], ident)
                q.then_inc(rope_tr, 1)

            pe.wait_ge(h_hi, 2 * KT)
            pe.wait_ge(h_lo, 2 * KT)
            for g in range(7):
                for s in range(2):
                    for t in range(NT):
                        q = project(g, s, t)
                        if s == 1:
                            q.then_inc(g_bank, 1)
                        elif t == NT - 1:
                            q.then_inc(g_half, 1)
                        if g in (4, 5) and s == 1 and t >= 1:
                            rope_transposes(NT * (g - 4) + t - 1)
                        if g in (5, 6) and s == 0 and t == 0:
                            rope_transposes(NT * (g - 5) + 4)

            pe.wait_ge(rope_t, 2 * NT)
            pe.wait_ge(g_free, 7 * NT)
            for c, (bank, off) in enumerate(((5, 0), (6, 0))):
                for t in range(NT):
                    dst = PS[0:HM, bank, t * P:(t + 1) * P] if t < NTP else PS[0:HM, 7, c * P:(c + 1) * P]
                    q = pe.transpose(dst, MQG[:, t, 256 + 4 * c:260 + 4 * c], ident)
            q.then_inc(gates_tr, 1)
            for a in range(5):
                for t in range(NTP) if a < 4 else (0, 1, 2, 3):
                    if a < 4:
                        src, j = (MQG, MK)[a // 2], a % 2
                        q = pe.transpose(PS[:, a, t * P:(t + 1) * P], src[:, t, j * P:(j + 1) * P], ident)
                    else:
                        src, j = (MQG, MK)[t // 2], t % 2
                        q = pe.transpose(PS[:, 4, t * P:(t + 1) * P], src[:, NTP, j * P:(j + 1) * P], ident)
                q.then_inc(q_tr, 1)
            pe.wait_ge(mst_landed, 16 * 10)
            for pr in range(DB // 2):
                pe.wait_ge(q_t, pr + 1)
                for h in range(HM):
                    q = pe.transpose(PS[:, pr, h * DV:(h + 1) * DV], SC[:, h, 2 * pr:2 * pr + 2, :], ident)
                q.then_inc(st_tr, 1)
            pe.wait_ge(q_t, 5)
            pe.transpose(PS[:, 4, 0:32], NROW[:, :], ident[0:32, 0:32]).then_inc(st_tr, 1)
            pe.wait_ge(rows_ready, 1)
            for a, row in enumerate((ROWA, ROWI, ROWR, ROWB)):
                for t in range(NT):
                    q = pe.transpose(PS[:, 5, (a * NT + t) * HM:(a * NT + t + 1) * HM], row[:, t * P:(t + 1) * P], ident[0:HM, 0:HM])
            q.then_inc(cols_tr, 1)
            pe.wait_ge(seg_exp, 1)
            pe.wait_ge(seg_d, 1)
            for j in range(2):
                mm(PS[:, 6, 4 * j:4 * j + 4], CON[0:HM, CPAIR + j * P:CPAIR + (j + 1) * P], WSR[:, 36:40])
            mm(PS[:, 6, 8:40], CON[0:HM, CONE:CONE + P], WSR[:, 48:80])
            pe.transpose(PS[0:DB, 6, 40:44], WSR[:, 40:48], ident[0:HM, 0:HM]).then_inc(seg_mm, 1)
            pe.wait_ge(qs_ready, 1)
            pe.wait_ge(st_t, 2)
            for j in range(2):
                for t in range(1, NTP):
                    q = pe.transpose(PS[:, j, t * P:(t + 1) * P], MQG[:, t, j * P:(j + 1) * P], ident)
                q.then_inc(qs_tr, 1)
            pe.wait_ge(qs_t, 2)
            pe.wait_ge(st_t, 4)
            pe.wait_ge(st_n, 2)
            pe.wait_ge(cols_exp, 2)
            pe.wait_ge(seg_bc, 2)

            def half(h):
                return slice(64 * (h % 2), 64 * (h % 2) + 64)

            for c in range(NT):
                tok = slice(c * P, (c + 1) * P)
                if c >= 2:
                    pe.wait_ge(m_s, c - 1)
                    pe.wait_ge(m_arg, c - 1)
                for h in (0, 2):
                    q = mm(PS[:, c % 2, h * P:(h + 1) * P], MKT[half(h), h // 2, tok], MQT[half(h), h // 2, tok])
                q.then_inc(m_even, 1)
                for h in range(HM):
                    q = mm(PS[:, 2 + c % 2, h * P:(h + 1) * P], CON[0:HM, CHEAD + h * P:CHEAD + (h + 1) * P], ROWM[:, tok])
                q.then_inc(m_scores, 1)
                pe.wait_ge(m_even, c + 1)
                for h in (1, 3):
                    q = mm(PS[:, c % 2, h * P:(h + 1) * P], MKT[half(h), h // 2, tok], MQT[half(h), h // 2, tok])
                q.then_inc(m_scores, 1)
                if c < NTP:
                    pe.wait_ge(m_kw, c + 1)
                    if c:
                        pe.wait_ge(m_state, c)
                    for h in range(HM):
                        o_ = 129 * (h // 2)
                        q = mm(PS[half(h), 6, o_:o_ + DV + 1], KW[:, h, :], MVX[:, c, h, :])
                    q.then_inc(m_cu, 1)
                pe.wait_ge(m_s, c + 1)
                if c:
                    pe.wait_ge(m_state, c)
                    pe.wait_ge(m_head, 2 * c)
                for h in range(HM):
                    out = PS[:, 4 + h % 2, 129 * (h // 2):129 * (h // 2) + DV + 1]
                    q = mm(out, ST[:, h, :], MVX[:, c, h, :], True, c == 0)
                    if 1 <= c < NTP:
                        q = mm(out, QST[half(h), h // 2, tok], CTX[half(h), h // 2, :], False, True)
                    elif c == NTP:
                        pe.wait_ge(qb_ready, h + 1)
                        if h:
                            pe.wait_ge(qb_t, h)
                        for r in range(DB // 2):
                            q = pe.transpose(PS[:, 7, r * P:(r + 1) * P], QB[:, 2 * r:2 * r + 2, :], ident)
                        q.then_inc(qb_tr, 1)
                        pe.wait_ge(qb_t, h + 1)
                        for r in range(DB // 2):
                            q = mm(out, QBT[:, r, :], SCT[:, r, h, :], False, r == DB // 2 - 1)
                        if h < 2:
                            q.then_inc(qb_mm, 1)
                    if h >= 2:
                        q.then_inc(m_hn, 1)
            for h in range(HM):
                pe.wait_ge(kb_ready, h + 1)
                if h:
                    pe.wait_ge(c_new, h)
                else:
                    pe.wait_ge(m_state, NTP)
                mm(PS[:, 6, :], MVX[:, NTP, h, 0:DV], KBM[:, :, :]).then_inc(cu_s, 1)
            pe.wait_ge(wb_ready, 1)
            pe.wait_ge(qb_t, HM)
            for h in range(HM):
                q = mm(PS[0:DB, 7, h * DQ:(h + 1) * DQ], WB[:, h, :], MK[:, NTP, h * DQ:(h + 1) * DQ])
            q.then_inc(n_mm, 1)
            pe.wait_ge(m_arg, NT)
            for j in range(2):
                q = pe.transpose(PS[:, 2, j * P:(j + 1) * P], CTX[:, j, 0:DV], ident)
            q.then_inc(fin_tr, 1)

            pe.wait_ge(fin_c, 1)
            pe.wait_ge(m_s, NT)
            pe.wait_ge(m_head, 2 * NT)
            pe.wait_ge(c_new, HM)
            pe.wait_ge(n_new, 1)

            def p_score(n):
                t, h = n // HD, n % HD
                if n >= 2:
                    pe.wait_ge(p_exp, 2 * (n - 1))
                for c in range(2):
                    q = mm(PS[:, 2 * (n % 2) + c, 0:P * (t + 1)], DQT[half(c), h, t * P:(t + 1) * P], DKT[half(c), h, 0:P * (t + 1)])
                q.then_inc(p_scores, 1)

            def p_transpose(n):
                pe.wait_ge(p_comb, n + 1)
                if n >= 2:
                    pe.wait_ge(p_t, n - 1)
                for k in range(n // HD + 1):
                    q = pe.transpose(PS[:, 4 + n % 2, k * P:(k + 1) * P], PR[:, n % 2, 0, k * P:(k + 1) * P], ident)
                q.then_inc(p_tr, 1)

            def p_out(n):
                t, h = n // HD, n % HD
                pe.wait_ge(p_t, n + 1)
                if t >= 2 and h == 0:
                    pe.wait_ge(p_copied, t - 1)
                for k in range(t + 1):
                    q = mm(PS[:, 6 + t % 2, h * DV:(h + 1) * DV], PTT[:, n % 2, k * P:(k + 1) * P], DVT[:, k, h * DV:(h + 1) * DV], k == 0, k == t)
                q.then_inc(p_o, 1)

            last_n = NTP * HD
            p_score(0)
            for n in range(last_n):
                if n + 1 < last_n:
                    p_score(n + 1)
                if n:
                    p_out(n - 1)
                p_transpose(n)
            p_out(last_n - 1)

            pe.wait_ge(p_exp, 2 * last_n)
            pe.wait_ge(p_copied, NTP)
            pe.wait_ge(qbd_ready, 1)

            def s_keys(b):
                pe.wait_ge(cache_landed[b % 2], 48 * (b // 2 + 1))
                if b >= 2:
                    pe.wait_ge(s_kta, b - 1)
                    pe.wait_ge(s_ktd, b - 1)
                for k in range(2):
                    for h in range(HD):
                        q = pe.transpose(PS[:, 6 * (b % 2) + k, h * P:(h + 1) * P], KC[:, b % 2, k, h * P:(h + 1) * P], ident)
                    q.then_inc(s_ktr, 1)

            s_keys(0)
            for b in range(DB):
                pe.wait_ge(s_kta, b + 1)
                pe.wait_ge(s_ktd, b + 1)
                if b >= 2:
                    pe.wait_ge(s_exp, b - 1)
                for h in range(HD):
                    rows = slice(32 * h, 32 * h + 32)
                    mm(PS[rows, 2 + b % 2, 0:PAST], QBD[:, b, h, :], KCT[:, h, :])
                    q = mm(PS[rows, 2 + b % 2, PAST:PAST + DS], QBD[:, b, h, :], DKT[:, h, SEQ + b * DS:SEQ + (b + 1) * DS])
                q.then_inc(s_scores, 1)
                if b + 1 < DB:
                    s_keys(b + 1)
                pe.wait_ge(s_mr, b + 1)
                if b:
                    pe.wait_ge(s_pt, 2 * b)
                for k in range(3):
                    n = P if k < 2 else DS
                    q = mm(PS[0:n, 4, k * 64:(k + 1) * 64], PS_[:, b % 2, k * P:k * P + n], MR[:, :])
                q.then_inc(s_ptr, 1)
                pe.wait_ge(s_pt, 2 * (b + 1))
                if b:
                    pe.wait_ge(s_ob, b)
                for h in range(HD):
                    cols = slice(h * DV, (h + 1) * DV)
                    out, hq = PS[0:DS, 5, cols], slice(h * DS, (h + 1) * DS)
                    mm(out, PTS[:, 0, hq], VC[:, b % 2, 0, cols], True, False)
                    mm(out, PTS[:, 1, hq], VC[:, b % 2, 1, cols], False, False)
                    q = mm(out, PTS[0:DS, 2, hq], VN[:, b % 2, cols], False, True)
                q.then_inc(s_o, 1)

            pe.wait_ge(s_ob, DB)
            for k in range(KT):
                pe.wait_ge(heads, k // 4 + 1)
                if k >= 2:
                    pe.wait_ge(hh_lo, k - 1)
                src = HHM if k < 4 else HDF
                for t in range(NT):
                    dst = PS[:, 4 + k % 2, t * P:(t + 1) * P] if t < NTP else PS[:, 6 + k % 2, 0:P]
                    q = pe.transpose(dst, src[:, t, (k % 4) * P:(k % 4 + 1) * P], ident)
                q.then_inc(hh_tr, 1)
            pe.wait_ge(hh_hi, KT)
            pe.wait_ge(hh_lo, KT)
            gate_mms(1)
            for g in (7, 8):
                for s in range(2):
                    for t in range(NT):
                        if s == 0 and g == 8:
                            pe.wait_ge(y_copied, 2 * NT + t + 1)
                        if s == 0 and g == 7 and t == 4:
                            pe.wait_ge(gate_rows, 8)
                        q = project(g, s, t)
                        if s == 1:
                            q.then_inc(g_bank, 1)
                        elif t == NT - 1:
                            q.then_inc(g_half, 1)
            norm(2)
            pe.wait_ge(h_hi, 3 * KT)
            pe.wait_ge(h_lo, 3 * KT)
            pe.wait_ge(y_copied, 4 * NT)
            with pe.Fori(FT, 2 * FT) as n:
                ffn_mm(0, n)
                ffn_mm(1, n)
            ffn_out(1)
        @block.vector
        def _(dve):
            link = chain(dve, dvec)
            dve.wait_ge(c_tr, 2)
            dve.wait_ge(c_hi, 1)
            dve.tensor_tensor(CT[:, :, NB:2 * NB], PS[:, 7, 0:KT * NB].rearrange("p (k b) -> p k b", k=KT),
                              CT[:, :, 0:NB].bitcast(F32), ALU.subtract).then_inc(c_ready, 1)
            dve.tensor_copy(BT[:, :], PS[:, 6, 0:NADA * KT]).then_inc(c_ready, 1)
            dve.tensor_copy(GT[:, :], PS[:, 6, P:P + 6 * KT]).then_inc(c_ready, 1)
            dve.wait_ge(c_ready, 3)

            def split_lo(dst, raw, hi):
                return dve.tensor_tensor(dst, raw, hi.bitcast(F32), ALU.subtract)

            def ada_lo(s, n):
                dve.wait_ge(a_hi[s], n + 1)
                split_lo(WL[:, s, :], RAW[:, s, :], WH[:, s, :]).then_inc(a_lo[s], 1)

            def ada_mod(s, unit, n):
                dve.wait_ge(a_tr[s], n + 1)
                dve.tensor_tensor(MODT[:, bass.ds(2 * unit, 2), :], PS[:, 6 + s, 0:2 * NB].rearrange("p (j b) -> p j b", j=2),
                                  BT[:, bass.ds(2 * unit, 2)].rearrange("p (j b) -> p j b", b=1).to_broadcast([P, 2, NB]), ALU.add).then_inc(a_mod[s], 1)

            def turn(t):
                for s in range(2):
                    ada_lo(s, t)
                for s in range(2):
                    ada_mod(s, 2 * t + s, t)

            from_zero(dve, ADA_FIRST, turn)

            def gain(g):
                return GT[:, g * KT:(g + 1) * KT].rearrange("p (k b) -> p k b", b=1).to_broadcast([P, KT, NB])

            def mod(j):
                return MODT[:, j * KT:(j + 1) * KT, :]

            def mods_known(units0, units1):
                dve.wait_ge(a_mod[0], units0)
                dve.wait_ge(a_mod[1], units1)

            def inverse_mean(col, squares, count, done):
                dve.wait_ge(squares, count)
                link(dve.tensor_scalar(SS[:, col, :], SS[:, col, :], 1.0 / D, EPS, ALU.mult, ALU.add))
                dve.reciprocal(SS[:, col, :], SS[:, col, :]).then_inc(done, 1)

            def norm(p):
                dve.scalar_tensor_tensor(SCA[:, :, :], mod(3 * p + 1), 1.0, gain(2 * p), ALU.add, ALU.mult).then_inc(sca_ready, 1)
                inverse_mean(0, x_sq, NT * (p + 1), x_ms)
                dve.wait_ge(x_rstd, p + 1)
                dve.wait_ge(sca_ready, p + 1)
                for t in range(NT):
                    dve.tensor_scalar(XN[:, t, :], X[:, t, :], RS[:, 0, t:t + 1], None, ALU.mult).then_inc(x_norm, 1)

                def lo(k):
                    dve.wait_ge(h_hi, KT * p + k + 1)
                    split_lo(HTL[:, k, :], V[:, k % 2, :], HTH[:, k, :]).then_inc(h_lo, 1)

                for k in range(KT):
                    dve.wait_ge(x_tr, KT * p + k + 1)
                    v = V[:, k % 2, SEQ:TOK].rearrange("p (b s) -> p b s", b=DB)
                    tr = PS[:, 6 + k % 2, 0:P].rearrange("p (b s) -> p b s", b=DB)
                    sc = SCA[:, k, 1:NB].rearrange("p (b s) -> p b s", s=1).to_broadcast([P, DB, DS])
                    sh = mod(3 * p)[:, k, 1:NB].rearrange("p (b s) -> p b s", s=1).to_broadcast([P, DB, DS])
                    if k >= 2:
                        dve.wait_ge(h_lo, KT * p + k - 1)
                    link(dve.tensor_tensor(v, tr, sc, ALU.mult))
                    dve.tensor_tensor(v, v, sh, ALU.add).then_inc(v_s, 1)
                    if k >= 1:
                        lo(k - 1)
                lo(KT - 1)

            def ffn_lo(s, n):
                dve.wait_ge(f_hi[s], n + 1)
                w = slice(s * 1024, (s + 1) * 1024)
                split_lo(WL[:, 0, w], RAW[:, 0, w], WH[:, 0, w]).then_inc(f_lo[s], 1)

            def ffn_act(m, n):
                dve.wait_ge(f_mm[1], n + 1)
                dve.wait_ge(f_silu, n + 1)
                dve.tensor_tensor(ACTT[:, bass.ds(m, 1), :].rearrange("p m (a n) -> p (m a) n", a=2), SIL[:, :].rearrange("p (a n) -> p a n", a=2),
                                  PS[:, 2:4, 0:HALF], ALU.mult).then_inc(f_act, 1)

            def out_lo(s, t, n):
                dve.wait_ge(k_hi[s], 2 * n + 1)
                w = slice(s * 1024, s * 1024 + 512)
                split_lo(WL[:, 0, w], RAW[:, 0, w], WH[:, 0, w]).then_inc(k_lo[s], 1)
                dve.wait_ge(k_hi[s], 2 * n + 2)
                split_lo(ASTL[:, s, :], ACTT[:, bass.ds(2 * t + s, 1), :].rearrange("p a n -> p (a n)"), ASTH[:, s, :]).then_inc(k_lo[s], 1)

            def y_copy(f, half):
                for t in range(NT):
                    n = 2 * f + half
                    if t < NT - 1:
                        dve.wait_ge(out_done, (NT - 1) * n + t + 1)
                    else:
                        dve.wait_ge(k_mm[1], OUT_TURNS * (n + 1))
                    dve.tensor_copy(Y[:, t, half * 512:(half + 1) * 512], PS[:, t, :]).then_inc(y_copied, 1)

            def gate(r):
                w = 1.0 if r == 1 else 0.5
                dve.scalar_tensor_tensor(GATE[:, :, :], mod(3 * r + 2), w, gain(2 * r + 1), ALU.mult, ALU.mult).then_inc(gate_t, 1)

            def ffn_out(f):
                n0 = 2 * f * OUT_TURNS
                def turn(t):
                    for s in range(2):
                        out_lo(s, t, n0 + t)
                from_zero(dve, OUT_TURNS, turn)

                n0 += OUT_TURNS
                out_lo(0, 0, n0)
                y_copy(f, 0)
                out_lo(1, 0, n0)
                with dve.Fori(1, OUT_TURNS) as t:
                    for s in range(2):
                        out_lo(s, t, n0 + t)
                y_copy(f, 1)

            def residual(r):
                inverse_mean(1, y_sq, NT * (r + 1), y_ms)
                dve.wait_ge(y_rstd, r + 1)
                dve.wait_ge(gate_rows, 4 * (r + 1))

                def add(t):
                    dve.wait_ge(y_scaled, NT * r + t + 1)
                    dve.tensor_tensor(X[:, t, :], X[:, t, :], Y[:, t, :], ALU.add).then_inc(x_new, 1)

                for t in range(NT):
                    dve.scalar_tensor_tensor(Y[:, t, :], Y[:, t, :], RS[:, 1, t:t + 1], GATE_BUF[r][2][:, t // NTP, :],
                                             ALU.mult, ALU.mult).then_inc(y_scaled, 1)
                    if t:
                        add(t - 1)
                add(NT - 1)

            mods_known(ADA_FIRST, ADA_FIRST)
            norm(0)
            ffn_lo(0, 0)
            ffn_lo(1, 0)
            ada_lo(1, ADA_FIRST)
            ffn_lo(0, 1)
            with dve.Fori(1, FT - 1) as m:
                ffn_act(m - 1, m - 1)
                ffn_lo(1, m)
                ada_lo(1, ADA_FIRST + m)
                ada_mod(1, 2 * ADA_FIRST - 1 + m, ADA_FIRST - 1 + m)
                ffn_lo(0, m + 1)
            ffn_act(FT - 2, FT - 2)
            ffn_lo(1, FT - 1)
            ada_lo(1, ADA_FIRST + FT - 1)
            ada_mod(1, 2 * ADA_FIRST + FT - 2, ADA_FIRST + FT - 2)
            ffn_act(FT - 1, FT - 1)
            ada_mod(1, 2 * ADA_FIRST + FT - 1, ADA_FIRST + FT - 1)
            mods_known(ADA_FIRST, ADA_FIRST + FT)
            gate(0)
            ffn_out(0)
            with dve.Fori(0, ADA_REST) as t:
                ada_lo(0, ADA_FIRST + t)
                ada_lo(1, ADA_FIRST + FT + t)
                ada_mod(0, 2 * ADA_FIRST + FT + 2 * t, ADA_FIRST + t)
                ada_mod(1, 2 * ADA_FIRST + FT + 1 + 2 * t, ADA_FIRST + FT + t)
            mods_known(ADA_FIRST + ADA_REST, ADA_FIRST + FT + ADA_REST)
            residual(0)
            norm(1)

            def grp_lo(g, s):
                n = 4 * GROUPS[g][2]
                dve.wait_ge(g_hi[s], g + 1)
                split_lo(WL[:, s, 0:n], RAW[:, s, 0:n], WH[:, s, 0:n]).then_inc(g_lo[s], 1)

            def rope(n):
                t = n % NT
                dve.wait_ge(g_free, NT * (4 + n // NT) + t + 1)
                x = DQK[:, n % 2, :].rearrange("p (h a j) -> p h a j", h=2 * HD, j=8)
                tab = CON[:, CROPE + 24 * t:CROPE + 24 * t + 24].rearrange("p (x a j) -> p x a j", x=1, j=8)
                cos, nsin, sin = (tab[:, :, a, :].to_broadcast([P, 2 * HD, 8]) for a in range(3))
                dve.tensor_tensor(R1[:, n % 2, :, 0, :], x[:, :, 0, :], cos, ALU.mult)
                dve.tensor_tensor(R1[:, n % 2, :, 1, :], x[:, :, 1, :], cos, ALU.mult)
                dve.tensor_tensor(R2[:, n % 2, :, 0, :], x[:, :, 1, :], nsin, ALU.mult)
                link(dve.tensor_tensor(R2[:, n % 2, :, 1, :], x[:, :, 0, :], sin, ALU.mult))
                dve.tensor_tensor(x[:, :, 0:2, :], R1[:, n % 2, :, :, :], R2[:, n % 2, :, :, :], ALU.add).then_inc(rope_done, 1)

            def rope_copy(n):
                dve.wait_ge(rope_tr, n + 1)
                dst = DKT if n >= NT else DQT
                t = n % NT
                dve.tensor_copy(dst[:, :, t * P:(t + 1) * P], PS[:, 5 + n % 2, :].rearrange("p (h t) -> p h t", h=HD)).then_inc(rope_t, 1)

            grp_lo(0, 0)
            grp_lo(0, 1)
            dve.wait_ge(g_bank, 1)
            dve.memset(MVX[:, :, :, DV:DV + 1], 1.0)
            for g in range(7):
                if g < 6:
                    grp_lo(g + 1, 0)
                if g in (5, 6):
                    rope_copy(NT * (g - 4) - 1)
                if g in (4, 5):
                    for t in range(NT):
                        rope(NT * (g - 4) + t)
                        if t:
                            rope_copy(NT * (g - 4) + t - 1)
                if g < 6:
                    grp_lo(g + 1, 1)
            for s in range(2):
                grp_lo(7, s)

            dve.wait_ge(gates_tr, 1)
            dve.wait_ge(mst_landed, 16 * 10)
            dve.tensor_scalar(ROWA[:, 0:SEQ], PS[0:HM, 5, :], WSR[:, 8:9], None, ALU.add).then_inc(gates_row, 1)
            dve.tensor_scalar(ROWA[:, SEQ:TOK], PS[0:HM, 7, 0:P], WSR[:, 8:9], None, ALU.add).then_inc(gates_row, 1)
            dve.tensor_scalar(ROWB[:, 0:SEQ], PS[0:HM, 6, :], WSR[:, 9:10], None, ALU.add).then_inc(gates_row, 1)
            dve.tensor_scalar(ROWB[:, SEQ:TOK], PS[0:HM, 7, P:2 * P], WSR[:, 9:10], None, ALU.add).then_inc(gates_row, 1)
            for a in range(4):
                dve.wait_ge(q_tr, a + 1)
                dve.tensor_copy((MQT, MKT)[a // 2][:, a % 2, 0:SEQ], PS[:, a, :]).then_inc(q_t, 1)
            dve.wait_ge(q_tr, 5)
            dve.tensor_copy(MQT[:, :, SEQ:TOK], PS[:, 4, 0:2 * P].rearrange("p (j t) -> p j t", j=2))
            dve.tensor_copy(MKT[:, :, SEQ:TOK], PS[:, 4, 2 * P:4 * P].rearrange("p (j t) -> p j t", j=2)).then_inc(q_t, 1)
            dve.wait_ge(ln_f, 1)
            dve.wait_ge(gates_row, 4)
            link(dve.scalar_tensor_tensor(ROWB[:, :], ROWB[:, :], 0.0, ROWR[:, :], ALU.min, ALU.subtract))

            def pseg(T):
                return T[:, 0:SEQ].rearrange("h (c s) -> h c s", c=NTP)

            def sseg(T):
                return T[:, SEQ:TOK].rearrange("h (b s) -> h b s", b=DB)

            def col(a, n):
                return WSR[:, a:a + n].rearrange("h (c s) -> h c s", s=1)

            link(dve.memset(ROWM[:, :], 1.0))
            link(dve.memset(pseg(ROWM)[:, :, 0:1], 0.0))
            link(dve.memset(sseg(ROWM)[:, :, 0:1], 0.0))
            link(dve.tensor_tensor_scan(ROWI[:, :], ROWM[:, :], ROWB[:, :], 0.0, ALU.mult, ALU.add))
            link(dve.tensor_tensor(ROWA[:, :], ROWA[:, :], ROWI[:, :], ALU.subtract))
            link(dve.memset(ROWR[:, :], 0.0))
            link(dve.memset(sseg(ROWR)[:, :, 0:1], BIG))
            link(dve.tensor_copy(ROWB[:, SEQ:TOK], ROWA[:, SEQ:TOK]))
            link(dve.tensor_tensor(sseg(ROWB)[:, :, 0:1], sseg(ROWA)[:, :, 0:1], col(0, DB), ALU.max))
            link(dve.memset(WSR[:, 10:11], 0.0))
            for c in range(NTP):
                w, e = slice(c * P, (c + 1) * P), (c + 1) * P - 1
                link(dve.tensor_tensor_scan(ROWM[:, w], ROWR[:, w], ROWA[:, w], WSR[:, 10 + c:11 + c], ALU.add, ALU.max))
                link(dve.tensor_tensor(WSR[:, 11 + c:12 + c], ROWI[:, e:e + 1], ROWM[:, e:e + 1], ALU.add))
            link(dve.tensor_tensor_scan(ROWM[:, SEQ:TOK], ROWR[:, SEQ:TOK], ROWB[:, SEQ:TOK], 0.0, ALU.add, ALU.max))
            link(dve.tensor_tensor(col(16, DB), sseg(ROWI)[:, :, DS - 1:DS], sseg(ROWM)[:, :, DS - 1:DS], ALU.add))
            dve.tensor_tensor(col(24, NTP), col(10, NTP), pseg(ROWM)[:, :, P - 1:P], ALU.subtract)
            dve.tensor_tensor(col(28, DB), col(0, DB), sseg(ROWM)[:, :, DS - 1:DS], ALU.subtract).then_inc(seg_arg, 1)
            dve.tensor_tensor(pseg(ROWB), pseg(ROWA), pseg(ROWM)[:, :, P - 1:P].to_broadcast([HM, NTP, P]), ALU.subtract)
            dve.tensor_tensor(sseg(ROWB), sseg(ROWA), sseg(ROWM)[:, :, DS - 1:DS].to_broadcast([HM, DB, DS]), ALU.subtract)
            link(dve.scalar_tensor_tensor(ROWR[:, :], ROWI[:, :], -1.0, ROWM[:, :], ALU.mult, ALU.subtract))
            dve.tensor_tensor(pseg(ROWI), col(10, NTP).to_broadcast([HM, NTP, P]), pseg(ROWM), ALU.subtract)
            dve.tensor_tensor(sseg(ROWI), col(0, DB).to_broadcast([HM, DB, DS]), sseg(ROWM), ALU.subtract).then_inc(rows_ready, 1)
            dve.wait_ge(st_tr, 5)
            for a in range(2):
                r = slice(64 * a, 64 * a + 64)
                dve.tensor_copy(SCT[r, :, :, DV:DV + 1], PS[r, 4, 0:32].rearrange("p (r i h w) -> p i r h w", i=2, h=HM, w=1)[:, a, :, :, :]).then_inc(st_n, 1)
            dve.wait_ge(seg_exp, 1)
            dve.tensor_tensor(WSR[:, 48:80].rearrange("p (h b) -> p h b", h=HM), CON[0:HM, CDELTA:CDELTA + HM * DB].rearrange("p (h b) -> p h b", h=HM),
                              WSR[:, 40:48].rearrange("p (h b) -> p h b", h=1).to_broadcast([HM, HM, DB]), ALU.mult).then_inc(seg_d, 1)
            dve.wait_ge(seg_mm, 1)
            dve.tensor_copy(WSB[:, :], PS[:, 6, 0:40]).then_inc(seg_bc, 1)
            dve.tensor_copy(WS8[:, :], PS[0:DB, 6, 40:44]).then_inc(seg_bc, 1)
            dve.wait_ge(cols_exp, 2)
            dve.wait_ge(q_tr, 5)

            def per_head(a, t):
                return COLE[:, a, t, :].rearrange("p (h d) -> p h d", d=1).to_broadcast([P, HM, DQ])

            for t in range(NT):
                q4 = MQG[:, t, 0:256].rearrange("p (h d) -> p h d", h=HM)
                q = dve.tensor_tensor(q4, q4, per_head(0, t), ALU.mult)
            q.then_inc(qs_ready, 1)
            bmask = CON[:, CBM:CBM + DB]
            dve.tensor_tensor(WB[:, :, :], bmask.rearrange("p (h b) -> p h b", h=1).to_broadcast([P, HM, DB]),
                              COLE[:, 2, NTP, :].rearrange("p (h b) -> p h b", b=1).to_broadcast([P, HM, DB]), ALU.mult).then_inc(wb_ready, 1)
            dve.wait_ge(st_tr, 4)
            dve.wait_ge(seg_bc, 2)
            link(dve.tensor_tensor(SC[:, :, :, :], SC[:, :, :, :],
                                   WSB[:, 8:40].rearrange("p (h b d) -> p h b d", h=HM, d=1).to_broadcast([P, HM, DB, DQ]), ALU.mult))
            link(dve.tensor_tensor(NNAT[:, :, :], NNAT[:, :, :], WS8[:, :].rearrange("p (h d) -> p h d", d=1).to_broadcast([DB, HM, DQ]), ALU.mult))
            for j in range(2):
                dve.wait_ge(qs_tr, j + 1)
                dve.tensor_copy(QST[:, j, P:SEQ], PS[:, j, P:SEQ]).then_inc(qs_t, 1)
            dve.wait_ge(k_sent[0], 16 * 2)
            dve.wait_ge(k_sent[1], 16 * 3)

            for c in range(NT):
                dve.wait_ge(m_scores, 2 * (c + 1))
                if c:
                    dve.wait_ge(m_s, c)
                mask = CON[:, (CMS if c == NTP else CMP):(CMS if c == NTP else CMP) + P]
                for h in range(HM):
                    q = dve.scalar_tensor_tensor(ARG[:, h, :], PS[:, 2 + c % 2, h * P:(h + 1) * P], COLA[:, c, h:h + 1], mask, ALU.add, ALU.add)
                q.then_inc(m_arg, 1)
                if c:
                    dve.wait_ge(m_cu, c)
                dve.tensor_tensor(KW[:, :, :], MK[:, c, :].rearrange("p (h d) -> p h d", h=HM), per_head(2, c), ALU.mult).then_inc(m_kw, 1)
                dve.wait_ge(m_exp, c + 1)
                if c:
                    dve.wait_ge(m_hn, 2 * c)
                dve.tensor_tensor(ST[:, :, :], ARG[:, :, :], PS[:, c % 2, :].rearrange("p (h t) -> p h t", h=HM), ALU.mult).then_inc(m_s, 1)
                if c == NTP:
                    for h in range(HM):
                        if h:
                            dve.wait_ge(qb_tr, h)
                        dve.tensor_tensor(QB[:, :, :], MQG[:, c, h * DQ:(h + 1) * DQ].rearrange("p (b d) -> p b d", b=1).to_broadcast([P, DB, DQ]),
                                          bmask.rearrange("p (b d) -> p b d", d=1).to_broadcast([P, DB, DQ]), ALU.mult).then_inc(qb_ready, 1)
                else:
                    dve.wait_ge(m_cu, c + 1)
                    dve.wait_ge(m_hn, 2 * (c + 1))
                    for j in range(2):
                        cu = PS[:, 6, 129 * j:129 * j + DV + 1]
                        if c == 0:
                            q = dve.tensor_copy(CTX[:, j, :], cu)
                        else:
                            q = dve.scalar_tensor_tensor(CTX[:, j, :], CTX[:, j, :], WSB[:, 4 * j + c:4 * j + c + 1], cu, ALU.mult, ALU.add)
                    q.then_inc(m_state, 1)
                    dve.wait_ge(m_state, c + 1)
                for a in range(2):
                    dve.wait_ge(m_hn, 2 * c + a + 1)
                    hn = PS[:, 4 + a, 0:258].rearrange("p (h v) -> p h v", h=2)
                    den = DEN[:, c, a:HM:2].rearrange("p (h v) -> p h v", v=1)
                    link(dve.scalar_tensor_tensor(den, hn[:, :, DV:DV + 1], -1.0, COLE[:, 1, c, a:HM:2].rearrange("p (h v) -> p h v", v=1), ALU.mult, ALU.max))
                    link(dve.tensor_tensor(den, den, hn[:, :, DV:DV + 1], ALU.max))
                    link(dve.reciprocal(den, den))
                    dve.tensor_tensor(HHM[:, c, :].rearrange("p (h v) -> p h v", h=HM)[:, a:HM:2, :], hn[:, :, 0:DV],
                                      den.to_broadcast([P, 2, DV]), ALU.mult).then_inc(m_head, 1)
            for h in range(HM):
                dve.wait_ge(m_s, NT)
                if h:
                    dve.wait_ge(cu_s, h)
                dve.wait_ge(m_kw, NT)
                dve.tensor_tensor(KBM[:, :, :], KW[:, h, :].rearrange("p (b d) -> p b d", b=1).to_broadcast([P, DB, DQ]),
                                  bmask.rearrange("p (b d) -> p b d", d=1).to_broadcast([P, DB, DQ]), ALU.mult).then_inc(kb_ready, 1)
                dve.wait_ge(cu_s, h + 1)
                dve.tensor_tensor(SC[:, h, :, :], SC[:, h, :, :], PS[:, 6, :].rearrange("p (b d) -> p b d", b=DB), ALU.add).then_inc(c_new, 1)
            dve.wait_ge(n_mm, 1)
            dve.tensor_tensor(NNAT[:, :, :], NNAT[:, :, :], PS[0:DB, 7, 0:256].rearrange("p (h d) -> p h d", h=HM), ALU.add).then_inc(n_new, 1)

            dve.wait_ge(g_lam_landed, 16 * 3)
            dve.tensor_tensor(LAM[:, 0, :], LAM[:, 0, :], LAM[:, 1, :], ALU.mult)
            link(dve.tensor_tensor(LAM[:, 2, :], LAM[:, 2, :], LAM[:, 3, :], ALU.mult))
            dve.reduce_sum(LS[:, 0:1], LAM[:, 0, :], AXX)
            dve.reduce_sum(LS[:, 1:2], LAM[:, 2, :], AXX).then_inc(lam_s, 1)
            dve.wait_ge(lam_e, 1)
            link(dve.scalar_tensor_tensor(LS[:, 4:5], LS[:, 3:4], -LAM_INIT, LS[:, 2:3], ALU.add, ALU.subtract))
            link(dve.scalar_tensor_tensor(LS[:, 5:6], CON[:, CSIGN + 1:CSIGN + 2], LS[:, 4:5], CON[:, CSIGN:CSIGN + 1], ALU.mult, ALU.add))

            def p_maxima(n):
                nk, m = P * (n // HD + 1), 8 * (n % 2)
                dve.wait_ge(p_scores, n + 1)
                ps = PS[:, 2 * (n % 2):2 * (n % 2) + 2, 0:nk]
                link(dve.memset(ps[0:64, :, nk - 64:nk], BIG))
                if n >= 2:
                    dve.wait_ge(p_exp, 2 * (n - 1))
                link(dve.reduce_max(MX[:, m:m + 2], ps, AXX))
                dve.tensor_scalar(MX[:, m + 2:m + 4], MX[:, m:m + 2], -SCALE, None, ALU.mult).then_inc(p_max, 1)

            def p_combine(n):
                nk, m = P * (n // HD + 1), 8 * (n % 2)
                dve.wait_ge(p_exp, 2 * (n + 1))
                link(dve.reciprocal(MX[:, m + 6:m + 8], MX[:, m + 4:m + 6]))
                link(dve.tensor_tensor(MX[:, m + 7:m + 8], MX[:, m + 7:m + 8], LS[:, 4:5], ALU.mult))
                p0, p1 = PR[:, n % 2, 0, 0:nk], PR[:, n % 2, 1, 0:nk]
                link(dve.tensor_scalar(p0, p0, MX[:, m + 6:m + 7], None, ALU.mult))
                dve.scalar_tensor_tensor(p0, p1, MX[:, m + 7:m + 8], p0, ALU.mult, ALU.add).then_inc(p_comb, 1)

            last_n = NTP * HD
            p_maxima(0)
            for n in range(1, last_n):
                p_maxima(n)
                p_combine(n - 1)
            p_combine(last_n - 1)

            dve.wait_ge(c_new, HM)
            link(dve.memset(QBD[:, :, :, :], 0.0))
            for h in range(HD):
                for c in range(2):
                    r = slice(64 * c, 64 * c + 64)
                    q = dve.tensor_copy(QBD[r, :, h, 16 * c:16 * c + 16], DQT[r, h, SEQ:TOK].rearrange("p (b q) -> p b q", b=DB))
            q.then_inc(qbd_ready, 1)
            for b in range(DB):
                dve.wait_ge(s_ktr, 2 * b + 2)
                if b:
                    dve.wait_ge(s_scores, b)
                dve.tensor_copy(KCT[:, :, P:2 * P], PS[:, 6 * (b % 2) + 1, :].rearrange("p (h t) -> p h t", h=HD)).then_inc(s_ktd, 1)
                dve.wait_ge(s_scores, b + 1)
                m = 16 + 4 * (b % 2)
                if b >= 2:
                    dve.wait_ge(s_exp, b - 1)
                link(dve.reduce_max(MX[:, m:m + 1], PS[:, 2 + b % 2, 0:PAST + DS], AXX))
                dve.tensor_scalar(MX[:, m + 1:m + 2], MX[:, m:m + 1], -SCALE, None, ALU.mult).then_inc(s_max, 1)
                dve.wait_ge(s_exp, b + 1)
                link(dve.reciprocal(MX[:, m + 3:m + 4], MX[:, m + 2:m + 3]))
                if b:
                    dve.wait_ge(s_ptr, b)
                dve.tensor_scalar(MR[:, :], CON[:, CSEL:CSEL + 64], MX[:, m + 3:m + 4], LS[:, 5:6], ALU.mult, ALU.mult).then_inc(s_mr, 1)

            dve.wait_ge(gate_bc, 2)
            gate(1)
            for a, T in enumerate((HHM, HDF)):
                if a:
                    for s in range(2):
                        dve.wait_ge(ob_moved[s], 16 * (DB // 2))
                    dve.wait_ge(p_copied, NTP)
                flat = T[:, :, :].rearrange("p t (h v) -> p (t h) v", h=HM)
                link(dve.tensor_tensor(SQ[:, :, :], T[:, :, :], T[:, :, :], ALU.mult))
                hr = HR[:, a, :, :].rearrange("p t h -> p (t h)")
                link(dve.reduce_sum(hr, SQ[:, :, :].rearrange("p t (h v) -> p (t h) v", h=HM), AXX))
                link(dve.tensor_scalar(hr, hr, 1.0 / DV, EPS, ALU.mult, ALU.add))
                dve.reciprocal(hr, hr).then_inc(hd_ms, 1)
                dve.wait_ge(hd_rstd, a + 1)
                if a:
                    link(dve.tensor_scalar(hr, hr, 1.0 - LAM_INIT, None, ALU.mult))
                link(dve.tensor_tensor(flat, flat, hr.rearrange("p (t v) -> p t v", v=1).to_broadcast([P, NT * HM, DV]), ALU.mult))
                if a == 0:
                    link(dve.tensor_tensor(T[:, :, :], T[:, :, :], OG[:, :, :], ALU.mult))
                dve.tensor_tensor(T[:, :, :], T[:, :, :], GH[:, 512 * a:512 * a + 512].rearrange("p (t n) -> p t n", t=1).to_broadcast([P, NT, 512]),
                                  ALU.mult).then_inc(heads, 1)
            for k in range(KT):
                dve.wait_ge(hh_hi, k + 1)
                dve.tensor_tensor(HTL[:, k, 0:SEQ], PS[:, 4 + k % 2, :], HTH[:, k, 0:SEQ].bitcast(F32), ALU.subtract)
                dve.tensor_tensor(HTL[:, k, SEQ:TOK], PS[:, 6 + k % 2, 0:P], HTH[:, k, SEQ:TOK].bitcast(F32), ALU.subtract).then_inc(hh_lo, 1)

            def y_project(g):
                for t in range(NT):
                    dve.wait_ge(g_bank, NT * g + t + 1)
                    dve.tensor_copy(Y[:, t, (g - 7) * 512:(g - 6) * 512], PS[:, t, :]).then_inc(y_copied, 1)

            grp_lo(8, 0)
            y_project(7)
            grp_lo(8, 1)
            y_project(8)
            residual(1)
            norm(2)
            ffn_lo(0, FT)
            ffn_lo(1, FT)
            ffn_lo(0, FT + 1)
            with dve.Fori(1, FT - 1) as m:
                ffn_act(m - 1, FT + m - 1)
                ffn_lo(1, FT + m)
                ffn_lo(0, FT + m + 1)
            ffn_act(FT - 2, 2 * FT - 2)
            ffn_lo(1, 2 * FT - 1)
            ffn_act(FT - 1, 2 * FT - 1)
            dve.wait_ge(gate_bc, 4)
            gate(2)
            ffn_out(1)
            residual(2)
        @block.gpsimd
        def _(pool):
            def gate_broadcast(r):
                gp, gs, _ = GATE_BUF[r]
                pool.wait_ge(gate_t, r + 1)
                pool.tensor_copy(gp[:, :, :], GATE[:, :, 0:1].to_broadcast([P, KT, P])).then_inc(gate_bc, 1)
                for k in range(KT):
                    q = pool.tensor_copy(gs[:, k, :].rearrange("p (b s) -> p b s", b=DB),
                                         GATE[:, k, 1:NB].rearrange("p (b s) -> p b s", s=1).to_broadcast([P, DB, DS]))
                q.then_inc(gate_bc, 1)

            gate_broadcast(0)
            k_out = [o["k_prompt"].rearrange("l b (t p) h d -> p (l b t) (h d)", p=P)[:, t, :] for t in range(NTP)]
            k_out.append(o["k_sample"].rearrange("l b s h d -> (l b s) (h d)"))
            v_out = [o["v_prompt"].rearrange("l b (t p) h d -> p (l b t) (h d)", p=P)[:, t, :] for t in range(NTP)]
            v_out.append(o["v_sample"].rearrange("l b s h d -> (l b s) (h d)"))
            for t in range(NT):
                pool.wait_ge(rope_done, NT + t + 1)
                pool.dma_start(k_out[t], DQK[:, (NT + t) % 2, :]).then_inc(k_sent[(NT + t) % 2], 16)
            for t in range(NT):
                pool.wait_ge(g_free, 6 * NT + t + 1)
                pool.dma_start(v_out[t], DVT[:, t, :]).then_inc(kv_out, 16)
            pool.wait_ge(g_bank, 7 * NT)
            for h in range(HM):
                pool.dma_start(SC[:, h, :, :], i["state_C"].rearrange("l b h v d -> h v (l b) d")[h]).then_inc(mst_landed, 16)
            nsrc = i["state_n"].rearrange("l b h d -> (l b h) d")
            pool.dma_start(NROW[:, 0:DQ], nsrc).then_inc(mst_landed, 16)
            pool.dma_start(NROW[:, DQ:P], nsrc).then_inc(mst_landed, 16)
            pool.dma_start(NNAT[:, :, :].rearrange("b h d -> b (h d)"), i["state_n"].rearrange("l b h d -> (l b) (h d)")).then_inc(mst_landed, 16)
            with nc.allow_non_contiguous_dma(reason="a few numbers"):
                pool.dma_start(WSR[:, 0:DB], i["state_m"].rearrange("l b h -> (l h) b")).then_inc(mst_landed, 16)
                pool.dma_start(WSR[:, 8:9], i["b_igate"].rearrange("l h -> h l")).then_inc(mst_landed, 16)
                pool.dma_start(WSR[:, 9:10], i["b_fgate"].rearrange("l h -> h l")).then_inc(mst_landed, 16)
            pool.wait_ge(n_mm, 1)
            pool.dma_start(LAM[:, :, :].rearrange("p a d -> p (a d)"), i["lambda_qk"].rearrange("l a d -> l (a d)").to_broadcast([P, 4 * DQ])).then_inc(g_lam_landed, 16)
            pool.dma_start(GH[:, 0:512], i["g_mlstm"].rearrange("l h v -> l (h v)").to_broadcast([P, 512])).then_inc(g_lam_landed, 16)
            pool.dma_start(GH[:, 512:1024], i["g_diff"].rearrange("l h v -> l (h v)").to_broadcast([P, 512])).then_inc(g_lam_landed, 16)
            pool.wait_ge(seg_arg, 1)
            with nc.allow_non_contiguous_dma(reason="a few numbers"):
                pool.dma_start(o["m_prompt"].rearrange("l b h -> (l h) b"), WSR[:, 14:15]).then_inc(st_out, 16)
                pool.dma_start(o["m_sample"].rearrange("l b h -> (l h) b"), WSR[:, 16:24]).then_inc(st_out, 16)
            pool.wait_ge(fin_c, 1)
            for a in range(2):
                pool.dma_start(o["C_prompt"].rearrange("l b (j i) v d -> i v (l b j) d", i=2)[a],
                               ST[:, 0:2, 64 * a:64 * a + 64]).then_inc(st_out, 16)
            with nc.allow_non_contiguous_dma(reason="one column"):
                for j in range(2):
                    pool.dma_start(o["n_prompt"].rearrange("l b (j i) d -> j (l b i d)", i=2)[j].rearrange("(a b) -> a b", b=1), CTX[:, j, DV:DV + 1]).then_inc(st_out, 16)
            pool.wait_ge(c_new, HM)
            for h in range(HM):
                pool.dma_start(o["C_sample"].rearrange("l b h v d -> h v (l b) d")[h], SC[:, h, :, :]).then_inc(st_out, 16)
            pool.wait_ge(n_new, 1)
            pool.dma_start(o["n_sample"].rearrange("l b h d -> (l b) (h d)"), NNAT[:, :, :].rearrange("b h d -> b (h d)")).then_inc(st_out, 16)
            pool.wait_ge(st_out, 16 * 11)

            def cache_load(b):
                pool.dma_start(KC[:, b % 2, :, :], k_cache[:, b, :, :]).then_inc(cache_landed[b % 2], 16)
                pool.dma_start(VC[:, b % 2, :, :], v_cache[:, b, :, :]).then_inc(cache_landed[b % 2], 16)
                pool.dma_start(VN[:, b % 2, :], DVT[b * DS:(b + 1) * DS, NTP, :]).then_inc(cache_landed[b % 2], 16)

            cache_load(0)
            cache_load(1)
            for b in range(DB):
                pool.wait_ge(s_ob, b + 1)
                pool.dma_start(HDF[b * DS:(b + 1) * DS, NTP, :], OB[:, b % 2, :]).then_inc(ob_moved[b % 2], 16)
                if b + 2 < DB:
                    pool.wait_ge(s_o, b + 1)
                    cache_load(b + 2)
            gate_broadcast(1)
            gate_broadcast(2)
            pool.wait_ge(k_sent[0], 16 * 2)
            pool.wait_ge(k_sent[1], 16 * 3)
            pool.wait_ge(kv_out, 16 * NT)


_INS = ["x_prompt", "x_sample", "cache_k", "cache_v", "state_C", "state_n", "state_m", "c_prompt", "c_sample",
        "w_ada", "b_ada", "g_norm", "w_ffn1_in", "w_ffn1_out", "w_in", "b_igate", "b_fgate", "g_mlstm", "g_diff",
        "lambda_qk", "w_out", "w_ffn2_in", "w_ffn2_out"]
_OUTS = [("y_prompt", (1, SEQ, D)), ("y_sample", (DB, DS, D)),
         ("k_prompt", (1, 1, SEQ, HD, 2 * DQ)), ("v_prompt", (1, 1, SEQ, HD, DV)),
         ("C_prompt", (1, 1, HM, DV, DQ)), ("n_prompt", (1, 1, HM, DQ)), ("m_prompt", (1, 1, HM)),
         ("k_sample", (1, DB, DS, HD, 2 * DQ)), ("v_sample", (1, DB, DS, HD, DV)),
         ("C_sample", (1, DB, HM, DV, DQ)), ("n_sample", (1, DB, HM, DQ)), ("m_sample", (1, DB, HM))]


def kernel(**inputs):
    import numpy as np
    import concourse.bacc as bacc
    from concourse.bass_utils import run_bass_kernel_spmd

    nc = bacc.Bacc("TRN2", target_bir_lowering=False, num_devices=1)
    arrays, ins, outs = {}, {}, {}
    for name in _INS:
        a = np.ascontiguousarray(inputs[name])
        arrays[f"in_{name}"] = a
        ins[name] = nc.dram_tensor(f"in_{name}", a.shape, mybir.dt.from_np(a.dtype), kind="ExternalInput").ap()
    arrays["in_const"] = constants()
    ins["const"] = nc.dram_tensor("in_const", (P, CW), F32, kind="ExternalInput").ap()
    for name, shape in _OUTS:
        outs[name] = nc.dram_tensor(f"out_{name}", shape, F32, kind="ExternalOutput").ap()
    build(nc, ins, outs)
    r = run_bass_kernel_spmd(nc, [arrays], core_ids=[0])
    return tuple(r.results[0][f"out_{name}"] for name, _ in _OUTS)
```

```python
from contextlib import ExitStack

import concourse.bass as bass
from concourse import mybir

P = 128
D = 1024
KT = D // P
SEQ, DB, DS, PAST = 512, 8, 16, 256
TOK = SEQ + DB * DS
NT = TOK // P
NTP = SEQ // P
HALF = TOK // 2
DFF = 2816
FT = DFF // P
NADA = 9
NB = 1 + DB
HM = HD = 4
DQ, DV = 64, 128
EPS = 1e-6
LAM_INIT = 0.8 - 0.6
SCALE = float(DQ) ** -0.5
BIG = -1.0e30

UNIT = 2048
ADA_COLS = UNIT // KT
ADA_UNITS = NADA * D // ADA_COLS
ADA_FIRST = 2 * D // ADA_COLS // 2
ADA_OUT = ADA_UNITS - 2 * ADA_FIRST - FT
OUT_TURNS = FT // 2
C_MK, C_MV, C_MO, C_G, C_DQ, C_DK, C_DV = 256, 512, 1024, 1536, 1544, 2056, 2568
GROUPS = [("mq", 0, 256 + 2 * HM), ("mk", C_MK, 256), ("mv", C_MV, 512), ("mo", C_MO, 512),
          ("dq", C_DQ, 512), ("dk", C_DK, 512), ("dv", C_DV, 512), ("o0", 0, 512), ("o1", 512, 512)]

_c = 0
def _col(n):
    global _c
    _c += n
    return _c - n
CI, CMP, CMS, CBM = _col(P), _col(P), _col(P), _col(DB)
CSEL, CS18, CROPE = _col(HD * DS), _col(NB), _col(NT * 24)
CHEAD, CPAIR, CONE, CDELTA, CSIGN = _col(HM * P), _col(2 * P), _col(P), _col(HM * DB), _col(2)
CW = _c


def constants():
    import numpy as np
    c = np.zeros((P, CW), np.float32)
    i = np.arange(P)
    c[:, CI:CI + P] = np.eye(P)
    causal = i[:, None] <= i[None, :]
    c[:, CMP:CMP + P] = np.where(causal, 0, BIG)
    same = i[:, None] // DS == i[None, :] // DS
    c[:, CMS:CMS + P] = np.where(causal & same, 0, BIG)
    c[:, CBM:CBM + DB] = i[:, None] // DS == np.arange(DB)
    row_head, row_q = i // 32, i % DS
    c[:, CSEL:CSEL + 64] = (row_head[:, None] == np.arange(64) // DS) & (row_q[:, None] == np.arange(64) % DS)
    for r in range(NB):
        c[r, CS18 + r] = c[NB + r, CS18 + r] = 1
    f = np.float32
    inv = f(500000.0) ** (-np.arange(8, dtype=f) * f(2.0 / 16))
    pos = np.concatenate([np.arange(SEQ), np.tile(PAST + np.arange(DS), DB)]).astype(f)
    ang = pos[:, None] * inv[None, :]
    rope = np.concatenate([np.cos(ang), -np.sin(ang), np.sin(ang)], axis=1)
    c[:, CROPE:CROPE + NT * 24] = rope.reshape(NT, P, 24).transpose(1, 0, 2).reshape(P, NT * 24)
    for h in range(HM):
        c[h, CHEAD + h * P:CHEAD + (h + 1) * P] = -1
        c[h, CDELTA + h * DB:CDELTA + (h + 1) * DB] = 1
        c[h, CPAIR + (h // 2) * P + 64 * (h % 2):CPAIR + (h // 2) * P + 64 * (h % 2) + 64] = 1
    c[:, CONE:CONE + P] = 1
    c[:, CSIGN] = i // DS % 2 == 0
    c[:, CSIGN + 1] = i // DS % 2 == 1
    return c


def chain(eng, done):
    count = [0]

    def link(ins):
        count[0] += 1
        ins.then_inc(done, 1)
        eng.wait_ge(done, count[0])
        return ins
    return link


def from_zero(eng, turns, body):
    body(0)
    with eng.Fori(1, turns) as t:
        body(t)


ALU = mybir.AluOpType
ACT = mybir.ActivationFunctionType
AXX = mybir.AxisListType.X
F32 = mybir.dt.float32
F32R = mybir.dt.float32r
KB = 1024


def build(nc, i, o):
    with ExitStack() as ctx:
        base = (nc.sbuf_base + 31) // 32 * 32

        def at(name, off, shape, dt=F32):
            return nc.alloc_sbuf_tensor_at(name, shape, dt, offset=base + off)

        def sem(name):
            return ctx.enter_context(nc.semaphore(name))

        X = at("resid", 0, [P, NT, D])
        HTH = at("h_t_hi", 20 * KB, [P, KT, TOK], F32R)
        HTL = at("h_t_lo", 40 * KB, [P, KT, TOK], F32R)
        RAW = at("w_raw", 60 * KB, [P, 2, UNIT])
        WH = at("w_hi", 76 * KB, [P, 2, UNIT], F32R)
        WL = at("w_lo", 92 * KB, [P, 2, UNIT], F32R)
        FIX = 193 * KB
        CON = at("const", FIX, [P, CW])
        off = FIX + CW * 4
        def fixed(name, shape, dt=F32):
            nonlocal off
            n = 4
            for s in shape[1:]:
                n *= s
            off += -off % 32
            t = at(name, off, shape, dt)
            off += n
            return t
        MODT = fixed("mod_t", [P, NADA * KT, NB])
        BT = fixed("b_ada_t", [P, NADA * KT])
        GT = fixed("g_norm_t", [P, 6 * KT])
        CT = fixed("c_t", [P, KT, 2 * NB], F32R)
        SCA = fixed("scale_t", [P, KT, NB])
        GATE = fixed("gate_t", [P, KT, NB])
        AROW = fixed("mod_rows", [2 * NB, 2, ADA_COLS])
        SS = fixed("sum_squares", [P, 3, NT])
        RS = fixed("rstd", [P, 2, NT])
        NNAT = fixed("state_n", [DB, HM, DQ])
        ASTH = at("act_hi", 108 * KB, [P, 2, TOK], F32R)
        ASTL = at("act_lo", 113 * KB, [P, 2, TOK], F32R)
        SIL = at("silu_gate", 108 * KB, [P, TOK])
        Y = at("y", 118 * KB, [P, NT, D])
        ACTT = at("act_t", 138 * KB, [P, FT, TOK])
        XN = at("x_norm", 138 * KB, [P, NT, D])
        V = at("modulated", 158 * KB, [P, 2, TOK])
        CALL = at("c_all", 138 * KB, [NB, D])
        CSI = at("c_silu", 142 * KB, [NB, D])
        BG = at("b_g_rows", 146 * KB, [P, 2, P])
        GSP = at("gate_bc_prompt", 28 * KB, [P, KT, P])
        GSS = at("gate_bc_sample", 32 * KB, [P, KT, P])
        GB = at("gate_rows", 20 * KB, [P, 2, D])
        GATE_BUF = [(GSP, GSS, GB),
                    (at("gate_bc_prompt1", 164 * KB, [P, KT, P]), at("gate_bc_sample1", 168 * KB, [P, KT, P]),
                     at("gate_rows1", 172 * KB, [P, 2, D])),
                    (GSP, GSS, GB)]
        M0 = 108 * KB
        MQG = at("mq_gates", M0, [P, NT, 264]); M0 += 264 * NT * 4
        MK = at("mk", M0, [P, NT, 256]); M0 += 5 * KB
        MQT = at("mq_t", M0, [P, 2, TOK]); M0 += 5 * KB
        MKT = at("mk_t", M0, [P, 2, TOK]); M0 += 5 * KB
        QST = at("mq_scaled_t", M0, [P, 2, SEQ]); M0 += 4 * KB
        MVX = at("mv_ones", M0, [P, NT, HM, DV + 1]); M0 += NT * HM * (DV + 1) * 4 + 16
        OG = at("o_gate", M0, [P, NT, 512]); M0 += 10 * KB
        DVT = at("dv", M0, [P, NT, 512]); M0 += 10 * KB
        DQT = at("dq_t", M0, [P, HD, TOK]); M0 += 10 * KB
        DKT = at("dk_t", M0, [P, HD, TOK]); M0 += 10 * KB
        DQK = at("rope_in", M0, [P, 2, 512])
        R1 = at("rope_cos", M0 + 4 * KB, [P, 2, 2 * HD, 2, 8])
        R2 = at("rope_sin", M0 + 5 * KB, [P, 2, 2 * HD, 2, 8])
        HHM = at("mlstm_heads", M0, [P, NT, 512]); M0 += 10 * KB
        assert M0 <= FIX
        HDF = at("diff_heads", 108 * KB + 264 * NT * 4 + 19 * KB, [P, NT, 512])
        N0 = 20 * KB
        ROWA = at("row_a", N0, [HM, TOK]); N0 += 2560
        ROWB = at("row_b", N0, [HM, TOK]); N0 += 2560
        ROWM = at("row_m", N0, [HM, TOK]); N0 += 2560
        ROWI = at("row_inter", N0, [HM, TOK]); N0 += 2560
        ROWR = at("row_rows", N0, [HM, TOK]); N0 += 2560
        ARG = at("w_arg", N0, [P, HM, P]); N0 += 2 * KB
        KBM = at("k_by_batch", N0 - 2 * KB, [P, DB, DQ])
        ST = at("s_t", N0, [P, HM, P]); N0 += 2 * KB
        KW = at("k_weighted", N0, [P, HM, DQ]); N0 += KB
        CTX = at("state_t", N0, [P, 2, DV + 1]); N0 += 1056
        SC = at("state_c", N0, [P, HM, DB, DQ]); N0 += 8 * KB
        SCT = at("state_ct", N0, [P, DB // 2, HM, DV + 1]); N0 += 8256
        QB = at("q_by_batch", N0, [P, DB, DQ]); N0 += 2 * KB
        NROW = at("state_n_rows", N0 - 2 * KB, [32, P])
        QBT = at("q_by_batch_t", N0, [P, DB // 2, P]); N0 += 2 * KB
        COLA = at("col_a", N0, [P, NT, HM]); N0 += 96
        COLE = at("col_exp", N0, [P, 3, NT, HM]); N0 += 256
        WSR = at("seg_rows", N0, [HM, 96]); N0 += 384
        WSB = at("seg_bc", N0, [P, 40]); N0 += 160
        WS8 = at("seg_by_batch", N0, [DB, HM]); N0 += 32
        DEN = at("denominators", N0, [P, NT, HM]); N0 += 96
        WB = at("rows_by_batch", N0, [P, HM, DB]); N0 += 128
        assert N0 <= 60 * KB, N0
        A0 = 20 * KB
        PR = at("probs", A0, [P, 2, 2, 512]); A0 += 8 * KB
        PTT = at("probs_t", A0, [P, 2, 512]); A0 += 4 * KB
        KC = at("k_cache", A0, [P, 2, 2, 512]); A0 += 8 * KB
        VC = at("v_cache", A0, [P, 2, 2, 512]); A0 += 8 * KB
        KCT = [at("k_cache_t0", A0, [P, HD, PAST]), at("k_cache_t1", 20 * KB, [P, HD, PAST])]; A0 += 4 * KB
        QBD = at("q_blocks", A0, [P, DB, HD, 32]); A0 += 4 * KB
        VN = at("v_new", A0, [DS, 2, 512]); A0 += 4 * KB
        assert A0 <= 60 * KB
        B0 = 108 * KB
        GH = at("g_heads", B0, [P, D]); B0 += 4 * KB
        OBT = at("out_t", B0, [P, 512]); B0 += 2 * KB
        PS_ = at("probs_s", B0, [P, 2, PAST + DS]); B0 += 2 * KB + 192
        B0 = 108 * KB + 264 * NT * 4 + 5 * KB
        PTS = at("probs_s_t", B0, [P, 3, 64]); B0 += KB
        LAM = at("lambda", B0, [P, 4, DQ]); B0 += KB
        LS = at("lambda_s", B0, [P, 16]); B0 += 64
        MX = at("max_den", B0, [P, 32]); B0 += 128
        MR = at("combine", B0, [P, 64]); B0 += 256
        HR = at("head_rstd", B0, [P, 2, NT, HM]); B0 += 160
        SQD = at("squares", B0, [P, HM, DV])

        PS = ctx.enter_context(nc.psum_tensor("ps", [P, 8, 512], F32))
        ident = CON[:, CI:CI + P]

        small_landed = sem("small_landed")
        x_landed = sem("x_landed")
        c_silu = sem("c_silu")
        c_tr = sem("c_tr")
        c_hi = sem("c_hi")
        c_ready = sem("c_ready")
        a_landed = [sem(f"a_landed{s}") for s in range(2)]
        a_hi = [sem(f"a_hi{s}") for s in range(2)]
        a_lo = [sem(f"a_lo{s}") for s in range(2)]
        a_mm = [sem(f"a_mm{s}") for s in range(2)]
        a_row = [sem(f"a_row{s}") for s in range(2)]
        a_tr = [sem(f"a_tr{s}") for s in range(2)]
        a_mod = [sem(f"a_mod{s}") for s in range(2)]
        f_landed = [sem(f"f_landed{s}") for s in range(2)]
        f_hi = [sem(f"f_hi{s}") for s in range(2)]
        f_lo = [sem(f"f_lo{s}") for s in range(2)]
        f_mm = [sem(f"f_mm{s}") for s in range(2)]
        f_silu = sem("f_silu")
        f_act = sem("f_act")
        k_landed = [sem(f"k_landed{s}") for s in range(2)]
        k_hi = [sem(f"k_hi{s}") for s in range(2)]
        k_lo = [sem(f"k_lo{s}") for s in range(2)]
        k_mm = [sem(f"k_mm{s}") for s in range(2)]
        out_done = sem("out_done")
        y_copied = sem("y_copied")
        gate_t = sem("gate_t")
        gate_bc = sem("gate_bc")
        gate_mm = sem("gate_mm")
        gate_rows = sem("gate_rows")
        y_sq = sem("y_sq")
        y_ms = sem("y_ms")
        y_rstd = sem("y_rstd")
        x_new = sem("x_new")
        x_sq = sem("x_sq")
        x_ms = sem("x_ms")
        x_rstd = sem("x_rstd")
        x_norm = sem("x_norm")
        x_tr = sem("x_tr")
        sca_ready = sem("sca_ready")
        v_p = sem("v_p")
        v_s = sem("v_s")
        h_hi = sem("h_hi")
        h_lo = sem("h_lo")
        g_landed = [sem(f"g_landed{s}") for s in range(2)]
        g_hi = [sem(f"g_hi{s}") for s in range(2)]
        g_lo = [sem(f"g_lo{s}") for s in range(2)]
        g_half = sem("g_half")
        g_free = sem("g_free")
        k_sent = [sem(f"k_sent{s}") for s in range(2)]
        g_bank = sem("g_bank")
        rope_done = sem("rope_done")
        rope_tr = sem("rope_tr")
        rope_t = sem("rope_t")
        kv_out = sem("kv_out")
        dvec = sem("dve_chain")
        actc = sem("act_chain")
        q_tr = sem("q_tr")
        q_t = sem("q_t")
        gates_tr = sem("gates_tr")
        gates_row = sem("gates_row")
        ln_f = sem("ln_f")
        mst_landed = sem("mst_landed")
        rows_ready = sem("rows_ready")
        cols_tr = sem("cols_tr")
        cols_exp = sem("cols_exp")
        seg_exp = sem("seg_exp")
        seg_d = sem("seg_d")
        seg_mm = sem("seg_mm")
        seg_bc = sem("seg_bc")
        qs_ready = sem("qs_ready")
        qs_tr = sem("qs_tr")
        qs_t = sem("qs_t")
        st_tr = sem("st_tr")
        st_t = sem("st_t")
        m_even = sem("m_even")
        m_scores = sem("m_scores")
        m_arg = sem("m_arg")
        m_exp = sem("m_exp")
        m_s = sem("m_s")
        m_kw = sem("m_kw")
        m_cu = sem("m_cu")
        m_state = sem("m_state")
        m_hn = sem("m_hn")
        m_head = sem("m_head")
        qb_ready = sem("qb_ready")
        qb_tr = sem("qb_tr")
        qb_t = sem("qb_t")
        kb_ready = sem("kb_ready")
        cu_s = sem("cu_s")
        c_new = sem("c_new")
        n_mm = sem("n_mm")
        fin_tr = sem("fin_tr")
        fin_c = sem("fin_c")
        st_out = sem("st_out")
        g_lam_landed = sem("g_lam_landed")
        lam_e = sem("lam_e")
        p_scores = sem("p_scores")
        p_max = sem("p_max")
        p_exp = sem("p_exp")
        p_comb = sem("p_comb")
        p_tr = sem("p_tr")
        p_t = sem("p_t")
        p_o = sem("p_o")
        p_copied = sem("p_copied")
        kc_landed = [sem(f"kc_landed{s}") for s in range(2)]
        vc_landed = [sem(f"vc_landed{s}") for s in range(2)]
        poolc = sem("pool_memset")
        poold = sem("pool_chain")
        hd_sq = sem("hd_sq")
        s_tok = sem("s_tok")
        heads_s = sem("heads_s")
        qbd_ready = sem("qbd_ready")
        s_ktr = sem("s_ktr")
        s_scores = sem("s_scores")
        s_max = sem("s_max")
        s_exp = sem("s_exp")
        s_mr = sem("s_mr")
        s_ptr = sem("s_ptr")
        s_pt = sem("s_pt")
        s_o = sem("s_o")
        s_ob = sem("s_ob")
        hd_ms = sem("hd_ms")
        hd_rstd = sem("hd_rstd")
        heads = sem("heads")
        hh_tr = sem("hh_tr")
        seg_arg = sem("seg_arg")
        st_n = sem("st_n")
        wb_ready = sem("wb_ready")
        qb_mm = sem("qb_mm")
        lam_s = sem("lam_s")
        s_kta = sem("s_kta")
        s_ktd = sem("s_ktd")
        hh_hi = sem("hh_hi")
        hh_lo = sem("hh_lo")
        n_new = sem("n_new")
        y_out = sem("y_out")

        w_ada = i["w_ada"].rearrange("l (k p) n -> p (l k) n", p=P)
        ffn_in = [i[n].rearrange("l (k p) n -> p (l k) n", p=P) for n in ("w_ffn1_in", "w_ffn2_in")]
        ffn_out = [i[n].rearrange("l f n -> (l f) n") for n in ("w_ffn1_out", "w_ffn2_out")]
        w_in = i["w_in"].rearrange("l (k p) n -> p (l k) n", p=P)
        w_o = i["w_out"].rearrange("l (k p) n -> p (l k) n", p=P)
        x_p = i["x_prompt"].rearrange("b (t p) d -> p (b t) d", p=P)
        x_s = i["x_sample"].rearrange("b s d -> (b s) d")
        k_cache = i["cache_k"].rearrange("l b (k p) h d -> p (l b) k (h d)", p=P)
        v_cache = i["cache_v"].rearrange("l b (k p) h d -> p (l b) k (h d)", p=P)

        def ada_view(T, s):
            return T[:, s, :].rearrange("p (k n) -> p k n", k=KT)

        def ffn_view(T, s):
            return T[:, 0, s * 1024:(s + 1) * 1024].rearrange("p (k n) -> p k n", k=KT)

        def out_view(T, s):
            return T[:, 0, s * 1024:s * 1024 + 512]

        def grp_view(T, s, n):
            return T[:, s, 0:4 * n].rearrange("p (k n) -> p k n", k=4)

        block = ctx.enter_context(nc.Block())

        @block.sync
        def _(sp):
            sp.dma_start(CON[:, :], i["const"]).then_inc(small_landed, 16)
            sp.dma_start(CALL[0:1, :], i["c_prompt"]).then_inc(small_landed, 16)
            sp.dma_start(CALL[1:NB, :], i["c_sample"]).then_inc(small_landed, 16)
            sp.dma_start(BG[0:NADA * KT, 0, :], i["b_ada"].rearrange("l (r p) -> (l r) p", p=P)).then_inc(small_landed, 16)
            sp.dma_start(BG[0:6 * KT, 1, :], i["g_norm"].rearrange("l g (k p) -> (l g k) p", p=P)).then_inc(small_landed, 16)

            sp.dma_start(X[:, 0:NTP, :], x_p).then_inc(x_landed, 16)
            sp.dma_start(X[:, NTP, :], x_s).then_inc(x_landed, 16)

            def ada_load(s, unit, n):
                sp.wait_ge(a_hi[s], n)
                sp.wait_ge(a_lo[s], n)
                sp.dma_start(ada_view(RAW, s), w_ada[:, :, bass.ds(unit * ADA_COLS, ADA_COLS)]).then_inc(a_landed[s], 16)

            def turn(t):
                for s in range(2):
                    ada_load(s, 2 * t + s, t)
            from_zero(sp, ADA_FIRST, turn)


            def ffn_in_loads(f, m, n):
                for s in range(2):
                    sp.wait_ge(f_hi[s], n)
                    sp.wait_ge(f_lo[s], n)
                    sp.dma_start(ffn_view(RAW, s), ffn_in[f][:, :, bass.ds(m * P + s * DFF, P)]).then_inc(f_landed[s], 16)

            def ffn_out_loads(f):
                for half in range(2):
                    def turn(t, ada=False):
                        for s in range(2):
                            n = (2 * f + half) * OUT_TURNS + t
                            sp.wait_ge(k_hi[s], 2 * n)
                            sp.wait_ge(k_lo[s], 2 * n)
                            sp.dma_start(out_view(RAW, s), ffn_out[f][bass.ds((2 * t + s) * P, P), half * 512:(half + 1) * 512]).then_inc(k_landed[s], 16)
                            if ada and s == 0:
                                ada_load(1, 2 * ADA_FIRST + FT + t, ADA_FIRST + FT + t)

                    if f == 0 and half == 0:
                        from_zero(sp, ADA_OUT, lambda t: turn(t, True))
                        with sp.Fori(ADA_OUT, OUT_TURNS) as t:
                            turn(t)
                    else:
                        from_zero(sp, OUT_TURNS, turn)

            sp.wait_ge(a_hi[0], ADA_FIRST)
            sp.wait_ge(a_lo[0], ADA_FIRST)
            def turn(m):
                ffn_in_loads(0, m, m)
                ada_load(1, 2 * ADA_FIRST + m, ADA_FIRST + m)
            from_zero(sp, FT, turn)

            for s in range(2):
                sp.wait_ge(f_hi[s], FT)
                sp.wait_ge(f_lo[s], FT)
            ffn_out_loads(0)
            def mixer_loads():
                sp.wait_ge(g_bank, 7 * NT)
                for h in range(HM):
                    sp.dma_start(SC[:, h, :, :], i["state_C"].rearrange("l b h v d -> h v (l b) d")[h]).then_inc(mst_landed, 16)
                nsrc = i["state_n"].rearrange("l b h d -> (l b h) d")
                sp.dma_start(NROW[:, 0:DQ], nsrc).then_inc(mst_landed, 16)
                sp.dma_start(NROW[:, DQ:P], nsrc).then_inc(mst_landed, 16)
                sp.dma_start(NNAT[:, :, :].rearrange("b h d -> b (h d)"), i["state_n"].rearrange("l b h d -> (l b) (h d)")).then_inc(mst_landed, 16)
                with nc.allow_non_contiguous_dma(reason="a few numbers"):
                    sp.dma_start(WSR[:, 0:DB], i["state_m"].rearrange("l b h -> (l h) b")).then_inc(mst_landed, 16)
                    sp.dma_start(WSR[:, 8:9], i["b_igate"].rearrange("l h -> h l")).then_inc(mst_landed, 16)
                    sp.dma_start(WSR[:, 9:10], i["b_fgate"].rearrange("l h -> h l")).then_inc(mst_landed, 16)
                sp.wait_ge(n_mm, 1)
                sp.dma_start(LAM[:, :, :].rearrange("p a d -> p (a d)"), i["lambda_qk"].rearrange("l a d -> l (a d)").to_broadcast([P, 4 * DQ])).then_inc(g_lam_landed, 16)
                sp.dma_start(GH[:, 0:512], i["g_mlstm"].rearrange("l h v -> l (h v)").to_broadcast([P, 512])).then_inc(g_lam_landed, 16)
                sp.dma_start(GH[:, 512:1024], i["g_diff"].rearrange("l h v -> l (h v)").to_broadcast([P, 512])).then_inc(g_lam_landed, 16)

            sp.wait_ge(a_hi[1], ADA_FIRST + FT + ADA_OUT)
            sp.wait_ge(a_lo[1], ADA_FIRST + FT + ADA_OUT)
            for s in range(2):
                sp.wait_ge(k_hi[s], 4 * OUT_TURNS)
                sp.wait_ge(k_lo[s], 4 * OUT_TURNS)
            for g, (name, c0, n) in enumerate(GROUPS):
                if g == 8:
                    mixer_loads()
                w = w_in if g < 7 else w_o
                for s in range(2):
                    sp.wait_ge(g_hi[s], g)
                    sp.wait_ge(g_lo[s], g)
                    v = grp_view(RAW, s, n)
                    if g == 0:
                        sp.dma_start(v[:, :, 0:256], w[:, 4 * s:4 * s + 4, 0:256]).then_inc(g_landed[s], 16)
                        with nc.allow_non_contiguous_dma(reason="the gates' few columns"):
                            sp.dma_start(v[:, :, 256:264], w[:, 4 * s:4 * s + 4, C_G:C_G + 8]).then_inc(g_landed[s], 16)
                    else:
                        sp.dma_start(v, w[:, 4 * s:4 * s + 4, c0:c0 + n]).then_inc(g_landed[s], 16)
            sp.wait_ge(st_out, 16 * 11)
            def keys_load(b):
                sp.dma_start(KC[:, b % 2, :, :], k_cache[:, b, :, :]).then_inc(kc_landed[b % 2], 16)

            def values_load(b):
                sp.dma_start(VC[:, b % 2, :, :], v_cache[:, b, :, :]).then_inc(vc_landed[b % 2], 16)
                sp.dma_start(VN[:, b % 2, :], DVT[b * DS:(b + 1) * DS, NTP, :]).then_inc(vc_landed[b % 2], 16)

            for b in range(2):
                keys_load(b)
                values_load(b)
            for b in range(DB):
                if b + 2 < DB:
                    sp.wait_ge(s_ktr, 2 * (b + 1))
                    keys_load(b + 2)
                if 2 <= b + 1 < DB:
                    sp.wait_ge(s_o, b)
                    values_load(b + 1)
            for s in range(2):
                sp.wait_ge(g_hi[s], len(GROUPS))
                sp.wait_ge(g_lo[s], len(GROUPS))
            with sp.Fori(0, FT) as m:
                ffn_in_loads(1, m, FT + m)
            for s in range(2):
                sp.wait_ge(f_hi[s], 2 * FT)
                sp.wait_ge(f_lo[s], 2 * FT)
            ffn_out_loads(1)
            for t in range(NT):
                sp.wait_ge(x_new, 2 * NT + t + 1)
                dst = o["y_prompt"].rearrange("b (t p) d -> (b t) p d", p=P)[t] if t < NTP else o["y_sample"].rearrange("b s d -> (b s) d")
                sp.dma_start(dst, X[:, t, :]).then_inc(y_out, 16)
            sp.wait_ge(y_out, 16 * NT)

        @block.scalar
        def _(act):
            link = chain(act, actc)
            act.wait_ge(small_landed, 16 * 5)
            act.activation(CSI[:, :], CALL[:, :], ACT.Silu).then_inc(c_silu, 1)
            act.wait_ge(c_tr, 1)
            act.activation(CT[:, :, 0:NB], PS[:, 7, 0:KT * NB].rearrange("p (k b) -> p k b", k=KT), ACT.Copy).then_inc(c_hi, 1)

            def norm_rows(p):
                for t in range(NT):
                    if p == 0:
                        act.wait_ge(x_landed, 32)
                    else:
                        act.wait_ge(x_new, (p - 1) * NT + t + 1)
                    act.activation(XN[:, t, :], X[:, t, :], ACT.Square, accum_out=SS[:, 0, t:t + 1]).then_inc(x_sq, 1)
                act.wait_ge(x_ms, p + 1)
                act.activation(RS[:, 0, :], SS[:, 0, :], ACT.Sqrt).then_inc(x_rstd, 1)

            act.wait_ge(c_tr, 2)
            norm_rows(0)

            def ada_hi(s, n):
                act.wait_ge(a_landed[s], 16 * (n + 1))
                act.wait_ge(a_mm[s], n)
                act.activation(WH[:, s, :], RAW[:, s, :], ACT.Copy).then_inc(a_hi[s], 1)

            def ada_row(s, n):
                act.wait_ge(a_mm[s], n + 1)
                act.wait_ge(a_tr[s], n)
                act.activation(AROW[:, s, :], PS[0:2 * NB, 4 + s, 0:ADA_COLS], ACT.Copy).then_inc(a_row[s], 1)

            def turn(t):
                for s in range(2):
                    ada_hi(s, t)
                for s in range(2):
                    ada_row(s, t)

            from_zero(act, ADA_FIRST, turn)

            def norm(p, between=None):
                act.wait_ge(sca_ready, p + 1)

                def hi(k):
                    act.wait_ge(v_s, KT * p + k + 1)
                    act.wait_ge(v_p, KT * p + k + 1)
                    act.activation(HTH[:, k, :], V[:, k % 2, :], ACT.Copy).then_inc(h_hi, 1)

                shift = MODT[:, 3 * p * KT:(3 * p + 1) * KT, 0:1]
                for k in range(KT):
                    act.wait_ge(x_tr, KT * p + k + 1)
                    if k >= 2:
                        act.wait_ge(h_lo, KT * p + k - 1)
                    act.activation(V[:, k % 2, 0:SEQ], PS[:, 4 + k % 2, :], ACT.Identity, bias=shift[:, k, :],
                                   scale=SCA[:, k, 0:1]).then_inc(v_p, 1)
                    if between:
                        between(k)
                    if k >= 1:
                        hi(k - 1)
                hi(KT - 1)

            def ffn_hi(s, n):
                act.wait_ge(f_landed[s], 16 * (n + 1))
                act.wait_ge(f_mm[s], n)
                act.activation(WH[:, 0, s * 1024:(s + 1) * 1024], RAW[:, 0, s * 1024:(s + 1) * 1024], ACT.Copy).then_inc(f_hi[s], 1)

            def ffn_silu(n):
                act.wait_ge(f_mm[0], n + 1)
                act.wait_ge(f_act, n)
                act.activation(SIL[:, :].rearrange("p (a n) -> p a n", a=2), PS[:, 0:2, 0:HALF], ACT.Silu).then_inc(f_silu, 1)

            def out_hi(s, t, n):
                act.wait_ge(k_landed[s], 16 * (n + 1))
                act.wait_ge(k_mm[s], n)
                act.activation(WH[:, 0, s * 1024:s * 1024 + 512], RAW[:, 0, s * 1024:s * 1024 + 512], ACT.Copy).then_inc(k_hi[s], 1)
                act.activation(ASTH[:, s, :], ACTT[:, bass.ds(2 * t + s, 1), :].rearrange("p a n -> p (a n)"), ACT.Copy).then_inc(k_hi[s], 1)

            def gate_evac(r):
                for j in range(4):
                    act.wait_ge(gate_mm, 4 * r + j + 1)
                    act.activation(GATE_BUF[r][2][:, j // 2, 512 * (j % 2):512 * (j % 2) + 512], PS[:, 5 + j % 3, :], ACT.Copy).then_inc(gate_rows, 1)

            def y_squares(r, half, done):
                for t in range(NT):
                    act.wait_ge(*done(t))
                    act.activation(Y[:, t, half * 512:(half + 1) * 512], PS[:, t, :], ACT.Square, accum_out=SS[:, 1 + half, t:t + 1]).then_inc(y_sq, 1)

            def out_bank(f, half):
                n = 2 * f + half
                return lambda t: (out_done, (NT - 1) * n + t + 1) if t < NT - 1 else (k_mm[1], OUT_TURNS * (n + 1))

            def ffn_out(f):
                act.wait_ge(f_act, (f + 1) * FT)
                n0 = 2 * f * OUT_TURNS
                def turn(t, ada=False):
                    out_hi(0, t, n0 + t)
                    if ada:
                        ada_hi(1, ADA_FIRST + FT + t)
                    out_hi(1, t, n0 + t)
                    if ada:
                        ada_row(1, ADA_FIRST + FT + t)
                from_zero(act, ADA_OUT, lambda t: turn(t, f == 0))
                turn(ADA_OUT)
                gate_evac(2 * f)
                with act.Fori(ADA_OUT + 1, OUT_TURNS) as t:
                    turn(t)

                n0 += OUT_TURNS
                out_hi(0, 0, n0)
                y_squares(2 * f, 0, out_bank(f, 0))
                out_hi(1, 0, n0)
                with act.Fori(1, OUT_TURNS) as t:
                    for s in range(2):
                        out_hi(s, t, n0 + t)
                y_squares(2 * f, 1, out_bank(f, 1))

            def residual(r):
                act.wait_ge(y_ms, r + 1)
                act.activation(RS[:, 1, :], SS[:, 1, :], ACT.Sqrt).then_inc(y_rstd, 1)

            for s in range(2):
                act.wait_ge(a_mm[s], ADA_FIRST)
            norm(0, lambda k: ffn_hi(k, 0) if k < 2 else None)
            def turn(m):
                if not isinstance(m, int):
                    for s in range(2):
                        ffn_hi(s, m)
                ada_hi(1, ADA_FIRST + m)
                ffn_silu(m)
                ada_row(1, ADA_FIRST + m)
            from_zero(act, FT, turn)

            ffn_out(0)
            residual(0)
            norm_rows(1)

            def grp_hi(g, s):
                n = 4 * GROUPS[g][2]
                act.wait_ge(g_landed[s], 16 * (g + 2))
                act.activation(WH[:, s, 0:n], RAW[:, s, 0:n], ACT.Copy).then_inc(g_hi[s], 1)

            act.wait_ge(a_mm[1], ADA_FIRST + FT + ADA_OUT)
            for s in range(2):
                act.wait_ge(k_mm[s], 2 * OUT_TURNS)
            norm(1, lambda k: grp_hi(0, k) if k < 2 else None)

            def evac(g, t, out, cols, func=ACT.Copy, scale=1.0):
                act.wait_ge(g_bank, NT * g + t + 1)
                act.activation(out, cols, func, scale=scale).then_inc(g_free, 1)

            for g in range(7):
                if g < 6:
                    n = 4 * GROUPS[g + 1][2]
                    act.wait_ge(g_landed[0], 16 * (g + 3))
                    act.wait_ge(g_half, g + 1)
                    act.activation(WH[:, 0, 0:n], RAW[:, 0, 0:n], ACT.Copy).then_inc(g_hi[0], 1)
                for t in range(NT):
                    ps = PS[:, t, :]
                    if g == 0:
                        evac(g, t, MQG[:, t, :], ps[:, 0:264])
                    elif g == 1:
                        evac(g, t, MK[:, t, :], ps[:, 0:256], scale=DQ ** -0.5)
                    elif g == 2:
                        evac(g, t, MVX[:, t, :, 0:DV], ps.rearrange("p (h v) -> p h v", h=HM))
                    elif g == 3:
                        evac(g, t, OG[:, t, :], ps, ACT.Sigmoid)
                    elif g in (4, 5):
                        r = NT * (g - 4) + t
                        if r >= 2:
                            act.wait_ge(rope_tr, r - 1)
                            if r - 2 >= NT:
                                act.wait_ge(k_sent[r % 2], 16 * ((r - 2 - NT) // 2 + 1))
                        evac(g, t, DQK[:, r % 2, :], ps)
                    else:
                        evac(g, t, DVT[:, t, :], ps)
                if g < 6:
                    act.wait_ge(g_landed[1], 16 * (g + 3))
                    act.wait_ge(g_bank, NT * (g + 1))
                    act.activation(WH[:, 1, 0:n], RAW[:, 1, 0:n], ACT.Copy).then_inc(g_hi[1], 1)
            for s in range(2):
                n = 4 * GROUPS[7][2]
                act.wait_ge(g_landed[s], 16 * (7 + 2))
                act.activation(WH[:, s, 0:n], RAW[:, s, 0:n], ACT.Copy).then_inc(g_hi[s], 1)

            act.wait_ge(gates_row, 4)
            link(act.activation(ROWI[:, :], ROWB[:, :], ACT.Abs))
            link(act.activation(ROWI[:, :], ROWI[:, :], ACT.Exp, scale=-1.0))
            act.activation(ROWR[:, :], ROWI[:, :], ACT.Ln, bias=1.0).then_inc(ln_f, 1)
            for pr in range(DB // 2):
                act.wait_ge(st_tr, pr + 1)
                act.activation(SCT[:, pr, :, 0:DV], PS[:, pr, :].rearrange("p (h v) -> p h v", h=HM), ACT.Copy).then_inc(st_t, 1)
            act.wait_ge(seg_arg, 1)
            act.activation(WSR[:, 36:48], WSR[:, 24:36], ACT.Exp).then_inc(seg_exp, 1)
            act.wait_ge(cols_tr, 1)
            act.activation(COLA[:, :, :], PS[:, 5, 0:NT * HM].rearrange("p (t h) -> p t h", t=NT), ACT.Copy).then_inc(cols_exp, 1)
            act.activation(COLE[:, :, :, :].rearrange("p a t h -> p (a t h)"), PS[:, 5, NT * HM:4 * NT * HM], ACT.Exp).then_inc(cols_exp, 1)
            for c in range(NT):
                act.wait_ge(m_arg, c + 1)
                act.activation(ARG[:, :, :], ARG[:, :, :], ACT.Exp).then_inc(m_exp, 1)
            for h in range(HM):
                act.wait_ge(qb_tr, h + 1)
                if h in (1, 2):
                    act.wait_ge(qb_mm, h)
                elif h == 3:
                    act.wait_ge(m_hn, 2 * NTP + 1)
                act.activation(QBT[:, :, :], PS[:, 7, :].rearrange("p (r t) -> p r t", r=DB // 2), ACT.Copy).then_inc(qb_t, 1)
            act.wait_ge(fin_tr, 1)
            act.activation(ST[:, 0:2, :], PS[:, 2, 0:2 * P].rearrange("p (j v) -> p j v", j=2), ACT.Copy).then_inc(fin_c, 1)

            act.wait_ge(lam_s, 1)
            act.activation(LS[:, 2:4], LS[:, 0:2], ACT.Exp).then_inc(lam_e, 1)

            def p_evac(n):
                nk = P * (n // HD + 1)
                act.wait_ge(p_tr, n + 1)
                if n >= 2:
                    act.wait_ge(p_o, n - 1)
                act.activation(PTT[:, n % 2, 0:nk], PS[:, 4 + n % 2, 0:nk], ACT.Copy).then_inc(p_t, 1)

            def o_evac(n):
                if n % HD == HD - 1:
                    act.wait_ge(p_o, n + 1)
                    act.activation(HDF[:, n // HD, :], PS[:, 6 + n // HD % 2, :], ACT.Copy).then_inc(p_copied, 1)

            def head_squares(a, t, T):
                if t or a:
                    act.wait_ge(hd_sq, NT * a + t)
                for h in range(HM):
                    q = act.activation(SQD[:, h, :], T[:, h * DV:(h + 1) * DV], ACT.Square, accum_out=HR[:, a, t, h:h + 1])
                q.then_inc(hd_sq, 1)

            for n in range(NTP * HD):
                nk = P * (n // HD + 1)
                act.wait_ge(p_max, n + 1)
                if n >= 2:
                    act.wait_ge(p_tr, n - 1)
                m = 8 * (n % 2)
                for c in range(2):
                    act.activation(PR[:, n % 2, c, 0:nk], PS[:, 2 * (n % 2) + c, 0:nk], ACT.Exp, bias=MX[:, m + 2 + c:m + 3 + c],
                                   scale=SCALE, accum_out=MX[:, m + 4 + c:m + 5 + c]).then_inc(p_exp, 1)
                if n:
                    p_evac(n - 1)
                if n > 1:
                    o_evac(n - 2)
                if n < NT:
                    act.wait_ge(m_head, 2 * NT)
                    head_squares(0, n, HHM[:, n, :])
            p_evac(NTP * HD - 1)
            o_evac(NTP * HD - 2)
            o_evac(NTP * HD - 1)
            act.wait_ge(p_copied, NTP)
            for t in range(NTP):
                head_squares(1, t, HDF[:, t, :])

            def keys_t(b):
                act.wait_ge(s_ktr, 2 * b + 1)
                if b >= 2:
                    act.wait_ge(s_scores, b - 1)
                act.activation(KCT[b % 2][:, :, 0:P], PS[:, 6 * (b % 2), :].rearrange("p (h t) -> p h t", h=HD), ACT.Copy).then_inc(s_kta, 1)

            def probs_t(b):
                act.wait_ge(s_ptr, b + 1)
                if b:
                    act.wait_ge(s_o, b)
                act.activation(PTS[:, 0:2, :], PS[:, 4, 0:128].rearrange("p (k n) -> p k n", k=2), ACT.Copy).then_inc(s_pt, 1)
                act.activation(PTS[0:DS, 2, :], PS[0:DS, 4, 128:192], ACT.Copy).then_inc(s_pt, 1)

            keys_t(0)
            for b in range(DB):
                if b == 2:
                    act.wait_ge(hd_ms, 1)
                    act.activation(HR[:, 0, :, :], HR[:, 0, :, :], ACT.Sqrt).then_inc(hd_rstd, 1)
                    act.activation(HR[:, 1, 0:NTP, :], HR[:, 1, 0:NTP, :], ACT.Sqrt, scale=(1.0 - LAM_INIT) ** 2).then_inc(hd_rstd, 1)
                act.wait_ge(s_max, b + 1)
                if b >= 2:
                    act.wait_ge(s_ptr, b - 1)
                m = 16 + 4 * (b % 2)
                act.activation(PS_[:, b % 2, :], PS[:, 2 + b % 2, 0:PAST + DS], ACT.Exp, bias=MX[:, m + 1:m + 2], scale=SCALE,
                               accum_out=MX[:, m + 2:m + 3]).then_inc(s_exp, 1)
                if b + 1 < DB:
                    keys_t(b + 1)
                if b:
                    probs_t(b - 1)
            probs_t(DB - 1)
            act.wait_ge(s_o, DB)
            act.activation(OBT[:, :], PS[:, 5, :], ACT.Copy).then_inc(s_ob, 1)
            act.wait_ge(s_tok, 1)
            head_squares(1, NTP, PS[:, 2, :])
            act.wait_ge(hd_ms, 2)
            act.activation(HR[:, 1, NTP, :], HR[:, 1, NTP, :], ACT.Sqrt, scale=(1.0 - LAM_INIT) ** 2).then_inc(hd_rstd, 1)
            for k in range(KT):
                act.wait_ge(hh_tr, k + 1)
                act.activation(HTH[:, k, 0:SEQ], PS[:, 4 + k % 2, :], ACT.Copy)
                act.activation(HTH[:, k, SEQ:TOK], PS[:, 6 + k % 2, 0:P], ACT.Copy).then_inc(hh_hi, 1)
            gate_evac(1)
            act.wait_ge(g_half, 8)
            grp_hi(8, 0)
            y_squares(1, 0, lambda t: (g_bank, NT * 7 + t + 1))
            grp_hi(8, 1)
            y_squares(1, 1, lambda t: (g_bank, NT * 8 + t + 1))
            residual(1)
            norm_rows(2)
            act.wait_ge(g_half, 9)
            norm(2, lambda k: ffn_hi(k, FT) if k < 2 else None)
            ffn_silu(FT)
            with act.Fori(FT + 1, 2 * FT) as n:
                for s in range(2):
                    ffn_hi(s, n)
                ffn_silu(n)
            ffn_out(1)
            residual(2)
        @block.tensor
        def _(pe):
            def mm(out, lhsT, rhs, start=True, stop=True):
                return pe.matmul(out, lhsT, rhs, start=start, stop=stop)

            pe.wait_ge(small_landed, 16 * 5)
            pe.wait_ge(c_silu, 1)
            for k in range(KT):
                q = pe.transpose(PS[:, 7, k * NB:(k + 1) * NB], CSI[:, k * P:(k + 1) * P], ident[0:NB, 0:NB])
            q.then_inc(c_tr, 1)
            pe.transpose(PS[:, 6, 0:NADA * KT], BG[0:NADA * KT, 0, :], ident[0:NADA * KT, 0:NADA * KT])
            pe.transpose(PS[:, 6, P:P + 6 * KT], BG[0:6 * KT, 1, :], ident[0:6 * KT, 0:6 * KT]).then_inc(c_tr, 1)
            pe.wait_ge(c_ready, 3)

            def ada_mm(s, n):
                pe.wait_ge(a_hi[s], n + 1)
                pe.wait_ge(a_lo[s], n + 1)
                pe.wait_ge(a_row[s], n)
                wh, wl = ada_view(WH, s), ada_view(WL, s)
                for k in range(KT):
                    mm(PS[0:2 * NB, 4 + s, 0:ADA_COLS], CT[:, k, :], wh[:, k, :], k == 0, False)
                    q = mm(PS[0:NB, 4 + s, 0:ADA_COLS], CT[:, k, 0:NB], wl[:, k, :], False, k == KT - 1)
                q.then_inc(a_mm[s], 1)

            def ada_tr(s, n):
                pe.wait_ge(a_row[s], n + 1)
                pe.wait_ge(a_mod[s], n)
                for j in range(2):
                    q = mm(PS[:, 6 + s, j * NB:(j + 1) * NB], AROW[:, s, j * P:(j + 1) * P], CON[0:2 * NB, CS18:CS18 + NB])
                q.then_inc(a_tr[s], 1)

            def turn(t):
                for s in range(2):
                    ada_mm(s, t)
                for s in range(2):
                    ada_tr(s, t)
            from_zero(pe, ADA_FIRST, turn)

            for s in range(2):
                pe.wait_ge(a_row[s], ADA_FIRST)
                pe.wait_ge(a_mod[s], ADA_FIRST)

            def norm(p):
                pe.wait_ge(x_norm, NT * (p + 1))
                for k in range(KT):
                    if k >= 2:
                        pe.wait_ge(v_p, KT * p + k - 1)
                        pe.wait_ge(v_s, KT * p + k - 1)
                    for t in range(NT):
                        dst = PS[:, 4 + k % 2, t * P:(t + 1) * P] if t < NTP else PS[:, 6 + k % 2, 0:P]
                        q = pe.transpose(dst, XN[:, t, k * P:(k + 1) * P], ident)
                    q.then_inc(x_tr, 1)

            def ffn_mm(s, n, first_norm=None):
                pe.wait_ge(f_hi[s], n + 1)
                pe.wait_ge(f_lo[s], n + 1)
                pe.wait_ge(f_act if s else f_silu, n)
                wh, wl = ffn_view(WH, s), ffn_view(WL, s)
                for k in range(KT):
                    if first_norm is not None:
                        pe.wait_ge(h_hi, KT * first_norm + k + 1)
                        pe.wait_ge(h_lo, KT * first_norm + k + 1)
                    for w, h, first, last in ((wh, HTH, True, False), (wh, HTL, False, False), (wl, HTH, False, True)):
                        for a in range(2):
                            q = mm(PS[:, 2 * s + a, 0:HALF], w[:, k, :], h[:, k, a * HALF:(a + 1) * HALF],
                                   k == 0 and first, k == KT - 1 and last)
                q.then_inc(f_mm[s], 1)

            def out_mm(s, n, start=False, stop=False, before=None):
                pe.wait_ge(k_hi[s], 2 * (n + 1))
                pe.wait_ge(k_lo[s], 2 * (n + 1))
                for t in range(NT):
                    if before:
                        before(t)
                    th, tl = ASTH[:, s, t * P:(t + 1) * P], ASTL[:, s, t * P:(t + 1) * P]
                    mm(PS[:, t, :], th, out_view(WH, s), start, False)
                    mm(PS[:, t, :], th, out_view(WL, s), False, False)
                    q = mm(PS[:, t, :], tl, out_view(WH, s), False, stop)
                    if stop and t < NT - 1:
                        q.then_inc(out_done, 1)
                return q

            def ffn_out(f):
                for half in range(2):
                    n0 = (2 * f + half) * OUT_TURNS
                    def free(t):
                        if half:
                            pe.wait_ge(y_copied, 4 * NT * f + t + 1)

                    def with_ada(n, start=False):
                        out_mm(0, n, start=start).then_inc(k_mm[0], 1)
                        ada_mm(1, ADA_FIRST + FT + n)
                        out_mm(1, n).then_inc(k_mm[1], 1)
                        ada_tr(1, ADA_FIRST + FT + n)

                    def turns(first, end):
                        with pe.Fori(n0 + first, n0 + end) as n:
                            for s in range(2):
                                out_mm(s, n).then_inc(k_mm[s], 1)

                    if half == 0:
                        if f == 0:
                            with_ada(0, True)
                            with pe.Fori(1, ADA_OUT) as n:
                                with_ada(n)
                            pe.wait_ge(a_row[1], ADA_FIRST + FT + ADA_OUT)
                        else:
                            out_mm(0, n0, start=True).then_inc(k_mm[0], 1)
                            out_mm(1, n0).then_inc(k_mm[1], 1)
                            turns(1, ADA_OUT)
                        turns(ADA_OUT, ADA_OUT + 1)
                        if f == 0:
                            pe.wait_ge(a_mod[1], ADA_FIRST + FT + ADA_OUT)
                        gate_mms(2 * f)
                        turns(ADA_OUT + 1, OUT_TURNS - 1)
                    else:
                        out_mm(0, n0, start=True, before=free).then_inc(k_mm[0], 1)
                        out_mm(1, n0).then_inc(k_mm[1], 1)
                        turns(1, OUT_TURNS - 1)
                    out_mm(0, n0 + OUT_TURNS - 1).then_inc(k_mm[0], 1)
                    out_mm(1, n0 + OUT_TURNS - 1, stop=True).then_inc(k_mm[1], 1)

            def gate_mms(r):
                pe.wait_ge(gate_bc, 2 * (r + 1))
                for j in range(4):
                    if j == 3:
                        pe.wait_ge(gate_rows, 4 * r + 1)
                    for k in range(4):
                        q = mm(PS[:, 5 + j % 3, k * P:(k + 1) * P], GATE_BUF[r][j // 2][:, 4 * (j % 2) + k, :], ident)
                    q.then_inc(gate_mm, 1)

            norm(0)
            def turn(m):
                ffn_mm(0, m, 0 if isinstance(m, int) else None)
                ada_mm(1, ADA_FIRST + m)
                ffn_mm(1, m)
                ada_tr(1, ADA_FIRST + m)
            from_zero(pe, FT, turn)

            ffn_out(0)
            pe.wait_ge(gate_rows, 4)
            pe.wait_ge(y_copied, 2 * NT)
            norm(1)

            def project(g, s, t):
                n = GROUPS[g][2]
                if t == 0:
                    pe.wait_ge(g_hi[s], g + 1)
                    pe.wait_ge(g_lo[s], g + 1)
                if s == 0 and 1 <= g <= 7:
                    pe.wait_ge(g_free, NT * (g - 1) + t + 1)
                wh, wl = grp_view(WH, s, n), grp_view(WL, s, n)
                for k in range(4):
                    if g == 0 and s == 0 and t == 0:
                        pe.wait_ge(h_hi, KT + k + 1)
                        pe.wait_ge(h_lo, KT + k + 1)
                    th, tl = (T[:, 4 * s + k, t * P:(t + 1) * P] for T in (HTH, HTL))
                    mm(PS[:, t, 0:n], th, wh[:, k, :], s == 0 and k == 0, False)
                    mm(PS[:, t, 0:n], th, wl[:, k, :], False, False)
                    q = mm(PS[:, t, 0:n], tl, wh[:, k, :], False, s == 1 and k == 3)
                return q

            def rope_transposes(n):
                pe.wait_ge(rope_done, n + 1)
                if n >= 2:
                    pe.wait_ge(rope_t, n - 1)
                for h in range(HD):
                    q = pe.transpose(PS[:, 5 + n % 2, h * P:(h + 1) * P], DQK[:, n % 2, h * P:(h + 1) * P], ident)
                q.then_inc(rope_tr, 1)

            for g in range(7):
                for s in range(2):
                    for t in range(NT):
                        if g == 0 and s == 0 and t == 4:
                            pe.wait_ge(h_hi, 2 * KT)
                            pe.wait_ge(h_lo, 2 * KT)
                        q = project(g, s, t)
                        if s == 1:
                            q.then_inc(g_bank, 1)
                        elif t == NT - 1:
                            q.then_inc(g_half, 1)
                        if g in (4, 5) and s == 1 and t >= 1:
                            rope_transposes(NT * (g - 4) + t - 1)
                        if g in (5, 6) and s == 0 and t == 0:
                            rope_transposes(NT * (g - 5) + 4)

            pe.wait_ge(rope_t, 2 * NT)
            pe.wait_ge(g_free, 7 * NT)
            for c, (bank, off) in enumerate(((5, 0), (6, 0))):
                for t in range(NT):
                    dst = PS[0:HM, bank, t * P:(t + 1) * P] if t < NTP else PS[0:HM, 7, c * P:(c + 1) * P]
                    q = pe.transpose(dst, MQG[:, t, 256 + 4 * c:260 + 4 * c], ident)
            q.then_inc(gates_tr, 1)
            for a in range(5):
                for t in range(NTP) if a < 4 else (0, 1, 2, 3):
                    if a < 4:
                        src, j = (MQG, MK)[a // 2], a % 2
                        q = pe.transpose(PS[:, a, t * P:(t + 1) * P], src[:, t, j * P:(j + 1) * P], ident)
                    else:
                        src, j = (MQG, MK)[t // 2], t % 2
                        q = pe.transpose(PS[:, 4, t * P:(t + 1) * P], src[:, NTP, j * P:(j + 1) * P], ident)
                q.then_inc(q_tr, 1)
            pe.wait_ge(mst_landed, 16 * 10)
            for pr in range(DB // 2):
                pe.wait_ge(q_t, pr + 1)
                for h in range(HM):
                    q = pe.transpose(PS[:, pr, h * DV:(h + 1) * DV], SC[:, h, 2 * pr:2 * pr + 2, :], ident)
                q.then_inc(st_tr, 1)
            pe.wait_ge(q_t, 5)
            pe.transpose(PS[:, 4, 0:32], NROW[:, :], ident[0:32, 0:32]).then_inc(st_tr, 1)
            pe.wait_ge(rows_ready, 1)
            for a, row in enumerate((ROWA, ROWI, ROWR, ROWB)):
                for t in range(NT):
                    q = pe.transpose(PS[:, 5, (a * NT + t) * HM:(a * NT + t + 1) * HM], row[:, t * P:(t + 1) * P], ident[0:HM, 0:HM])
            q.then_inc(cols_tr, 1)
            pe.wait_ge(seg_exp, 1)
            pe.wait_ge(seg_d, 1)
            for j in range(2):
                mm(PS[:, 6, 4 * j:4 * j + 4], CON[0:HM, CPAIR + j * P:CPAIR + (j + 1) * P], WSR[:, 36:40])
            mm(PS[:, 6, 8:40], CON[0:HM, CONE:CONE + P], WSR[:, 48:80])
            pe.transpose(PS[0:DB, 6, 40:44], WSR[:, 40:48], ident[0:HM, 0:HM]).then_inc(seg_mm, 1)
            pe.wait_ge(qs_ready, 1)
            pe.wait_ge(st_t, 2)
            for j in range(2):
                for t in range(1, NTP):
                    q = pe.transpose(PS[:, j, t * P:(t + 1) * P], MQG[:, t, j * P:(j + 1) * P], ident)
                q.then_inc(qs_tr, 1)
            pe.wait_ge(qs_t, 2)
            pe.wait_ge(st_t, 4)
            pe.wait_ge(st_n, 2)
            pe.wait_ge(cols_exp, 2)
            pe.wait_ge(seg_bc, 2)

            def half(h):
                return slice(64 * (h % 2), 64 * (h % 2) + 64)

            for c in range(NT):
                tok = slice(c * P, (c + 1) * P)
                if c >= 2:
                    pe.wait_ge(m_s, c - 1)
                    pe.wait_ge(m_arg, c - 1)
                for h in (0, 2):
                    q = mm(PS[:, c % 2, h * P:(h + 1) * P], MKT[half(h), h // 2, tok], MQT[half(h), h // 2, tok])
                q.then_inc(m_even, 1)
                for h in range(HM):
                    q = mm(PS[:, 2 + c % 2, h * P:(h + 1) * P], CON[0:HM, CHEAD + h * P:CHEAD + (h + 1) * P], ROWM[:, tok])
                q.then_inc(m_scores, 1)
                pe.wait_ge(m_even, c + 1)
                for h in (1, 3):
                    q = mm(PS[:, c % 2, h * P:(h + 1) * P], MKT[half(h), h // 2, tok], MQT[half(h), h // 2, tok])
                q.then_inc(m_scores, 1)
                if c < NTP:
                    pe.wait_ge(m_kw, c + 1)
                    if c:
                        pe.wait_ge(m_state, c)
                    for h in range(HM):
                        o_ = 129 * (h // 2)
                        q = mm(PS[half(h), 6, o_:o_ + DV + 1], KW[:, h, :], MVX[:, c, h, :])
                    q.then_inc(m_cu, 1)
                pe.wait_ge(m_s, c + 1)
                if c:
                    pe.wait_ge(m_state, c)
                    pe.wait_ge(m_head, 2 * c)
                for h in range(HM):
                    out = PS[:, 4 + h % 2, 129 * (h // 2):129 * (h // 2) + DV + 1]
                    q = mm(out, ST[:, h, :], MVX[:, c, h, :], True, c == 0)
                    if 1 <= c < NTP:
                        q = mm(out, QST[half(h), h // 2, tok], CTX[half(h), h // 2, :], False, True)
                    elif c == NTP:
                        pe.wait_ge(qb_ready, h + 1)
                        if h:
                            pe.wait_ge(qb_t, h)
                        for r in range(DB // 2):
                            q = pe.transpose(PS[:, 7, r * P:(r + 1) * P], QB[:, 2 * r:2 * r + 2, :], ident)
                        q.then_inc(qb_tr, 1)
                        pe.wait_ge(qb_t, h + 1)
                        for r in range(DB // 2):
                            q = mm(out, QBT[:, r, :], SCT[:, r, h, :], False, r == DB // 2 - 1)
                        if h < 2:
                            q.then_inc(qb_mm, 1)
                    if h >= 2:
                        q.then_inc(m_hn, 1)
            for h in range(HM):
                pe.wait_ge(kb_ready, h + 1)
                if h:
                    pe.wait_ge(c_new, h)
                else:
                    pe.wait_ge(m_state, NTP)
                mm(PS[:, 6, :], MVX[:, NTP, h, 0:DV], KBM[:, :, :]).then_inc(cu_s, 1)
            pe.wait_ge(wb_ready, 1)
            pe.wait_ge(qb_t, HM)
            for h in range(HM):
                q = mm(PS[0:DB, 7, h * DQ:(h + 1) * DQ], WB[:, h, :], MK[:, NTP, h * DQ:(h + 1) * DQ])
            q.then_inc(n_mm, 1)
            pe.wait_ge(m_arg, NT)
            for j in range(2):
                q = pe.transpose(PS[:, 2, j * P:(j + 1) * P], CTX[:, j, 0:DV], ident)
            q.then_inc(fin_tr, 1)

            pe.wait_ge(fin_c, 1)
            pe.wait_ge(m_s, NT)
            pe.wait_ge(m_head, 2 * NT)
            pe.wait_ge(c_new, HM)
            pe.wait_ge(n_new, 1)

            def p_score(n):
                t, h = n // HD, n % HD
                if n >= 2:
                    pe.wait_ge(p_exp, 2 * (n - 1))
                for c in range(2):
                    q = mm(PS[:, 2 * (n % 2) + c, 0:P * (t + 1)], DQT[half(c), h, t * P:(t + 1) * P], DKT[half(c), h, 0:P * (t + 1)])
                q.then_inc(p_scores, 1)

            def p_transpose(n):
                pe.wait_ge(p_comb, n + 1)
                if n >= 2:
                    pe.wait_ge(p_t, n - 1)
                for k in range(n // HD + 1):
                    q = pe.transpose(PS[:, 4 + n % 2, k * P:(k + 1) * P], PR[:, n % 2, 0, k * P:(k + 1) * P], ident)
                q.then_inc(p_tr, 1)

            def p_out(n):
                t, h = n // HD, n % HD
                pe.wait_ge(p_t, n + 1)
                if t >= 2 and h == 0:
                    pe.wait_ge(p_copied, t - 1)
                for k in range(t + 1):
                    q = mm(PS[:, 6 + t % 2, h * DV:(h + 1) * DV], PTT[:, n % 2, k * P:(k + 1) * P], DVT[:, k, h * DV:(h + 1) * DV], k == 0, k == t)
                q.then_inc(p_o, 1)

            last_n = NTP * HD
            p_score(0)
            for n in range(last_n):
                if n + 1 < last_n:
                    p_score(n + 1)
                if n:
                    p_out(n - 1)
                p_transpose(n)
            p_out(last_n - 1)

            pe.wait_ge(p_exp, 2 * last_n)
            pe.wait_ge(p_copied, NTP)
            pe.wait_ge(qbd_ready, 1)

            def s_key_transposes(b):
                pe.wait_ge(kc_landed[b % 2], 16 * (b // 2 + 1))
                if b >= 2:
                    pe.wait_ge(s_kta, b - 1)
                    pe.wait_ge(s_ktd, b - 1)
                for k in range(2):
                    for h in range(HD):
                        q = pe.transpose(PS[:, 6 * (b % 2) + k, h * P:(h + 1) * P], KC[:, b % 2, k, h * P:(h + 1) * P], ident)
                    q.then_inc(s_ktr, 1)

            def s_score(b):
                pe.wait_ge(s_kta, b + 1)
                pe.wait_ge(s_ktd, b + 1)
                if b >= 2:
                    pe.wait_ge(s_exp, b - 1)
                for h in range(HD):
                    rows = slice(32 * h, 32 * h + 32)
                    mm(PS[rows, 2 + b % 2, 0:PAST], QBD[:, b, h, :], KCT[b % 2][:, h, :])
                    q = mm(PS[rows, 2 + b % 2, PAST:PAST + DS], QBD[:, b, h, :], DKT[:, h, SEQ + b * DS:SEQ + (b + 1) * DS])
                q.then_inc(s_scores, 1)

            def s_combine(b):
                pe.wait_ge(s_mr, b + 1)
                if b:
                    pe.wait_ge(s_pt, 2 * b)
                for k in range(3):
                    n = P if k < 2 else DS
                    q = mm(PS[0:n, 4, k * 64:(k + 1) * 64], PS_[:, b % 2, k * P:k * P + n], MR[:, :])
                q.then_inc(s_ptr, 1)

            def s_out(b):
                pe.wait_ge(s_pt, 2 * (b + 1))
                pe.wait_ge(vc_landed[b % 2], 32 * (b // 2 + 1))
                for h in range(HD):
                    cols, hq = slice(h * DV, (h + 1) * DV), slice(h * DS, (h + 1) * DS)
                    out = PS[:, 5, h * P + b * DS:h * P + (b + 1) * DS]
                    mm(out, VC[:, b % 2, 0, cols], PTS[:, 0, hq], True, False)
                    mm(out, VC[:, b % 2, 1, cols], PTS[:, 1, hq], False, False)
                    q = mm(out, VN[:, b % 2, cols], PTS[0:DS, 2, hq], False, True)
                q.then_inc(s_o, 1)

            s_key_transposes(0)
            for b in range(DB + 2):
                if b < DB:
                    s_score(b)
                if b + 1 < DB:
                    s_key_transposes(b + 1)
                if b >= 2:
                    s_out(b - 2)
                if 1 <= b <= DB:
                    s_combine(b - 1)
            pe.wait_ge(s_ob, 1)
            for h in range(HD):
                q = pe.transpose(PS[:, 2, h * P:(h + 1) * P], OBT[:, h * P:(h + 1) * P], ident)
            q.then_inc(s_tok, 1)

            for k in range(KT):
                if k == 0:
                    pe.wait_ge(heads, NT)
                elif k == 4:
                    pe.wait_ge(heads, NT + NTP)
                    pe.wait_ge(heads_s, 1)
                if k >= 2:
                    pe.wait_ge(hh_lo, k - 1)
                src = HHM if k < 4 else HDF
                for t in range(NT):
                    dst = PS[:, 4 + k % 2, t * P:(t + 1) * P] if t < NTP else PS[:, 6 + k % 2, 0:P]
                    q = pe.transpose(dst, src[:, t, (k % 4) * P:(k % 4 + 1) * P], ident)
                q.then_inc(hh_tr, 1)
            pe.wait_ge(hh_hi, KT)
            pe.wait_ge(hh_lo, KT)
            for g in (7, 8):
                for s in range(2):
                    if g == 7 and s == 1:
                        gate_mms(1)
                    for t in range(NT):
                        if s == 0 and g == 8:
                            pe.wait_ge(y_copied, 2 * NT + t + 1)
                        q = project(g, s, t)
                        if s == 1:
                            q.then_inc(g_bank, 1)
                        elif t == NT - 1:
                            q.then_inc(g_half, 1)
            norm(2)
            pe.wait_ge(y_copied, 4 * NT)
            ffn_mm(0, FT, 2)
            ffn_mm(1, FT)
            with pe.Fori(FT + 1, 2 * FT) as n:
                ffn_mm(0, n)
                ffn_mm(1, n)
            ffn_out(1)
        @block.vector
        def _(dve):
            link = chain(dve, dvec)
            dve.wait_ge(c_tr, 2)
            dve.wait_ge(c_hi, 1)
            dve.tensor_tensor(CT[:, :, NB:2 * NB], PS[:, 7, 0:KT * NB].rearrange("p (k b) -> p k b", k=KT),
                              CT[:, :, 0:NB].bitcast(F32), ALU.subtract).then_inc(c_ready, 1)
            dve.tensor_copy(BT[:, :], PS[:, 6, 0:NADA * KT]).then_inc(c_ready, 1)
            dve.tensor_copy(GT[:, :], PS[:, 6, P:P + 6 * KT]).then_inc(c_ready, 1)
            dve.wait_ge(c_ready, 3)

            def split_lo(dst, raw, hi):
                return dve.tensor_tensor(dst, raw, hi.bitcast(F32), ALU.subtract)

            def inverse_mean(col, squares, count, done):
                dve.wait_ge(squares, count)
                if col:
                    link(dve.tensor_tensor(SS[:, 1, :], SS[:, 1, :], SS[:, 2, :], ALU.add))
                link(dve.tensor_scalar(SS[:, col, :], SS[:, col, :], 1.0 / D, EPS, ALU.mult, ALU.add))
                dve.reciprocal(SS[:, col, :], SS[:, col, :]).then_inc(done, 1)

            def norm_rows(p):
                inverse_mean(0, x_sq, NT * (p + 1), x_ms)
                dve.wait_ge(x_rstd, p + 1)
                for t in range(NT):
                    dve.tensor_scalar(XN[:, t, :], X[:, t, :], RS[:, 0, t:t + 1], None, ALU.mult).then_inc(x_norm, 1)

            norm_rows(0)

            def ada_lo(s, n):
                dve.wait_ge(a_hi[s], n + 1)
                split_lo(WL[:, s, :], RAW[:, s, :], WH[:, s, :]).then_inc(a_lo[s], 1)

            def ada_mod(s, unit, n):
                dve.wait_ge(a_tr[s], n + 1)
                dve.tensor_tensor(MODT[:, bass.ds(2 * unit, 2), :], PS[:, 6 + s, 0:2 * NB].rearrange("p (j b) -> p j b", j=2),
                                  BT[:, bass.ds(2 * unit, 2)].rearrange("p (j b) -> p j b", b=1).to_broadcast([P, 2, NB]), ALU.add).then_inc(a_mod[s], 1)

            def turn(t):
                for s in range(2):
                    ada_lo(s, t)
                for s in range(2):
                    ada_mod(s, 2 * t + s, t)

            from_zero(dve, ADA_FIRST, turn)

            def gain(g):
                return GT[:, g * KT:(g + 1) * KT].rearrange("p (k b) -> p k b", b=1).to_broadcast([P, KT, NB])

            def mod(j):
                return MODT[:, j * KT:(j + 1) * KT, :]

            def mods_known(units0, units1):
                dve.wait_ge(a_mod[0], units0)
                dve.wait_ge(a_mod[1], units1)

            def norm(p, between=None):
                dve.scalar_tensor_tensor(SCA[:, :, :], mod(3 * p + 1), 1.0, gain(2 * p), ALU.add, ALU.mult).then_inc(sca_ready, 1)
                dve.wait_ge(sca_ready, p + 1)

                def lo(k):
                    dve.wait_ge(h_hi, KT * p + k + 1)
                    split_lo(HTL[:, k, :], V[:, k % 2, :], HTH[:, k, :]).then_inc(h_lo, 1)

                for k in range(KT):
                    dve.wait_ge(x_tr, KT * p + k + 1)
                    v = V[:, k % 2, SEQ:TOK].rearrange("p (b s) -> p b s", b=DB)
                    tr = PS[:, 6 + k % 2, 0:P].rearrange("p (b s) -> p b s", b=DB)
                    sc = SCA[:, k, 1:NB].rearrange("p (b s) -> p b s", s=1).to_broadcast([P, DB, DS])
                    sh = mod(3 * p)[:, k, 1:NB].rearrange("p (b s) -> p b s", s=1).to_broadcast([P, DB, DS])
                    if k >= 2:
                        dve.wait_ge(h_lo, KT * p + k - 1)
                    link(dve.tensor_tensor(v, tr, sc, ALU.mult))
                    dve.tensor_tensor(v, v, sh, ALU.add).then_inc(v_s, 1)
                    if between:
                        between(k)
                    if k >= 1:
                        lo(k - 1)
                lo(KT - 1)

            def ffn_lo(s, n):
                dve.wait_ge(f_hi[s], n + 1)
                w = slice(s * 1024, (s + 1) * 1024)
                split_lo(WL[:, 0, w], RAW[:, 0, w], WH[:, 0, w]).then_inc(f_lo[s], 1)

            def ffn_act(m, n):
                dve.wait_ge(f_mm[1], n + 1)
                dve.wait_ge(f_silu, n + 1)
                dve.tensor_tensor(ACTT[:, bass.ds(m, 1), :].rearrange("p m (a n) -> p (m a) n", a=2), SIL[:, :].rearrange("p (a n) -> p a n", a=2),
                                  PS[:, 2:4, 0:HALF], ALU.mult).then_inc(f_act, 1)

            def out_lo(s, t, n):
                dve.wait_ge(k_hi[s], 2 * n + 1)
                w = slice(s * 1024, s * 1024 + 512)
                split_lo(WL[:, 0, w], RAW[:, 0, w], WH[:, 0, w]).then_inc(k_lo[s], 1)
                dve.wait_ge(k_hi[s], 2 * n + 2)
                split_lo(ASTL[:, s, :], ACTT[:, bass.ds(2 * t + s, 1), :].rearrange("p a n -> p (a n)"), ASTH[:, s, :]).then_inc(k_lo[s], 1)

            def y_gated(r, half):
                for t in range(NT):
                    dve.wait_ge(y_sq, 2 * NT * r + NT * half + t + 1)
                    if t == 0 and half == 0:
                        dve.wait_ge(gate_rows, 4 * (r + 1))
                    cols = slice(half * 512, (half + 1) * 512)
                    dve.tensor_tensor(Y[:, t, cols], PS[:, t, :], GATE_BUF[r][2][:, t // NTP, cols], ALU.mult).then_inc(y_copied, 1)

            def gate(r):
                w = 1.0 if r == 1 else 0.5
                dve.scalar_tensor_tensor(GATE[:, :, :], mod(3 * r + 2), w, gain(2 * r + 1), ALU.mult, ALU.mult).then_inc(gate_t, 1)

            def ffn_out(f):
                n0 = 2 * f * OUT_TURNS
                def turn(t, ada=False):
                    out_lo(0, t, n0 + t)
                    if ada:
                        ada_lo(1, ADA_FIRST + FT + t)
                        ada_mod(1, 2 * ADA_FIRST + FT - 1 + t, ADA_FIRST + FT - 1 + t)
                    out_lo(1, t, n0 + t)
                from_zero(dve, ADA_OUT, lambda t: turn(t, f == 0))
                turn(ADA_OUT)
                if f == 0:
                    ada_mod(1, ADA_UNITS - 1, ADA_FIRST + FT + ADA_OUT - 1)
                with dve.Fori(ADA_OUT + 1, OUT_TURNS) as t:
                    turn(t)

                n0 += OUT_TURNS
                out_lo(0, 0, n0)
                y_gated(2 * f, 0)
                out_lo(1, 0, n0)
                with dve.Fori(1, OUT_TURNS) as t:
                    for s in range(2):
                        out_lo(s, t, n0 + t)
                y_gated(2 * f, 1)

            def residual(r):
                inverse_mean(1, y_sq, 2 * NT * (r + 1), y_ms)
                dve.wait_ge(y_rstd, r + 1)
                dve.wait_ge(y_copied, 2 * NT * (r + 1))
                for t in range(NT):
                    dve.scalar_tensor_tensor(X[:, t, :], Y[:, t, :], RS[:, 1, t:t + 1], X[:, t, :], ALU.mult, ALU.add).then_inc(x_new, 1)

            mods_known(ADA_FIRST, ADA_FIRST)
            norm(0, lambda k: ffn_lo(k - 1, 0) if k in (1, 2) else None)
            ada_lo(1, ADA_FIRST)
            ffn_lo(0, 1)
            with dve.Fori(1, FT - 1) as m:
                ffn_act(m - 1, m - 1)
                ffn_lo(1, m)
                ada_lo(1, ADA_FIRST + m)
                ada_mod(1, 2 * ADA_FIRST - 1 + m, ADA_FIRST - 1 + m)
                ffn_lo(0, m + 1)
            ffn_act(FT - 2, FT - 2)
            ffn_lo(1, FT - 1)
            ada_lo(1, ADA_FIRST + FT - 1)
            ada_mod(1, 2 * ADA_FIRST + FT - 2, ADA_FIRST + FT - 2)
            ffn_act(FT - 1, FT - 1)
            mods_known(ADA_FIRST, ADA_FIRST + FT - 1)
            gate(0)
            ffn_out(0)
            mods_known(ADA_FIRST, ADA_FIRST + FT + ADA_OUT)
            residual(0)
            norm_rows(1)

            def grp_lo(g, s):
                n = 4 * GROUPS[g][2]
                dve.wait_ge(g_hi[s], g + 1)
                split_lo(WL[:, s, 0:n], RAW[:, s, 0:n], WH[:, s, 0:n]).then_inc(g_lo[s], 1)

            norm(1, lambda k: grp_lo(0, k - 1) if k in (1, 2) else None)

            def rope(n):
                t = n % NT
                dve.wait_ge(g_free, NT * (4 + n // NT) + t + 1)
                x = DQK[:, n % 2, :].rearrange("p (h a j) -> p h a j", h=2 * HD, j=8)
                tab = CON[:, CROPE + 24 * t:CROPE + 24 * t + 24].rearrange("p (x a j) -> p x a j", x=1, j=8)
                cos, nsin, sin = (tab[:, :, a, :].to_broadcast([P, 2 * HD, 8]) for a in range(3))
                dve.tensor_tensor(R1[:, n % 2, :, 0, :], x[:, :, 0, :], cos, ALU.mult)
                dve.tensor_tensor(R1[:, n % 2, :, 1, :], x[:, :, 1, :], cos, ALU.mult)
                dve.tensor_tensor(R2[:, n % 2, :, 0, :], x[:, :, 1, :], nsin, ALU.mult)
                link(dve.tensor_tensor(R2[:, n % 2, :, 1, :], x[:, :, 0, :], sin, ALU.mult))
                dve.tensor_tensor(x[:, :, 0:2, :], R1[:, n % 2, :, :, :], R2[:, n % 2, :, :, :], ALU.add).then_inc(rope_done, 1)

            def rope_copy(n):
                dve.wait_ge(rope_tr, n + 1)
                dst = DKT if n >= NT else DQT
                t = n % NT
                dve.tensor_copy(dst[:, :, t * P:(t + 1) * P], PS[:, 5 + n % 2, :].rearrange("p (h t) -> p h t", h=HD)).then_inc(rope_t, 1)

            dve.wait_ge(g_bank, 1)
            dve.memset(MVX[:, :, :, DV:DV + 1], 1.0)
            for g in range(7):
                if g < 6:
                    grp_lo(g + 1, 0)
                if g in (5, 6):
                    rope_copy(NT * (g - 4) - 1)
                if g in (4, 5):
                    for t in range(NT):
                        rope(NT * (g - 4) + t)
                        if t:
                            rope_copy(NT * (g - 4) + t - 1)
                if g < 6:
                    grp_lo(g + 1, 1)
            for s in range(2):
                grp_lo(7, s)

            dve.wait_ge(gates_tr, 1)
            dve.wait_ge(mst_landed, 16 * 10)
            dve.tensor_scalar(ROWA[:, 0:SEQ], PS[0:HM, 5, :], WSR[:, 8:9], None, ALU.add).then_inc(gates_row, 1)
            dve.tensor_scalar(ROWA[:, SEQ:TOK], PS[0:HM, 7, 0:P], WSR[:, 8:9], None, ALU.add).then_inc(gates_row, 1)
            dve.tensor_scalar(ROWB[:, 0:SEQ], PS[0:HM, 6, :], WSR[:, 9:10], None, ALU.add).then_inc(gates_row, 1)
            dve.tensor_scalar(ROWB[:, SEQ:TOK], PS[0:HM, 7, P:2 * P], WSR[:, 9:10], None, ALU.add).then_inc(gates_row, 1)
            for a in range(4):
                dve.wait_ge(q_tr, a + 1)
                dve.tensor_copy((MQT, MKT)[a // 2][:, a % 2, 0:SEQ], PS[:, a, :]).then_inc(q_t, 1)
            dve.wait_ge(q_tr, 5)
            dve.tensor_copy(MQT[:, :, SEQ:TOK], PS[:, 4, 0:2 * P].rearrange("p (j t) -> p j t", j=2))
            dve.tensor_copy(MKT[:, :, SEQ:TOK], PS[:, 4, 2 * P:4 * P].rearrange("p (j t) -> p j t", j=2)).then_inc(q_t, 1)
            dve.wait_ge(ln_f, 1)
            dve.wait_ge(gates_row, 4)
            link(dve.scalar_tensor_tensor(ROWB[:, :], ROWB[:, :], 0.0, ROWR[:, :], ALU.min, ALU.subtract))

            def pseg(T):
                return T[:, 0:SEQ].rearrange("h (c s) -> h c s", c=NTP)

            def sseg(T):
                return T[:, SEQ:TOK].rearrange("h (b s) -> h b s", b=DB)

            def col(a, n):
                return WSR[:, a:a + n].rearrange("h (c s) -> h c s", s=1)

            link(dve.memset(ROWM[:, :], 1.0))
            link(dve.memset(pseg(ROWM)[:, :, 0:1], 0.0))
            link(dve.memset(sseg(ROWM)[:, :, 0:1], 0.0))
            link(dve.tensor_tensor_scan(ROWI[:, :], ROWM[:, :], ROWB[:, :], 0.0, ALU.mult, ALU.add))
            link(dve.tensor_tensor(ROWA[:, :], ROWA[:, :], ROWI[:, :], ALU.subtract))
            link(dve.memset(ROWR[:, :], 0.0))
            link(dve.memset(sseg(ROWR)[:, :, 0:1], BIG))
            link(dve.tensor_copy(ROWB[:, SEQ:TOK], ROWA[:, SEQ:TOK]))
            link(dve.tensor_tensor(sseg(ROWB)[:, :, 0:1], sseg(ROWA)[:, :, 0:1], col(0, DB), ALU.max))
            link(dve.memset(WSR[:, 10:11], 0.0))
            for c in range(NTP):
                w, e = slice(c * P, (c + 1) * P), (c + 1) * P - 1
                link(dve.tensor_tensor_scan(ROWM[:, w], ROWR[:, w], ROWA[:, w], WSR[:, 10 + c:11 + c], ALU.add, ALU.max))
                link(dve.tensor_tensor(WSR[:, 11 + c:12 + c], ROWI[:, e:e + 1], ROWM[:, e:e + 1], ALU.add))
            link(dve.tensor_tensor_scan(ROWM[:, SEQ:TOK], ROWR[:, SEQ:TOK], ROWB[:, SEQ:TOK], 0.0, ALU.add, ALU.max))
            link(dve.tensor_tensor(col(16, DB), sseg(ROWI)[:, :, DS - 1:DS], sseg(ROWM)[:, :, DS - 1:DS], ALU.add))
            dve.tensor_tensor(col(24, NTP), col(10, NTP), pseg(ROWM)[:, :, P - 1:P], ALU.subtract)
            dve.tensor_tensor(col(28, DB), col(0, DB), sseg(ROWM)[:, :, DS - 1:DS], ALU.subtract).then_inc(seg_arg, 1)
            dve.tensor_tensor(pseg(ROWB), pseg(ROWA), pseg(ROWM)[:, :, P - 1:P].to_broadcast([HM, NTP, P]), ALU.subtract)
            dve.tensor_tensor(sseg(ROWB), sseg(ROWA), sseg(ROWM)[:, :, DS - 1:DS].to_broadcast([HM, DB, DS]), ALU.subtract)
            link(dve.scalar_tensor_tensor(ROWR[:, :], ROWI[:, :], -1.0, ROWM[:, :], ALU.mult, ALU.subtract))
            dve.tensor_tensor(pseg(ROWI), col(10, NTP).to_broadcast([HM, NTP, P]), pseg(ROWM), ALU.subtract)
            dve.tensor_tensor(sseg(ROWI), col(0, DB).to_broadcast([HM, DB, DS]), sseg(ROWM), ALU.subtract).then_inc(rows_ready, 1)
            dve.wait_ge(st_tr, 5)
            for a in range(2):
                r = slice(64 * a, 64 * a + 64)
                dve.tensor_copy(SCT[r, :, :, DV:DV + 1], PS[r, 4, 0:32].rearrange("p (r i h w) -> p i r h w", i=2, h=HM, w=1)[:, a, :, :, :]).then_inc(st_n, 1)
            dve.wait_ge(seg_exp, 1)
            dve.tensor_tensor(WSR[:, 48:80].rearrange("p (h b) -> p h b", h=HM), CON[0:HM, CDELTA:CDELTA + HM * DB].rearrange("p (h b) -> p h b", h=HM),
                              WSR[:, 40:48].rearrange("p (h b) -> p h b", h=1).to_broadcast([HM, HM, DB]), ALU.mult).then_inc(seg_d, 1)
            dve.wait_ge(seg_mm, 1)
            dve.tensor_copy(WSB[:, :], PS[:, 6, 0:40]).then_inc(seg_bc, 1)
            dve.tensor_copy(WS8[:, :], PS[0:DB, 6, 40:44]).then_inc(seg_bc, 1)
            dve.wait_ge(cols_exp, 2)
            dve.wait_ge(q_tr, 5)

            def per_head(a, t):
                return COLE[:, a, t, :].rearrange("p (h d) -> p h d", d=1).to_broadcast([P, HM, DQ])

            for t in range(NT):
                q4 = MQG[:, t, 0:256].rearrange("p (h d) -> p h d", h=HM)
                q = dve.tensor_tensor(q4, q4, per_head(0, t), ALU.mult)
            q.then_inc(qs_ready, 1)
            bmask = CON[:, CBM:CBM + DB]
            dve.tensor_tensor(WB[:, :, :], bmask.rearrange("p (h b) -> p h b", h=1).to_broadcast([P, HM, DB]),
                              COLE[:, 2, NTP, :].rearrange("p (h b) -> p h b", b=1).to_broadcast([P, HM, DB]), ALU.mult).then_inc(wb_ready, 1)
            dve.wait_ge(st_tr, 4)
            dve.wait_ge(seg_bc, 2)
            link(dve.tensor_tensor(SC[:, :, :, :], SC[:, :, :, :],
                                   WSB[:, 8:40].rearrange("p (h b d) -> p h b d", h=HM, d=1).to_broadcast([P, HM, DB, DQ]), ALU.mult))
            link(dve.tensor_tensor(NNAT[:, :, :], NNAT[:, :, :], WS8[:, :].rearrange("p (h d) -> p h d", d=1).to_broadcast([DB, HM, DQ]), ALU.mult))
            for j in range(2):
                dve.wait_ge(qs_tr, j + 1)
                dve.tensor_copy(QST[:, j, P:SEQ], PS[:, j, P:SEQ]).then_inc(qs_t, 1)
            dve.wait_ge(k_sent[0], 16 * 2)
            dve.wait_ge(k_sent[1], 16 * 3)

            for c in range(NT):
                dve.wait_ge(m_scores, 2 * (c + 1))
                if c:
                    dve.wait_ge(m_s, c)
                mask = CON[:, (CMS if c == NTP else CMP):(CMS if c == NTP else CMP) + P]
                for h in range(HM):
                    q = dve.scalar_tensor_tensor(ARG[:, h, :], PS[:, 2 + c % 2, h * P:(h + 1) * P], COLA[:, c, h:h + 1], mask, ALU.add, ALU.add)
                q.then_inc(m_arg, 1)
                if c:
                    dve.wait_ge(m_cu, c)
                dve.tensor_tensor(KW[:, :, :], MK[:, c, :].rearrange("p (h d) -> p h d", h=HM), per_head(2, c), ALU.mult).then_inc(m_kw, 1)
                dve.wait_ge(m_exp, c + 1)
                if c:
                    dve.wait_ge(m_hn, 2 * c)
                dve.tensor_tensor(ST[:, :, :], ARG[:, :, :], PS[:, c % 2, :].rearrange("p (h t) -> p h t", h=HM), ALU.mult).then_inc(m_s, 1)
                if c == NTP:
                    for h in range(HM):
                        if h:
                            dve.wait_ge(qb_tr, h)
                        dve.tensor_tensor(QB[:, :, :], MQG[:, c, h * DQ:(h + 1) * DQ].rearrange("p (b d) -> p b d", b=1).to_broadcast([P, DB, DQ]),
                                          bmask.rearrange("p (b d) -> p b d", d=1).to_broadcast([P, DB, DQ]), ALU.mult).then_inc(qb_ready, 1)
                else:
                    dve.wait_ge(m_cu, c + 1)
                    dve.wait_ge(m_hn, 2 * (c + 1))
                    for j in range(2):
                        cu = PS[:, 6, 129 * j:129 * j + DV + 1]
                        if c == 0:
                            q = dve.tensor_copy(CTX[:, j, :], cu)
                        else:
                            q = dve.scalar_tensor_tensor(CTX[:, j, :], CTX[:, j, :], WSB[:, 4 * j + c:4 * j + c + 1], cu, ALU.mult, ALU.add)
                    q.then_inc(m_state, 1)
                    dve.wait_ge(m_state, c + 1)
                for a in range(2):
                    dve.wait_ge(m_hn, 2 * c + a + 1)
                    hn = PS[:, 4 + a, 0:258].rearrange("p (h v) -> p h v", h=2)
                    den = DEN[:, c, a:HM:2].rearrange("p (h v) -> p h v", v=1)
                    link(dve.scalar_tensor_tensor(den, hn[:, :, DV:DV + 1], -1.0, COLE[:, 1, c, a:HM:2].rearrange("p (h v) -> p h v", v=1), ALU.mult, ALU.max))
                    link(dve.tensor_tensor(den, den, hn[:, :, DV:DV + 1], ALU.max))
                    link(dve.reciprocal(den, den))
                    dve.tensor_tensor(HHM[:, c, :].rearrange("p (h v) -> p h v", h=HM)[:, a:HM:2, :], hn[:, :, 0:DV],
                                      den.to_broadcast([P, 2, DV]), ALU.mult).then_inc(m_head, 1)
            for h in range(HM):
                dve.wait_ge(m_s, NT)
                if h:
                    dve.wait_ge(cu_s, h)
                dve.wait_ge(m_kw, NT)
                dve.tensor_tensor(KBM[:, :, :], KW[:, h, :].rearrange("p (b d) -> p b d", b=1).to_broadcast([P, DB, DQ]),
                                  bmask.rearrange("p (b d) -> p b d", d=1).to_broadcast([P, DB, DQ]), ALU.mult).then_inc(kb_ready, 1)
                dve.wait_ge(cu_s, h + 1)
                dve.tensor_tensor(SC[:, h, :, :], SC[:, h, :, :], PS[:, 6, :].rearrange("p (b d) -> p b d", b=DB), ALU.add).then_inc(c_new, 1)
            dve.wait_ge(n_mm, 1)
            dve.tensor_tensor(NNAT[:, :, :], NNAT[:, :, :], PS[0:DB, 7, 0:256].rearrange("p (h d) -> p h d", h=HM), ALU.add).then_inc(n_new, 1)

            dve.wait_ge(g_lam_landed, 16 * 3)
            dve.tensor_tensor(LAM[:, 0, :], LAM[:, 0, :], LAM[:, 1, :], ALU.mult)
            link(dve.tensor_tensor(LAM[:, 2, :], LAM[:, 2, :], LAM[:, 3, :], ALU.mult))
            dve.reduce_sum(LS[:, 0:1], LAM[:, 0, :], AXX)
            dve.reduce_sum(LS[:, 1:2], LAM[:, 2, :], AXX).then_inc(lam_s, 1)
            dve.wait_ge(lam_e, 1)
            link(dve.scalar_tensor_tensor(LS[:, 4:5], LS[:, 3:4], -LAM_INIT, LS[:, 2:3], ALU.add, ALU.subtract))
            link(dve.scalar_tensor_tensor(LS[:, 5:6], CON[:, CSIGN + 1:CSIGN + 2], LS[:, 4:5], CON[:, CSIGN:CSIGN + 1], ALU.mult, ALU.add))

            def p_maxima(n):
                nk, m = P * (n // HD + 1), 8 * (n % 2)
                dve.wait_ge(p_scores, n + 1)
                ps = PS[:, 2 * (n % 2):2 * (n % 2) + 2, 0:nk]
                link(dve.memset(ps[0:64, :, nk - 64:nk], BIG))
                if n >= 2:
                    dve.wait_ge(p_exp, 2 * (n - 1))
                link(dve.reduce_max(MX[:, m:m + 2], ps, AXX))
                dve.tensor_scalar(MX[:, m + 2:m + 4], MX[:, m:m + 2], -SCALE, None, ALU.mult).then_inc(p_max, 1)

            def p_combine(n):
                nk, m = P * (n // HD + 1), 8 * (n % 2)
                dve.wait_ge(p_exp, 2 * (n + 1))
                link(dve.reciprocal(MX[:, m + 6:m + 8], MX[:, m + 4:m + 6]))
                link(dve.tensor_tensor(MX[:, m + 7:m + 8], MX[:, m + 7:m + 8], LS[:, 4:5], ALU.mult))
                p0, p1 = PR[:, n % 2, 0, 0:nk], PR[:, n % 2, 1, 0:nk]
                link(dve.tensor_scalar(p0, p0, MX[:, m + 6:m + 7], None, ALU.mult))
                dve.scalar_tensor_tensor(p0, p1, MX[:, m + 7:m + 8], p0, ALU.mult, ALU.add).then_inc(p_comb, 1)

            last_n = NTP * HD
            p_maxima(0)
            for n in range(last_n):
                p_combine(n)
                if n + 1 < last_n:
                    p_maxima(n + 1)

            def heads_ms(hr, count):
                dve.wait_ge(hd_sq, count)
                link(dve.tensor_scalar(hr, hr, 1.0 / DV, EPS, ALU.mult, ALU.add))
                dve.reciprocal(hr, hr).then_inc(hd_ms, 1)

            def keys_t(b):
                dve.wait_ge(s_ktr, 2 * b + 2)
                if b >= 2:
                    dve.wait_ge(s_scores, b - 1)
                dve.tensor_copy(KCT[b % 2][:, :, P:2 * P], PS[:, 6 * (b % 2) + 1, :].rearrange("p (h t) -> p h t", h=HD)).then_inc(s_ktd, 1)

            keys_t(0)
            for b in range(DB):
                dve.wait_ge(s_scores, b + 1)
                m = 16 + 4 * (b % 2)
                if b >= 2:
                    dve.wait_ge(s_exp, b - 1)
                link(dve.reduce_max(MX[:, m:m + 1], PS[:, 2 + b % 2, 0:PAST + DS], AXX))
                dve.tensor_scalar(MX[:, m + 1:m + 2], MX[:, m:m + 1], -SCALE, None, ALU.mult).then_inc(s_max, 1)
                if b + 1 < DB:
                    keys_t(b + 1)
                dve.wait_ge(s_exp, b + 1)
                link(dve.reciprocal(MX[:, m + 3:m + 4], MX[:, m + 2:m + 3]))
                if b:
                    dve.wait_ge(s_ptr, b)
                dve.tensor_scalar(MR[:, :], CON[:, CSEL:CSEL + 64], MX[:, m + 3:m + 4], LS[:, 5:6], ALU.mult, ALU.mult).then_inc(s_mr, 1)
                if b == 0:
                    heads_ms(HR[:, :, :, :].rearrange("p a t h -> p (a t h)")[:, 0:(NT + NTP) * HM], NT + NTP)
                if b == 1:
                    dve.wait_ge(gate_bc, 2)
                    gate(1)
            heads_ms(HR[:, 1, NTP, :], 2 * NT)
            dve.wait_ge(hd_rstd, 3)
            for h in range(HD):
                cols = slice(h * DV, (h + 1) * DV)
                q = dve.scalar_tensor_tensor(HDF[:, NTP, cols], PS[:, 2, cols], HR[:, 1, NTP, h:h + 1], GH[:, 512 + h * DV:512 + (h + 1) * DV], ALU.mult, ALU.mult)
            q.then_inc(heads_s, 1)
            for k in range(KT):
                dve.wait_ge(hh_hi, k + 1)
                dve.tensor_tensor(HTL[:, k, 0:SEQ], PS[:, 4 + k % 2, :], HTH[:, k, 0:SEQ].bitcast(F32), ALU.subtract)
                dve.tensor_tensor(HTL[:, k, SEQ:TOK], PS[:, 6 + k % 2, 0:P], HTH[:, k, SEQ:TOK].bitcast(F32), ALU.subtract).then_inc(hh_lo, 1)

            grp_lo(8, 0)
            y_gated(1, 0)
            grp_lo(8, 1)
            y_gated(1, 1)
            residual(1)
            norm_rows(2)
            norm(2, lambda k: ffn_lo(k - 1, FT) if k in (1, 2) else None)
            ffn_lo(0, FT + 1)
            with dve.Fori(1, FT - 1) as m:
                ffn_act(m - 1, FT + m - 1)
                ffn_lo(1, FT + m)
                ffn_lo(0, FT + m + 1)
            ffn_act(FT - 2, 2 * FT - 2)
            ffn_lo(1, 2 * FT - 1)
            ffn_act(FT - 1, 2 * FT - 1)
            dve.wait_ge(gate_bc, 4)
            gate(2)
            ffn_out(1)
            residual(2)
        @block.gpsimd
        def _(pool):
            def gate_broadcast(r):
                gp, gs, _ = GATE_BUF[r]
                pool.wait_ge(gate_t, r + 1)
                pool.tensor_copy(gp[:, :, :], GATE[:, :, 0:1].to_broadcast([P, KT, P])).then_inc(gate_bc, 1)
                for k in range(KT):
                    q = pool.tensor_copy(gs[:, k, :].rearrange("p (b s) -> p b s", b=DB),
                                         GATE[:, k, 1:NB].rearrange("p (b s) -> p b s", s=1).to_broadcast([P, DB, DS]))
                q.then_inc(gate_bc, 1)

            gate_broadcast(0)
            k_out = [o["k_prompt"].rearrange("l b (t p) h d -> p (l b t) (h d)", p=P)[:, t, :] for t in range(NTP)]
            k_out.append(o["k_sample"].rearrange("l b s h d -> (l b s) (h d)"))
            v_out = [o["v_prompt"].rearrange("l b (t p) h d -> p (l b t) (h d)", p=P)[:, t, :] for t in range(NTP)]
            v_out.append(o["v_sample"].rearrange("l b s h d -> (l b s) (h d)"))
            for t in range(NT):
                pool.wait_ge(rope_done, NT + t + 1)
                pool.dma_start(k_out[t], DQK[:, (NT + t) % 2, :]).then_inc(k_sent[(NT + t) % 2], 16)
            for t in range(NT):
                pool.wait_ge(g_free, 6 * NT + t + 1)
                pool.dma_start(v_out[t], DVT[:, t, :]).then_inc(kv_out, 16)
            pool.wait_ge(seg_arg, 1)
            with nc.allow_non_contiguous_dma(reason="a few numbers"):
                pool.dma_start(o["m_prompt"].rearrange("l b h -> (l h) b"), WSR[:, 14:15]).then_inc(st_out, 16)
                pool.dma_start(o["m_sample"].rearrange("l b h -> (l h) b"), WSR[:, 16:24]).then_inc(st_out, 16)
            pool.wait_ge(fin_c, 1)
            for a in range(2):
                pool.dma_start(o["C_prompt"].rearrange("l b (j i) v d -> i v (l b j) d", i=2)[a],
                               ST[:, 0:2, 64 * a:64 * a + 64]).then_inc(st_out, 16)
            with nc.allow_non_contiguous_dma(reason="one column"):
                for j in range(2):
                    pool.dma_start(o["n_prompt"].rearrange("l b (j i) d -> j (l b i d)", i=2)[j].rearrange("(a b) -> a b", b=1), CTX[:, j, DV:DV + 1]).then_inc(st_out, 16)
            pool.wait_ge(c_new, HM)
            for h in range(HM):
                pool.dma_start(o["C_sample"].rearrange("l b h v d -> h v (l b) d")[h], SC[:, h, :, :]).then_inc(st_out, 16)
            pool.wait_ge(n_new, 1)
            pool.dma_start(o["n_sample"].rearrange("l b h d -> (l b) (h d)"), NNAT[:, :, :].rearrange("b h d -> b (h d)")).then_inc(st_out, 16)
            pool.wait_ge(st_out, 16 * 11)
            pool.wait_ge(c_new, HM)
            pool.memset(QBD[:, :, :, :], 0.0).then_inc(poolc, 1)
            pool.wait_ge(poolc, 1)
            for h in range(HD):
                for c in range(2):
                    r = slice(64 * c, 64 * c + 64)
                    q = pool.tensor_copy(QBD[r, :, h, 16 * c:16 * c + 16], DQT[r, h, SEQ:TOK].rearrange("p (b q) -> p b q", b=DB))
            q.then_inc(qbd_ready, 1)
            link = chain(pool, poold)
            pool.wait_ge(qbd_ready, 1)
            pool.wait_ge(g_lam_landed, 16 * 3)
            for t in range(NT):
                q = pool.tensor_tensor(OG[:, t, :], OG[:, t, :], GH[:, 0:512], ALU.mult)
            link(q)
            for t in range(NT):
                pool.wait_ge(hd_sq, t + 1)
                q = pool.tensor_tensor(HHM[:, t, :], HHM[:, t, :], OG[:, t, :], ALU.mult)
            link(q)
            for t in range(NTP):
                pool.wait_ge(hd_sq, NT + t + 1)
                q = pool.tensor_tensor(HDF[:, t, :], HDF[:, t, :], GH[:, 512:1024], ALU.mult)
            link(q)
            pool.wait_ge(hd_rstd, 2)
            for a, T in enumerate((HHM, HDF)):
                for t in range(NT if a == 0 else NTP):
                    heads4 = T[:, t, :].rearrange("p (h v) -> p h v", h=HM)
                    pool.tensor_tensor(heads4, heads4, HR[:, a, t, :].rearrange("p (h v) -> p h v", v=1).to_broadcast([P, HM, DV]), ALU.mult).then_inc(heads, 1)
            pool.wait_ge(s_scores, DB)
            gate_broadcast(1)
            gate_broadcast(2)
            pool.wait_ge(k_sent[0], 16 * 2)
            pool.wait_ge(k_sent[1], 16 * 3)
            pool.wait_ge(kv_out, 16 * NT)


_INS = ["x_prompt", "x_sample", "cache_k", "cache_v", "state_C", "state_n", "state_m", "c_prompt", "c_sample",
        "w_ada", "b_ada", "g_norm", "w_ffn1_in", "w_ffn1_out", "w_in", "b_igate", "b_fgate", "g_mlstm", "g_diff",
        "lambda_qk", "w_out", "w_ffn2_in", "w_ffn2_out"]
_OUTS = [("y_prompt", (1, SEQ, D)), ("y_sample", (DB, DS, D)),
         ("k_prompt", (1, 1, SEQ, HD, 2 * DQ)), ("v_prompt", (1, 1, SEQ, HD, DV)),
         ("C_prompt", (1, 1, HM, DV, DQ)), ("n_prompt", (1, 1, HM, DQ)), ("m_prompt", (1, 1, HM)),
         ("k_sample", (1, DB, DS, HD, 2 * DQ)), ("v_sample", (1, DB, DS, HD, DV)),
         ("C_sample", (1, DB, HM, DV, DQ)), ("n_sample", (1, DB, HM, DQ)), ("m_sample", (1, DB, HM))]


def kernel(**inputs):
    import numpy as np
    import concourse.bacc as bacc
    from concourse.bass_utils import run_bass_kernel_spmd

    nc = bacc.Bacc("TRN2", target_bir_lowering=False, num_devices=1)
    arrays, ins, outs = {}, {}, {}
    for name in _INS:
        a = np.ascontiguousarray(inputs[name])
        arrays[f"in_{name}"] = a
        ins[name] = nc.dram_tensor(f"in_{name}", a.shape, mybir.dt.from_np(a.dtype), kind="ExternalInput").ap()
    arrays["in_const"] = constants()
    ins["const"] = nc.dram_tensor("in_const", (P, CW), F32, kind="ExternalInput").ap()
    for name, shape in _OUTS:
        outs[name] = nc.dram_tensor(f"out_{name}", shape, F32, kind="ExternalOutput").ap()
    build(nc, ins, outs)
    r = run_bass_kernel_spmd(nc, [arrays], core_ids=[0])
    return tuple(r.results[0][f"out_{name}"] for name, _ in _OUTS)
```

```python
from contextlib import ExitStack

import concourse.bass as bass
from concourse import mybir

P = 128
D = 1024
KT = D // P
SEQ, DB, DS, PAST = 512, 8, 16, 256
TOK = SEQ + DB * DS
NT = TOK // P
NTP = SEQ // P
HALF = TOK // 2
DFF = 2816
FT = DFF // P
NADA = 9
NB = 1 + DB
HM = HD = 4
DQ, DV = 64, 128
EPS = 1e-6
LAM_INIT = 0.8 - 0.6
SCALE = float(DQ) ** -0.5
BIG = -1.0e30

UNIT = 2048
ADA_COLS = UNIT // KT
ADA_UNITS = NADA * D // ADA_COLS
ADA_FIRST = 2 * D // ADA_COLS // 2
ADA_OUT = ADA_UNITS - 2 * ADA_FIRST - FT
OUT_TURNS = FT // 2
C_MK, C_MV, C_MO, C_G, C_DQ, C_DK, C_DV = 256, 512, 1024, 1536, 1544, 2056, 2568
GROUPS = [("mq", 0, 256 + 2 * HM), ("mk", C_MK, 256), ("mv", C_MV, 512), ("mo", C_MO, 512),
          ("dq", C_DQ, 512), ("dk", C_DK, 512), ("dv", C_DV, 512), ("o0", 0, 512), ("o1", 512, 512)]

_c = 0
def _col(n):
    global _c
    _c += n
    return _c - n
CI, CMP, CMS, CBM = _col(P), _col(P), _col(P), _col(DB)
CSEL, CS18, CROPE = _col(P), _col(NB), _col(NT * 24)
CHEAD, CPAIR, CONE, CDELTA, CSIGN = _col(HM * P), _col(2 * P), _col(P), _col(HM * DB), _col(2)
CW = _c


def constants():
    import numpy as np
    c = np.zeros((P, CW), np.float32)
    i = np.arange(P)
    c[:, CI:CI + P] = np.eye(P)
    causal = i[:, None] <= i[None, :]
    c[:, CMP:CMP + P] = np.where(causal, 0, BIG)
    same = i[:, None] // DS == i[None, :] // DS
    c[:, CMS:CMS + P] = np.where(causal & same, 0, BIG)
    c[:, CBM:CBM + DB] = i[:, None] // DS == np.arange(DB)
    row_head, row_q = i // 32, i % DS
    c[:, CSEL:CSEL + P] = (row_head[:, None] == i // 32) & (row_q[:, None] == i % 32)
    for r in range(NB):
        c[r, CS18 + r] = c[NB + r, CS18 + r] = 1
    f = np.float32
    inv = f(500000.0) ** (-np.arange(8, dtype=f) * f(2.0 / 16))
    pos = np.concatenate([np.arange(SEQ), np.tile(PAST + np.arange(DS), DB)]).astype(f)
    ang = pos[:, None] * inv[None, :]
    rope = np.concatenate([np.cos(ang), -np.sin(ang), np.sin(ang)], axis=1)
    c[:, CROPE:CROPE + NT * 24] = rope.reshape(NT, P, 24).transpose(1, 0, 2).reshape(P, NT * 24)
    for h in range(HM):
        c[h, CHEAD + h * P:CHEAD + (h + 1) * P] = -1
        c[h, CDELTA + h * DB:CDELTA + (h + 1) * DB] = 1
        c[h, CPAIR + (h // 2) * P + 64 * (h % 2):CPAIR + (h // 2) * P + 64 * (h % 2) + 64] = 1
    c[:, CONE:CONE + P] = 1
    c[:, CSIGN] = i // DS % 2 == 0
    c[:, CSIGN + 1] = i // DS % 2 == 1
    return c


def chain(eng, done):
    count = [0]

    def link(ins):
        count[0] += 1
        ins.then_inc(done, 1)
        eng.wait_ge(done, count[0])
        return ins
    return link


def from_zero(eng, turns, body):
    body(0)
    with eng.Fori(1, turns) as t:
        body(t)


ALU = mybir.AluOpType
ACT = mybir.ActivationFunctionType
AXX = mybir.AxisListType.X
F32 = mybir.dt.float32
F32R = mybir.dt.float32r
KB = 1024


def build(nc, i, o):
    with ExitStack() as ctx:
        base = (nc.sbuf_base + 31) // 32 * 32

        def at(name, off, shape, dt=F32):
            return nc.alloc_sbuf_tensor_at(name, shape, dt, offset=base + off)

        def sem(name):
            return ctx.enter_context(nc.semaphore(name))

        X = at("resid", 0, [P, NT, D])
        HTH = at("h_t_hi", 20 * KB, [P, KT, TOK], F32R)
        HTL = at("h_t_lo", 40 * KB, [P, KT, TOK], F32R)
        RAW = at("w_raw", 60 * KB, [P, 2, UNIT])
        START_SLOTS = 7
        RAW_START = at("w_raw_start", 20 * KB, [P, START_SLOTS, UNIT])
        MORE_HI = [at(f"w_hi{s}", (92 + 8 * s) * KB, [P, UNIT], F32R) for s in (2, 3)]
        MORE_LO = [at("w_lo2", 124 * KB, [P, UNIT], F32R), at("w_lo3", 170 * KB, [P, UNIT], F32R)]
        WH = at("w_hi", 76 * KB, [P, 2, UNIT], F32R)
        WL = at("w_lo", 92 * KB, [P, 2, UNIT], F32R)
        FIX = 193 * KB
        CON = at("const", FIX, [P, CW])
        off = FIX + CW * 4
        def fixed(name, shape, dt=F32):
            nonlocal off
            n = 4
            for s in shape[1:]:
                n *= s
            off += -off % 32
            t = at(name, off, shape, dt)
            off += n
            return t
        MODT = fixed("mod_t", [P, NADA * KT, NB])
        BT = fixed("b_ada_t", [P, NADA * KT])
        GT = fixed("g_norm_t", [P, 6 * KT])
        CT = fixed("c_t", [P, KT, 2 * NB], F32R)
        SCA = fixed("scale_t", [P, KT, NB])
        GATE = fixed("gate_t", [P, KT, NB])
        off += -off % 32
        AROW0 = off
        AROW = fixed("mod_rows", [2 * NB, 2, ADA_COLS])
        SS = fixed("sum_squares", [P, 3, NT])
        RS = fixed("rstd", [P, 2, NT])
        NNAT = fixed("state_n", [DB, HM, DQ])
        LAM = fixed("lambda", [P, 4, DQ])
        LS = fixed("lambda_s", [P, 16])
        WARM = fixed("root_of_one", [P, 1])
        ASTH = at("act_hi", 108 * KB, [P, 2, TOK], F32R)
        ASTL = at("act_lo", 113 * KB, [P, 2, TOK], F32R)
        SIL = at("silu_gate", 118 * KB, [P, TOK])
        Y = at("y", 118 * KB, [P, NT, D])
        ACTT = at("act_t", 138 * KB, [P, FT, TOK])
        XN = at("x_norm", 138 * KB, [P, NT, D])
        V = at("modulated", 158 * KB, [P, 4, TOK])
        CALL = at("c_all", 138 * KB, [NB, D])
        CSI = at("c_silu", 142 * KB, [NB, D])
        BG = at("b_g_rows", 146 * KB, [P, 2, P])
        GSP = at("gate_bc_prompt", 28 * KB, [P, KT, P])
        GSS = at("gate_bc_sample", 32 * KB, [P, KT, P])
        GB = at("gate_rows", 20 * KB, [P, 2, D])
        GATE_BUF = [(GSP, GSS, GB),
                    (at("gate_bc_prompt1", 164 * KB, [P, KT, P]), at("gate_bc_sample1", 168 * KB, [P, KT, P]),
                     at("gate_rows1", 172 * KB, [P, 2, D])),
                    (GSP, GSS, GB)]
        M0 = 108 * KB
        MQG = at("mq_gates", M0, [P, NT, 264]); M0 += 264 * NT * 4
        MK = at("mk", M0, [P, NT, 256]); M0 += 5 * KB
        MQT = at("mq_t", M0, [P, 2, TOK]); M0 += 5 * KB
        MKT = at("mk_t", M0, [P, 2, TOK]); M0 += 5 * KB
        QST = at("mq_scaled_t", M0, [P, 2, SEQ]); M0 += 4 * KB
        MVX = at("mv_ones", M0, [P, NT, HM, DV + 1]); M0 += NT * HM * (DV + 1) * 4 + 16
        OG = at("o_gate", M0, [P, NT, 512]); M0 += 10 * KB
        DV0 = M0
        DVT = at("dv", M0, [P, NT, 512]); M0 += 10 * KB
        DQT = at("dq_t", M0, [P, HD, TOK]); M0 += 10 * KB
        DKT = at("dk_t", M0, [P, HD, TOK]); M0 += 10 * KB
        DQK = at("rope_in", M0, [P, 2, 512])
        R1 = at("rope_cos", M0 + 4 * KB, [P, 2, 2 * HD, 2, 8])
        R2 = at("rope_sin", M0 + 5 * KB, [P, 2, 2 * HD, 2, 8])
        HHM = at("mlstm_heads", M0, [P, NT, 512]); M0 += 10 * KB
        assert M0 <= FIX
        HDF = at("diff_heads", 108 * KB + 264 * NT * 4 + 19 * KB, [P, NT, 512])
        N0 = 32 * KB + 512
        ARG = [at("w_arg0", N0, [P, HM, P]), at("w_arg1", 24 * KB, [P, HM, P])]; N0 += 2 * KB
        KBM = [at("k_by_batch0", N0 - 2 * KB, [P, DB, DQ]), at("k_by_batch1", 22 * KB, [P, DB, DQ])]
        ST = at("s_t", N0, [P, HM, P]); N0 += 2 * KB
        KW = at("k_weighted", N0, [P, HM, DQ]); N0 += KB
        CTX = at("state_t", N0, [P, 2, DV + 1]); N0 += 1056
        SC = at("state_c", N0, [P, HM, DB, DQ]); N0 += 8 * KB
        SCT = at("state_ct", N0, [P, DB // 2, HM, DV + 1]); N0 += 8256
        QB = at("q_by_batch", N0, [P, DB, DQ]); N0 += 2 * KB
        NROW = at("state_n_rows", N0 - 2 * KB, [32, P])
        QBT = [at("q_by_batch_t0", N0, [P, DB // 2, P]), at("q_by_batch_t1", 20 * KB, [P, DB // 2, P])]; N0 += 2 * KB
        assert N0 <= 60 * KB, N0
        ROWA, ROWB, ROWI, ROWR = (at(n, DV0 + 2560 * k, [HM, TOK]) for k, n in enumerate(("row_a", "row_b", "row_inter", "row_rows")))
        ROWM = at("row_m", M0 - 2560, [HM, TOK])
        S0 = AROW0
        COLA = at("col_a", S0, [P, NT, HM]); S0 += 96
        COLE = at("col_exp", S0, [P, 3, NT, HM]); S0 += 256
        WSR = at("seg_rows", S0, [HM, 96]); S0 += 384
        WSB = at("seg_bc", S0, [P, 40]); S0 += 160
        WS8 = at("seg_by_batch", S0, [DB, HM]); S0 += 32
        DEN = at("denominators", S0, [P, NT, HM]); S0 += 96
        WB = at("rows_by_batch", S0, [P, HM, DB]); S0 += 128
        A0 = 20 * KB
        PR = at("probs", A0, [P, 2, 2, 512]); A0 += 8 * KB
        PTT = at("probs_t", A0, [P, 2, 512]); A0 += 4 * KB
        C3 = 108 * KB + 264 * NT * 4 + 10 * KB
        KC = [at("k_cache0", A0, [P, 2, 512]), at("k_cache1", A0 + 4 * KB, [P, 2, 512]), at("k_cache2", C3, [P, 2, 512])]; A0 += 8 * KB
        VC = [at("v_cache0", A0, [P, 2, 512]), at("v_cache1", A0 + 4 * KB, [P, 2, 512]), at("v_cache2", C3 + 4 * KB, [P, 2, 512])]; A0 += 8 * KB
        KCT = [at("k_cache_t0", A0, [P, HD, PAST]), at("k_cache_t1", 20 * KB, [P, HD, PAST])]; A0 += 4 * KB
        QBD = at("q_blocks", A0, [P, DB, HD, 32]); A0 += 4 * KB
        VN = [at("v_new0", A0, [DS, 512]), at("v_new1", A0 + 2 * KB, [DS, 512]), at("v_new2", 28 * KB, [DS, 512])]; A0 += 4 * KB
        assert A0 <= 60 * KB
        B0 = 108 * KB
        GH = at("g_heads", B0, [P, D]); B0 += 4 * KB
        OB = [at("out_b0", B0, [DS, 512]), at("out_b1", 30 * KB, [DS, 512])]; B0 += 2 * KB
        PS_ = at("probs_s", B0, [P, 2, PAST + DS]); B0 += 2 * KB + 192
        B0 = 108 * KB + 264 * NT * 4 + 5 * KB
        PTS = at("probs_s_t", B0, [P, 3, P]); B0 += 1536
        MX = at("max_den", B0, [P, 32]); B0 += 128
        MR = at("combine", B0, [P, P]); B0 += 512
        HR = at("head_rstd", B0, [P, 2, NT, HM]); B0 += 160
        SQD = at("squares", B0, [P, HM, DV])
        assert B0 + 2 * KB <= C3

        PS = ctx.enter_context(nc.psum_tensor("ps", [P, 8, 512], F32))
        ident = CON[:, CI:CI + P]

        small_landed = sem("small_landed")
        x_landed = sem("x_landed")
        c_silu = sem("c_silu")
        c_tr = sem("c_tr")
        c_ready = sem("c_ready")
        a_landed = [sem(f"a_landed{s}") for s in range(2)]
        a_hi = [sem(f"a_hi{s}") for s in range(2)]
        a_lo = [sem(f"a_lo{s}") for s in range(2)]
        a_mm = [sem(f"a_mm{s}") for s in range(2)]
        a_row = [sem(f"a_row{s}") for s in range(2)]
        a_tr = [sem(f"a_tr{s}") for s in range(2)]
        a_mod = [sem(f"a_mod{s}") for s in range(2)]
        f_landed = [sem(f"f_landed{s}") for s in range(2)]
        f_hi = [sem(f"f_hi{s}") for s in range(2)]
        f_lo = [sem(f"f_lo{s}") for s in range(2)]
        f_mm = [sem(f"f_mm{s}") for s in range(2)]
        f_silu = sem("f_silu")
        f_act = sem("f_act")
        k_landed = [sem(f"k_landed{s}") for s in range(2)]
        k_hi = [sem(f"k_hi{s}") for s in range(2)]
        k_lo = [sem(f"k_lo{s}") for s in range(2)]
        k_mm = [sem(f"k_mm{s}") for s in range(2)]
        out_done = sem("out_done")
        y_copied = sem("y_copied")
        gate_t = sem("gate_t")
        gate_bc = sem("gate_bc")
        gate_mm = sem("gate_mm")
        gate_rows = sem("gate_rows")
        y_sq = sem("y_sq")
        y_ms = sem("y_ms")
        y_rstd = sem("y_rstd")
        x_new = sem("x_new")
        x_sq = sem("x_sq")
        x_ms = sem("x_ms")
        x_rstd = sem("x_rstd")
        x_norm = sem("x_norm")
        x_tr = sem("x_tr")
        sca_ready = sem("sca_ready")
        v_p = sem("v_p")
        v_s = sem("v_s")
        h_hi = sem("h_hi")
        h_lo = sem("h_lo")
        g_landed = [sem(f"g_landed{s}") for s in range(2)]
        g_hi = [sem(f"g_hi{s}") for s in range(2)]
        g_lo = [sem(f"g_lo{s}") for s in range(2)]
        g_half = sem("g_half")
        g_free = sem("g_free")
        k_sent = [sem(f"k_sent{s}") for s in range(2)]
        g_bank = sem("g_bank")
        rope_done = sem("rope_done")
        rope_tr = sem("rope_tr")
        rope_t = sem("rope_t")
        kv_out = sem("kv_out")
        dvec = sem("dve_chain")
        actc = sem("act_chain")
        q_tr = sem("q_tr")
        q_t = sem("q_t")
        gates_tr = sem("gates_tr")
        gates_row = sem("gates_row")
        ln_f = sem("ln_f")
        mst_landed = sem("mst_landed")
        gb_landed = sem("gb_landed")
        rows_ready = sem("rows_ready")
        cols_tr = sem("cols_tr")
        cols_exp = sem("cols_exp")
        seg_exp = sem("seg_exp")
        seg_d = sem("seg_d")
        seg_mm = sem("seg_mm")
        seg_bc = sem("seg_bc")
        qs_ready = sem("qs_ready")
        qs_tr = sem("qs_tr")
        qs_t = sem("qs_t")
        st_tr = sem("st_tr")
        st_t = sem("st_t")
        m_even = sem("m_even")
        m_scores = sem("m_scores")
        m_arg = sem("m_arg")
        m_exp = sem("m_exp")
        m_s = sem("m_s")
        m_kw = sem("m_kw")
        m_cu = sem("m_cu")
        m_state = sem("m_state")
        m_hn = sem("m_hn")
        m_head = sem("m_head")
        qb_ready = sem("qb_ready")
        qb_tr = sem("qb_tr")
        qb_t = sem("qb_t")
        kb_ready = sem("kb_ready")
        cu_s = sem("cu_s")
        c_new = sem("c_new")
        n_mm = sem("n_mm")
        fin_tr = sem("fin_tr")
        fin_c = sem("fin_c")
        st_out = sem("st_out")
        g_lam_landed = sem("g_lam_landed")
        lam_e = sem("lam_e")
        p_scores = sem("p_scores")
        p_max = sem("p_max")
        p_exp = sem("p_exp")
        p_comb = sem("p_comb")
        p_tr = sem("p_tr")
        p_t = sem("p_t")
        p_o = sem("p_o")
        p_copied = sem("p_copied")
        kc_landed = [sem(f"kc_landed{s}") for s in range(3)]
        vc_landed = [sem(f"vc_landed{s}") for s in range(3)]
        poold = sem("pool_chain")
        hd_sq = sem("hd_sq")
        heads_s = sem("heads_s")
        qbd_ready = sem("qbd_ready")
        s_ktr = sem("s_ktr")
        s_scores = sem("s_scores")
        s_max = sem("s_max")
        s_exp = sem("s_exp")
        s_mr = sem("s_mr")
        s_ptr = sem("s_ptr")
        s_pt = sem("s_pt")
        s_o = sem("s_o")
        s_ob = sem("s_ob")
        ob_moved = [sem(f"ob_moved{s}") for s in range(2)]
        hd_ms = sem("hd_ms")
        hd_rstd = sem("hd_rstd")
        heads = sem("heads")
        hh_tr = sem("hh_tr")
        seg_arg = sem("seg_arg")
        st_n = sem("st_n")
        qb_mm = sem("qb_mm")
        lam_s = sem("lam_s")
        s_kta = sem("s_kta")
        s_ktd = sem("s_ktd")
        hh_hi = sem("hh_hi")
        hh_lo = sem("hh_lo")
        y_out = sem("y_out")

        w_ada = i["w_ada"].rearrange("l (k p) n -> p (l k) n", p=P)
        ffn_in = [i[n].rearrange("l (k p) n -> p (l k) n", p=P) for n in ("w_ffn1_in", "w_ffn2_in")]
        ffn_out = [i[n].rearrange("l f n -> (l f) n") for n in ("w_ffn1_out", "w_ffn2_out")]
        w_in = i["w_in"].rearrange("l (k p) n -> p (l k) n", p=P)
        w_o = i["w_out"].rearrange("l (k p) n -> p (l k) n", p=P)
        x_p = i["x_prompt"].rearrange("b (t p) d -> p (b t) d", p=P)
        x_s = i["x_sample"].rearrange("b s d -> (b s) d")
        k_cache = i["cache_k"].rearrange("l b (k p) h d -> p (l b) k (h d)", p=P)
        v_cache = i["cache_v"].rearrange("l b (k p) h d -> p (l b) k (h d)", p=P)

        def ada_view(T, s):
            return T[:, s, :].rearrange("p (k n) -> p k n", k=KT)

        def ffn_view(T, s):
            return T[:, 0, s * 1024:(s + 1) * 1024].rearrange("p (k n) -> p k n", k=KT)

        def out_view(T, s):
            return T[:, 0, s * 1024:s * 1024 + 512]

        def grp_view(T, s, n):
            return T[:, s, 0:4 * n].rearrange("p (k n) -> p k n", k=4)

        def start_hi(unit):
            return WH[:, unit % 4, :] if unit % 4 < 2 else MORE_HI[unit % 4 - 2][:, :]

        def start_lo(unit):
            return WL[:, unit % 4, :] if unit % 4 < 2 else MORE_LO[unit % 4 - 2][:, :]

        block = ctx.enter_context(nc.Block())

        @block.sync
        def _(sp):
            sp.dma_start(CON[:, :], i["const"]).then_inc(small_landed, 16)
            sp.dma_start(CALL[0:1, :], i["c_prompt"]).then_inc(small_landed, 16)
            sp.dma_start(CALL[1:NB, :], i["c_sample"]).then_inc(small_landed, 16)
            sp.dma_start(BG[0:NADA * KT, 0, :], i["b_ada"].rearrange("l (r p) -> (l r) p", p=P)).then_inc(small_landed, 16)
            sp.dma_start(BG[0:6 * KT, 1, :], i["g_norm"].rearrange("l g (k p) -> (l g k) p", p=P)).then_inc(small_landed, 16)

            sp.dma_start(X[:, 0:NTP, :], x_p).then_inc(x_landed, 16)
            sp.dma_start(X[:, NTP, :], x_s).then_inc(x_landed, 16)

            def ada_load(s, unit, n):
                sp.wait_ge(a_hi[s], n)
                sp.wait_ge(a_lo[s], n)
                sp.dma_start(ada_view(RAW, s), w_ada[:, :, bass.ds(unit * ADA_COLS, ADA_COLS)]).then_inc(a_landed[s], 16)

            for unit in range(2 * ADA_FIRST):
                s, n = unit % 2, unit // 2
                if n:
                    sp.wait_ge(a_landed[s], 16 * n)
                if unit >= START_SLOTS:
                    sp.wait_ge(a_hi[(unit - START_SLOTS) % 2], (unit - START_SLOTS) // 2 + 1)
                    sp.wait_ge(a_lo[(unit - START_SLOTS) % 2], (unit - START_SLOTS) // 2 + 1)
                sp.dma_start(ada_view(RAW_START, unit % START_SLOTS), w_ada[:, :, unit * ADA_COLS:(unit + 1) * ADA_COLS]).then_inc(a_landed[s], 16)


            def ffn_in_loads(f, m, n):
                for s in range(2):
                    sp.wait_ge(f_hi[s], n)
                    sp.wait_ge(f_lo[s], n)
                    sp.dma_start(ffn_view(RAW, s), ffn_in[f][:, :, bass.ds(m * P + s * DFF, P)]).then_inc(f_landed[s], 16)

            def ffn_out_loads(f):
                for half in range(2):
                    def turn(t, ada=False):
                        for s in range(2):
                            n = (2 * f + half) * OUT_TURNS + t
                            sp.wait_ge(k_hi[s], 2 * n)
                            sp.wait_ge(k_lo[s], 2 * n)
                            sp.dma_start(out_view(RAW, s), ffn_out[f][bass.ds((2 * t + s) * P, P), half * 512:(half + 1) * 512]).then_inc(k_landed[s], 16)
                            if ada and s == 0:
                                ada_load(1, 2 * ADA_FIRST + FT + t, ADA_FIRST + FT + t)

                    if f == 0 and half == 0:
                        from_zero(sp, ADA_OUT, lambda t: turn(t, True))
                        with sp.Fori(ADA_OUT, OUT_TURNS) as t:
                            turn(t)
                    else:
                        from_zero(sp, OUT_TURNS, turn)

            sp.wait_ge(a_hi[0], ADA_FIRST)
            sp.wait_ge(a_lo[0], ADA_FIRST)
            def turn(m):
                ffn_in_loads(0, m, m)
                ada_load(1, 2 * ADA_FIRST + m, ADA_FIRST + m)
            from_zero(sp, FT, turn)

            for s in range(2):
                sp.wait_ge(f_hi[s], FT)
                sp.wait_ge(f_lo[s], FT)
            ffn_out_loads(0)
            def mixer_loads():
                sp.wait_ge(g_bank, 7 * NT)
                for h in range(HM):
                    sp.dma_start(SC[:, h, :, :], i["state_C"].rearrange("l b h v d -> h v (l b) d")[h]).then_inc(mst_landed, 16)
                nsrc = i["state_n"].rearrange("l b h d -> (l b h) d")
                sp.dma_start(NROW[:, 0:DQ], nsrc).then_inc(mst_landed, 16)
                sp.dma_start(NROW[:, DQ:P], nsrc).then_inc(mst_landed, 16)
                sp.dma_start(NNAT[:, :, :].rearrange("b h d -> b (h d)"), i["state_n"].rearrange("l b h d -> (l b) (h d)")).then_inc(mst_landed, 16)
                sp.wait_ge(n_mm, 1)
                sp.dma_start(GH[:, 0:512], i["g_mlstm"].rearrange("l h v -> l (h v)").to_broadcast([P, 512])).then_inc(g_lam_landed, 16)
                sp.dma_start(GH[:, 512:1024], i["g_diff"].rearrange("l h v -> l (h v)").to_broadcast([P, 512])).then_inc(g_lam_landed, 16)

            sp.dma_start(LAM[:, :, :].rearrange("p a d -> p (a d)"), i["lambda_qk"].rearrange("l a d -> l (a d)").to_broadcast([P, 4 * DQ])).then_inc(g_lam_landed, 16)
            sp.wait_ge(a_mod[1], ADA_FIRST + FT + ADA_OUT)
            with nc.allow_non_contiguous_dma(reason="a few numbers"):
                sp.dma_start(WSR[:, 0:DB], i["state_m"].rearrange("l b h -> (l h) b")).then_inc(gb_landed, 16)
                sp.dma_start(WSR[:, 8:9], i["b_igate"].rearrange("l h -> h l")).then_inc(gb_landed, 16)
                sp.dma_start(WSR[:, 9:10], i["b_fgate"].rearrange("l h -> h l")).then_inc(gb_landed, 16)
            sp.wait_ge(a_hi[1], ADA_FIRST + FT + ADA_OUT)
            sp.wait_ge(a_lo[1], ADA_FIRST + FT + ADA_OUT)
            for s in range(2):
                sp.wait_ge(k_hi[s], 4 * OUT_TURNS)
                sp.wait_ge(k_lo[s], 4 * OUT_TURNS)
            for g, (name, c0, n) in enumerate(GROUPS):
                if g == 8:
                    mixer_loads()
                w = w_in if g < 7 else w_o
                for s in range(2):
                    sp.wait_ge(g_hi[s], g)
                    sp.wait_ge(g_lo[s], g)
                    v = grp_view(RAW, s, n)
                    if g == 0:
                        sp.dma_start(v[:, :, 0:256], w[:, 4 * s:4 * s + 4, 0:256]).then_inc(g_landed[s], 16)
                        with nc.allow_non_contiguous_dma(reason="the gates' few columns"):
                            sp.dma_start(v[:, :, 256:264], w[:, 4 * s:4 * s + 4, C_G:C_G + 8]).then_inc(g_landed[s], 16)
                    else:
                        sp.dma_start(v, w[:, 4 * s:4 * s + 4, c0:c0 + n]).then_inc(g_landed[s], 16)
            sp.wait_ge(st_out, 16 * 11)
            def keys_load(b):
                sp.dma_start(KC[b % 3][:, :, :], k_cache[:, b, :, :]).then_inc(kc_landed[b % 3], 16)

            def values_load(b):
                sp.dma_start(VC[b % 3][:, :, :], v_cache[:, b, :, :]).then_inc(vc_landed[b % 3], 16)
                sp.dma_start(VN[b % 3][:, :], DVT[b * DS:(b + 1) * DS, NTP, :]).then_inc(vc_landed[b % 3], 16)

            for b in range(3):
                if b == 2:
                    sp.wait_ge(p_tr, NTP * HD)
                    sp.wait_ge(p_o, NTP * HD)
                keys_load(b)
                values_load(b)
            for b in range(3, DB + 4):
                if b < DB:
                    sp.wait_ge(s_ktr, 2 * (b - 2))
                    keys_load(b)
                if 3 < b <= DB:
                    sp.wait_ge(s_o, b - 3)
                    values_load(b - 1)
                if b > 3:
                    n = b - 4
                    sp.wait_ge(s_ob, n + 1)
                    sp.dma_start(HDF[n * DS:(n + 1) * DS, NTP, :], OB[n % 2][:, :]).then_inc(ob_moved[n % 2], 16)
            for s in range(2):
                sp.wait_ge(g_hi[s], len(GROUPS))
                sp.wait_ge(g_lo[s], len(GROUPS))
            with sp.Fori(0, FT) as m:
                ffn_in_loads(1, m, FT + m)
            for s in range(2):
                sp.wait_ge(f_hi[s], 2 * FT)
                sp.wait_ge(f_lo[s], 2 * FT)
            ffn_out_loads(1)
            for t in range(NT):
                sp.wait_ge(x_new, 2 * NT + t + 1)
                dst = o["y_prompt"].rearrange("b (t p) d -> (b t) p d", p=P)[t] if t < NTP else o["y_sample"].rearrange("b s d -> (b s) d")
                sp.dma_start(dst, X[:, t, :]).then_inc(y_out, 16)
            sp.wait_ge(y_out, 16 * NT)

        @block.scalar
        def _(act):
            link = chain(act, actc)
            act.wait_ge(small_landed, 16 * 5)
            act.activation(CSI[:, :], CALL[:, :], ACT.Silu).then_inc(c_silu, 1)
            act.wait_ge(c_tr, 1)
            act.activation(CT[:, :, 0:NB], PS[:, 7, 0:KT * NB].rearrange("p (k b) -> p k b", k=KT), ACT.Copy).then_inc(c_silu, 1)

            def norm_rows(p):
                for t in range(NT):
                    if p == 0:
                        act.wait_ge(x_landed, 32)
                    else:
                        act.wait_ge(x_new, (p - 1) * NT + t + 1)
                    act.activation(XN[:, t, :], X[:, t, :], ACT.Square, accum_out=SS[:, 0, t:t + 1]).then_inc(x_sq, 1)
                act.wait_ge(x_ms, p + 1)
                act.activation(RS[:, 0, :], SS[:, 0, :], ACT.Sqrt).then_inc(x_rstd, 1)
                act.wait_ge(x_rstd, p + 1)
                for t in range(NT - 2, NT):
                    act.activation(XN[:, t, :], X[:, t, :], ACT.Copy, scale=RS[:, 0, t:t + 1]).then_inc(x_norm, 1)

            act.wait_ge(c_tr, 2)
            norm_rows(0)

            def ada_hi_start(unit):
                s, n = unit % 2, unit // 2
                act.wait_ge(a_landed[s], 16 * (n + 1))
                if unit >= 4:
                    act.wait_ge(a_mm[s], n - 1)
                act.activation(start_hi(unit), RAW_START[:, unit % START_SLOTS, :], ACT.Copy).then_inc(a_hi[s], 1)

            def ada_hi(s, n):
                act.wait_ge(a_landed[s], 16 * (n + 1))
                act.wait_ge(a_mm[s], n)
                act.activation(WH[:, s, :], RAW[:, s, :], ACT.Copy).then_inc(a_hi[s], 1)

            def ada_row(s, n):
                act.wait_ge(a_mm[s], n + 1)
                act.wait_ge(a_tr[s], n)
                act.activation(AROW[:, s, :], PS[0:2 * NB, 4 + s, 0:ADA_COLS], ACT.Copy).then_inc(a_row[s], 1)

            for unit in range(2 * ADA_FIRST + 2):
                if unit < 2 * ADA_FIRST:
                    ada_hi_start(unit)
                if unit >= 2:
                    ada_row(unit % 2, unit // 2 - 1)

            def norm(p, between=None):
                act.wait_ge(sca_ready, p + 1)

                def hi(k):
                    act.wait_ge(v_s, KT * p + k + 1)
                    act.wait_ge(v_p, KT * p + k + 1)
                    act.activation(HTH[:, k, :], V[:, k % 4, :], ACT.Copy).then_inc(h_hi, 1)

                shift = MODT[:, 3 * p * KT:(3 * p + 1) * KT, 0:1]
                for k in range(KT):
                    act.wait_ge(x_tr, KT * p + k + 1)
                    if k >= 4:
                        act.wait_ge(h_lo, KT * p + k - 3)
                    act.activation(V[:, k % 4, 0:SEQ], PS[:, 4 + k % 2, :], ACT.Identity, bias=shift[:, k, :],
                                   scale=SCA[:, k, 0:1]).then_inc(v_p, 1)
                    if between:
                        between(k)
                    if k >= 1:
                        hi(k - 1)
                hi(KT - 1)

            def ffn_hi(s, n):
                act.wait_ge(f_landed[s], 16 * (n + 1))
                act.wait_ge(f_mm[s], n)
                act.activation(WH[:, 0, s * 1024:(s + 1) * 1024], RAW[:, 0, s * 1024:(s + 1) * 1024], ACT.Copy).then_inc(f_hi[s], 1)

            def ffn_silu(n):
                act.wait_ge(f_mm[0], n + 1)
                act.wait_ge(f_act, n)
                act.activation(SIL[:, :].rearrange("p (a n) -> p a n", a=2), PS[:, 0:2, 0:HALF], ACT.Silu).then_inc(f_silu, 1)

            def out_hi(s, t, n):
                act.wait_ge(k_landed[s], 16 * (n + 1))
                act.wait_ge(k_mm[s], n)
                act.activation(WH[:, 0, s * 1024:s * 1024 + 512], RAW[:, 0, s * 1024:s * 1024 + 512], ACT.Copy).then_inc(k_hi[s], 1)
                act.activation(ASTH[:, s, :], ACTT[:, bass.ds(2 * t + s, 1), :].rearrange("p a n -> p (a n)"), ACT.Copy).then_inc(k_hi[s], 1)

            def roots_table():
                act.activation(WARM[:, :], CON[:, CONE:CONE + 1], ACT.Sqrt)

            def gate_evac(r, js):
                for j in js:
                    act.wait_ge(gate_mm, 4 * r + j + 1)
                    act.activation(GATE_BUF[r][2][:, j // 2, 512 * (j % 2):512 * (j % 2) + 512], PS[:, 5 + j % 3, :], ACT.Copy).then_inc(gate_rows, 1)

            def y_squares(r, half, done):
                for t in range(NT):
                    act.wait_ge(*done(t))
                    act.activation(Y[:, t, half * 512:(half + 1) * 512], PS[:, t, :], ACT.Square, accum_out=SS[:, 1 + half, t:t + 1]).then_inc(y_sq, 1)

            def out_bank(f, half):
                n = 2 * f + half
                return lambda t: (out_done, (NT - 1) * n + t + 1) if t < NT - 1 else (k_mm[1], OUT_TURNS * (n + 1))

            def ffn_out(f):
                n0 = 2 * f * OUT_TURNS
                def turn(t, ada=False):
                    out_hi(0, t, n0 + t)
                    if ada:
                        ada_hi(1, ADA_FIRST + FT + t)
                    if isinstance(t, int) and t == 0:
                        act.wait_ge(f_mm[1], (f + 1) * FT)
                    out_hi(1, t, n0 + t)
                    if ada:
                        ada_row(1, ADA_FIRST + FT + t)
                from_zero(act, ADA_OUT, lambda t: turn(t, f == 0))
                turn(ADA_OUT)
                turn(ADA_OUT + 1)
                gate_evac(2 * f, range(3))
                turn(ADA_OUT + 2)
                gate_evac(2 * f, [3])
                with act.Fori(ADA_OUT + 3, OUT_TURNS) as t:
                    turn(t)

                n0 += OUT_TURNS
                out_hi(0, 0, n0)
                y_squares(2 * f, 0, out_bank(f, 0))
                out_hi(1, 0, n0)
                with act.Fori(1, OUT_TURNS) as t:
                    for s in range(2):
                        out_hi(s, t, n0 + t)
                roots_table()
                y_squares(2 * f, 1, out_bank(f, 1))

            def residual(r):
                act.wait_ge(y_ms, r + 1)
                act.activation(RS[:, 1, :], SS[:, 1, :], ACT.Sqrt).then_inc(y_rstd, 1)

            for s in range(2):
                act.wait_ge(a_mm[s], ADA_FIRST)
            norm(0, lambda k: ffn_hi(k, 0) if k < 2 else None)
            def turn(m):
                if not isinstance(m, int):
                    for s in range(2):
                        ffn_hi(s, m)
                ada_hi(1, ADA_FIRST + m)
                ffn_silu(m)
                ada_row(1, ADA_FIRST + m)
            from_zero(act, FT, turn)

            ffn_out(0)
            residual(0)
            norm_rows(1)

            def grp_hi(g, s):
                n = 4 * GROUPS[g][2]
                act.wait_ge(g_landed[s], 16 * (g + 2))
                act.activation(WH[:, s, 0:n], RAW[:, s, 0:n], ACT.Copy).then_inc(g_hi[s], 1)

            act.wait_ge(a_mm[1], ADA_FIRST + FT + ADA_OUT)
            for s in range(2):
                act.wait_ge(k_mm[s], 2 * OUT_TURNS)
            norm(1, lambda k: grp_hi(0, k) if k < 2 else None)

            def evac(g, t, out, cols, func=ACT.Copy, scale=1.0):
                act.wait_ge(g_bank, NT * g + t + 1)
                act.activation(out, cols, func, scale=scale).then_inc(g_free, 1)

            def log_forget():
                act.wait_ge(gates_row, 4)
                link(act.activation(ROWI[:, :], ROWB[:, :], ACT.Abs))
                link(act.activation(ROWI[:, :], ROWI[:, :], ACT.Exp, scale=-1.0))
                act.activation(ROWR[:, :], ROWI[:, :], ACT.Ln, bias=1.0).then_inc(ln_f, 1)

            def gate_columns():
                act.wait_ge(lam_s, 1)
                act.activation(LS[:, 2:4], LS[:, 0:2], ACT.Exp).then_inc(lam_e, 1)
                act.wait_ge(seg_arg, 1)
                act.activation(WSR[:, 36:48], WSR[:, 24:36], ACT.Exp).then_inc(seg_exp, 1)
                act.wait_ge(cols_tr, 1)
                act.activation(COLA[:, :, :], PS[:, 7, 0:NT * HM].rearrange("p (t h) -> p t h", t=NT), ACT.Copy).then_inc(cols_exp, 1)
                act.activation(COLE[:, :, :, :].rearrange("p a t h -> p (a t h)"), PS[:, 7, NT * HM:4 * NT * HM], ACT.Exp).then_inc(cols_exp, 1)

            for g in range(7):
                if g < 6:
                    n = 4 * GROUPS[g + 1][2]
                    act.wait_ge(g_landed[0], 16 * (g + 3))
                    act.wait_ge(g_half, g + 1)
                    act.activation(WH[:, 0, 0:n], RAW[:, 0, 0:n], ACT.Copy).then_inc(g_hi[0], 1)
                if g == 4:
                    gate_columns()
                for t in range(NT):
                    ps = PS[:, t, :]
                    if g == 0:
                        evac(g, t, MQG[:, t, :], ps[:, 0:264])
                    elif g == 1:
                        evac(g, t, MK[:, t, :], ps[:, 0:256], scale=DQ ** -0.5)
                    elif g == 2:
                        evac(g, t, MVX[:, t, :, 0:DV], ps.rearrange("p (h v) -> p h v", h=HM))
                    elif g == 3:
                        evac(g, t, OG[:, t, :], ps, ACT.Sigmoid)
                    elif g in (4, 5):
                        r = NT * (g - 4) + t
                        if r >= 2:
                            act.wait_ge(rope_tr, r - 1)
                            if r - 2 >= NT:
                                act.wait_ge(k_sent[r % 2], 16 * ((r - 2 - NT) // 2 + 1))
                        evac(g, t, DQK[:, r % 2, :], ps)
                    else:
                        act.wait_ge(cols_tr, 1)
                        act.wait_ge(rows_ready, 1)
                        evac(g, t, DVT[:, t, :], ps)
                if g < 6:
                    act.wait_ge(g_landed[1], 16 * (g + 3))
                    act.wait_ge(g_bank, NT * (g + 1))
                    act.activation(WH[:, 1, 0:n], RAW[:, 1, 0:n], ACT.Copy).then_inc(g_hi[1], 1)
                if g == 1:
                    log_forget()
            for c in range(NT):
                act.wait_ge(m_arg, c + 1)
                act.activation(ARG[c % 2][:, :, :], ARG[c % 2][:, :, :], ACT.Exp).then_inc(m_exp, 1)
                for pr in {3: (0,), 4: (1, 2, 3)}.get(c, ()):
                    act.wait_ge(st_tr, pr + 1)
                    act.activation(SCT[:, pr, :, 0:DV], PS[:, 7, :].rearrange("p (h v) -> p h v", h=HM), ACT.Copy).then_inc(st_t, 1)
            for h in range(HM):
                act.wait_ge(qb_tr, h + 1)
                if h >= 2:
                    act.wait_ge(qb_mm, h - 1)
                act.activation(QBT[h % 2][:, :, :], PS[:, 6 + h % 2, :].rearrange("p (r t) -> p r t", r=DB // 2), ACT.Copy).then_inc(qb_t, 1)
            grp_hi(7, 0)
            grp_hi(7, 1)
            act.wait_ge(fin_tr, 1)
            act.activation(ST[:, 0:2, :], PS[:, 2, 0:2 * P].rearrange("p (j v) -> p j v", j=2), ACT.Copy).then_inc(fin_c, 1)


            def p_evac(n):
                nk = P * (n // HD + 1)
                act.wait_ge(p_tr, n + 1)
                if n >= 2:
                    act.wait_ge(p_o, n - 1)
                act.activation(PTT[:, n % 2, 0:nk], PS[:, 4 + n % 2, 0:nk], ACT.Copy).then_inc(p_t, 1)

            def o_evac(n):
                if n % HD == HD - 1:
                    act.wait_ge(p_o, n + 1)
                    act.activation(HDF[:, n // HD, :], PS[:, 6 + n // HD % 2, :], ACT.Copy).then_inc(p_copied, 1)

            def head_squares(a, t, T):
                if t or a:
                    act.wait_ge(hd_sq, NT * a + t)
                for h in range(HM):
                    q = act.activation(SQD[:, h, :], T[:, h * DV:(h + 1) * DV], ACT.Square, accum_out=HR[:, a, t, h:h + 1])
                q.then_inc(hd_sq, 1)

            for n in range(NTP * HD):
                nk = P * (n // HD + 1)
                act.wait_ge(p_max, n + 1)
                if n >= 2:
                    act.wait_ge(p_tr, n - 1)
                m = 8 * (n % 2)
                for c in range(2):
                    act.activation(PR[:, n % 2, c, 0:nk], PS[:, 2 * (n % 2) + c, 0:nk], ACT.Exp, bias=MX[:, m + 2 + c:m + 3 + c],
                                   scale=SCALE, accum_out=MX[:, m + 4 + c:m + 5 + c]).then_inc(p_exp, 1)
                if n:
                    p_evac(n - 1)
                if n > 1:
                    o_evac(n - 2)
                if n < NT:
                    act.wait_ge(m_head, 2 * NT)
                    head_squares(0, n, HHM[:, n, :])
            p_evac(NTP * HD - 1)
            o_evac(NTP * HD - 2)
            o_evac(NTP * HD - 1)
            act.wait_ge(p_copied, NTP)

            def keys_t(b):
                act.wait_ge(s_ktr, 2 * b + 1)
                if b >= 2:
                    act.wait_ge(s_scores, b - 1)
                act.activation(KCT[b % 2][:, :, 0:P], PS[:, 6 * (b % 2), :].rearrange("p (h t) -> p h t", h=HD), ACT.Copy).then_inc(s_kta, 1)

            def probs_t(b):
                act.wait_ge(s_ptr, b + 1)
                if b:
                    act.wait_ge(s_o, b)
                act.activation(PTS[:, 0:2, :], PS[:, 4, 0:2 * P].rearrange("p (k n) -> p k n", k=2), ACT.Copy).then_inc(s_pt, 1)
                act.activation(PTS[0:DS, 2, :], PS[0:DS, 4, 2 * P:3 * P], ACT.Copy).then_inc(s_pt, 1)

            def out_copy(b):
                act.wait_ge(s_o, b + 1)
                if b >= 2:
                    act.wait_ge(ob_moved[b % 2], 16 * (b // 2))
                for h in range(HD):
                    cols = slice(h * DV, (h + 1) * DV)
                    q = act.activation(OB[b % 2][:, cols], PS[32 * h:32 * h + DS, 5, cols], ACT.Copy)
                q.then_inc(s_ob, 1)

            keys_t(0)
            for b in range(DB):
                if b == NTP + 1:
                    act.wait_ge(hd_ms, 1)
                    act.activation(HR[:, 0, :, :], HR[:, 0, :, :], ACT.Sqrt).then_inc(hd_rstd, 1)
                    act.activation(HR[:, 1, 0:NTP, :], HR[:, 1, 0:NTP, :], ACT.Sqrt, scale=(1.0 - LAM_INIT) ** 2).then_inc(hd_rstd, 1)
                act.wait_ge(s_max, b + 1)
                if b >= 2:
                    act.wait_ge(s_ptr, b - 1)
                m = 16 + 4 * (b % 2)
                act.activation(PS_[:, b % 2, :], PS[:, 2 + b % 2, 0:PAST + DS], ACT.Exp, bias=MX[:, m + 1:m + 2], scale=SCALE,
                               accum_out=MX[:, m + 2:m + 3]).then_inc(s_exp, 1)
                if b + 1 < DB:
                    keys_t(b + 1)
                if b >= 2:
                    out_copy(b - 2)
                if b:
                    probs_t(b - 1)
                if b < NTP:
                    head_squares(1, b, HDF[:, b, :])
            out_copy(DB - 2)
            probs_t(DB - 1)
            out_copy(DB - 1)
            for k in range(KT):
                if k == 2:
                    for s in range(2):
                        act.wait_ge(ob_moved[s], 16 * (DB // 2))
                    head_squares(1, NTP, HDF[:, NTP, :])
                    act.wait_ge(hd_ms, 2)
                    act.activation(HR[:, 1, NTP, :], HR[:, 1, NTP, :], ACT.Sqrt, scale=(1.0 - LAM_INIT) ** 2).then_inc(hd_rstd, 1)
                act.wait_ge(hh_tr, k + 1)
                if k % 4 == 0:
                    act.activation(HTH[:, k:k + 4, SEQ:TOK], PS[:, 7, :].rearrange("p (j t) -> p j t", j=4), ACT.Copy)
                act.activation(HTH[:, k, 0:SEQ], PS[:, 5 + k % 2, :], ACT.Copy).then_inc(hh_hi, 1)
            act.wait_ge(g_half, 8)
            grp_hi(8, 0)
            gate_evac(1, range(4))
            y_squares(1, 0, lambda t: (g_bank, NT * 7 + t + 1))
            grp_hi(8, 1)
            roots_table()
            y_squares(1, 1, lambda t: (g_bank, NT * 8 + t + 1))
            residual(1)
            norm_rows(2)
            act.wait_ge(g_half, 9)
            norm(2, lambda k: ffn_hi(k, FT) if k < 2 else None)
            ffn_silu(FT)
            with act.Fori(FT + 1, 2 * FT) as n:
                for s in range(2):
                    ffn_hi(s, n)
                ffn_silu(n)
            ffn_out(1)
            residual(2)
        @block.tensor
        def _(pe):
            def mm(out, lhsT, rhs, start=True, stop=True):
                return pe.matmul(out, lhsT, rhs, start=start, stop=stop)

            pe.wait_ge(small_landed, 16 * 5)
            pe.wait_ge(c_silu, 1)
            for k in range(KT):
                q = pe.transpose(PS[:, 7, k * NB:(k + 1) * NB], CSI[:, k * P:(k + 1) * P], ident[0:NB, 0:NB])
            q.then_inc(c_tr, 1)
            pe.transpose(PS[:, 6, 0:NADA * KT], BG[0:NADA * KT, 0, :], ident[0:NADA * KT, 0:NADA * KT])
            pe.transpose(PS[:, 6, P:P + 6 * KT], BG[0:6 * KT, 1, :], ident[0:6 * KT, 0:6 * KT]).then_inc(c_tr, 1)
            pe.wait_ge(c_ready, 3)

            def ada_mm(s, n, unit=None):
                pe.wait_ge(a_hi[s], n + 1)
                pe.wait_ge(a_lo[s], n + 1)
                pe.wait_ge(a_row[s], n)
                if unit is None:
                    wh, wl = ada_view(WH, s), ada_view(WL, s)
                else:
                    wh, wl = (T.rearrange("p (k n) -> p k n", k=KT) for T in (start_hi(unit), start_lo(unit)))
                for k in range(KT):
                    mm(PS[0:2 * NB, 4 + s, 0:ADA_COLS], CT[:, k, :], wh[:, k, :], k == 0, False)
                    q = mm(PS[0:NB, 4 + s, 0:ADA_COLS], CT[:, k, 0:NB], wl[:, k, :], False, k == KT - 1)
                q.then_inc(a_mm[s], 1)

            def ada_tr(s, n):
                pe.wait_ge(a_row[s], n + 1)
                pe.wait_ge(a_mod[s], n)
                for j in range(2):
                    q = mm(PS[:, 6 + s, j * NB:(j + 1) * NB], AROW[:, s, j * P:(j + 1) * P], CON[0:2 * NB, CS18:CS18 + NB])
                q.then_inc(a_tr[s], 1)

            for unit in range(2 * ADA_FIRST + 2):
                if unit < 2 * ADA_FIRST:
                    ada_mm(unit % 2, unit // 2, unit)
                if unit >= 2:
                    ada_tr(unit % 2, unit // 2 - 1)

            for s in range(2):
                pe.wait_ge(a_row[s], ADA_FIRST)
                pe.wait_ge(a_mod[s], ADA_FIRST)

            def norm(p, product):
                pe.wait_ge(x_norm, NT * (p + 1))
                for k in range(KT + 3):
                    if k < KT:
                        if k >= 2:
                            pe.wait_ge(v_p, KT * p + k - 1)
                            pe.wait_ge(v_s, KT * p + k - 1)
                        for t in range(NT):
                            dst = PS[:, 4 + k % 2, t * P:(t + 1) * P] if t < NTP else PS[:, 6 + k % 2, 0:P]
                            q = pe.transpose(dst, XN[:, t, k * P:(k + 1) * P], ident)
                        q.then_inc(x_tr, 1)
                    if k >= 3:
                        pe.wait_ge(h_hi, KT * p + k - 2)
                        pe.wait_ge(h_lo, KT * p + k - 2)
                        product(k - 3)

            def ffn_block(s, k):
                wh, wl = ffn_view(WH, s), ffn_view(WL, s)
                for w, h, first, last in ((wh, HTH, True, False), (wh, HTL, False, False), (wl, HTH, False, True)):
                    for a in range(2):
                        q = mm(PS[:, 2 * s + a, 0:HALF], w[:, k, :], h[:, k, a * HALF:(a + 1) * HALF],
                               k == 0 and first, k == KT - 1 and last)
                return q

            def ffn_first(n):
                def product(k):
                    if k == 0:
                        pe.wait_ge(f_hi[0], n + 1)
                        pe.wait_ge(f_lo[0], n + 1)
                    q = ffn_block(0, k)
                    if k == KT - 1:
                        q.then_inc(f_mm[0], 1)
                return product

            def ffn_mm(s, n):
                pe.wait_ge(f_hi[s], n + 1)
                pe.wait_ge(f_lo[s], n + 1)
                pe.wait_ge(f_act if s else f_silu, n)
                for k in range(KT):
                    q = ffn_block(s, k)
                q.then_inc(f_mm[s], 1)

            def out_mm(s, n, start=False, stop=False, before=None):
                pe.wait_ge(k_hi[s], 2 * (n + 1))
                pe.wait_ge(k_lo[s], 2 * (n + 1))
                for t in range(NT):
                    if before:
                        before(t)
                    th, tl = ASTH[:, s, t * P:(t + 1) * P], ASTL[:, s, t * P:(t + 1) * P]
                    mm(PS[:, t, :], th, out_view(WH, s), start, False)
                    mm(PS[:, t, :], th, out_view(WL, s), False, False)
                    q = mm(PS[:, t, :], tl, out_view(WH, s), False, stop)
                    if stop and t < NT - 1:
                        q.then_inc(out_done, 1)
                return q

            def ffn_out(f):
                for half in range(2):
                    n0 = (2 * f + half) * OUT_TURNS
                    def free(t):
                        if half:
                            pe.wait_ge(y_copied, 4 * NT * f + t + 1)
                        elif t == 0:
                            pe.wait_ge(f_silu, (f + 1) * FT)
                        elif t == 2:
                            pe.wait_ge(f_act, (f + 1) * FT)

                    def with_ada(n, start=False):
                        out_mm(0, n, start=start, before=free if start else None).then_inc(k_mm[0], 1)
                        ada_mm(1, ADA_FIRST + FT + n)
                        out_mm(1, n).then_inc(k_mm[1], 1)
                        ada_tr(1, ADA_FIRST + FT + n)

                    def turns(first, end):
                        with pe.Fori(n0 + first, n0 + end) as n:
                            for s in range(2):
                                out_mm(s, n).then_inc(k_mm[s], 1)

                    if half == 0:
                        if f == 0:
                            with_ada(0, True)
                            with pe.Fori(1, ADA_OUT) as n:
                                with_ada(n)
                            pe.wait_ge(a_row[1], ADA_FIRST + FT + ADA_OUT)
                        else:
                            out_mm(0, n0, start=True, before=free).then_inc(k_mm[0], 1)
                            out_mm(1, n0).then_inc(k_mm[1], 1)
                            turns(1, ADA_OUT)
                        turns(ADA_OUT, ADA_OUT + 1)
                        if f == 0:
                            pe.wait_ge(a_mod[1], ADA_FIRST + FT + ADA_OUT)
                        gate_mms(2 * f, range(3))
                        turns(ADA_OUT + 1, ADA_OUT + 2)
                        gate_mms(2 * f, [3])
                        turns(ADA_OUT + 2, OUT_TURNS - 1)
                    else:
                        out_mm(0, n0, start=True, before=free).then_inc(k_mm[0], 1)
                        out_mm(1, n0).then_inc(k_mm[1], 1)
                        turns(1, OUT_TURNS - 1)
                    out_mm(0, n0 + OUT_TURNS - 1).then_inc(k_mm[0], 1)
                    out_mm(1, n0 + OUT_TURNS - 1, stop=True).then_inc(k_mm[1], 1)

            def gate_mms(r, js):
                pe.wait_ge(gate_bc, 2 * (r + 1))
                for j in js:
                    if j == 3:
                        pe.wait_ge(gate_rows, 4 * r + 1)
                    for k in range(4):
                        q = pe.transpose(PS[:, 5 + j % 3, k * P:(k + 1) * P], GATE_BUF[r][j // 2][:, 4 * (j % 2) + k, :], ident)
                    q.then_inc(gate_mm, 1)

            norm(0, ffn_first(0))
            def rest_of_turn(m):
                ada_mm(1, ADA_FIRST + m)
                ffn_mm(1, m)
                ada_tr(1, ADA_FIRST + m)
            rest_of_turn(0)
            with pe.Fori(1, FT) as m:
                ffn_mm(0, m)
                rest_of_turn(m)

            ffn_out(0)
            pe.wait_ge(gate_rows, 4)
            pe.wait_ge(y_copied, 2 * NT)
            def project_block(k):
                half, n = k // 4, GROUPS[0][2]
                if k % 4 == 0:
                    pe.wait_ge(g_hi[half], 1)
                    pe.wait_ge(g_lo[half], 1)
                wh, wl = grp_view(WH, half, n), grp_view(WL, half, n)
                for t in range(NTP):
                    th, tl = (T[:, k, t * P:(t + 1) * P] for T in (HTH, HTL))
                    mm(PS[:, t, 0:n], th, wh[:, k % 4, :], k == 0, False)
                    mm(PS[:, t, 0:n], th, wl[:, k % 4, :], False, False)
                    q = mm(PS[:, t, 0:n], tl, wh[:, k % 4, :], False, k == KT - 1)
                    if k == KT - 1:
                        q.then_inc(g_bank, 1)

            norm(1, project_block)

            def project(g, s, t):
                n = GROUPS[g][2]
                if t == 0:
                    pe.wait_ge(g_hi[s], g + 1)
                    pe.wait_ge(g_lo[s], g + 1)
                if s == 0 and 1 <= g <= 7:
                    pe.wait_ge(g_free, NT * (g - 1) + t + 1)
                wh, wl = grp_view(WH, s, n), grp_view(WL, s, n)
                for k in range(4):
                    th, tl = (T[:, 4 * s + k, t * P:(t + 1) * P] for T in (HTH, HTL))
                    mm(PS[:, t, 0:n], th, wh[:, k, :], s == 0 and k == 0, False)
                    mm(PS[:, t, 0:n], th, wl[:, k, :], False, False)
                    q = mm(PS[:, t, 0:n], tl, wh[:, k, :], False, s == 1 and k == 3)
                return q

            def rope_transposes(n):
                pe.wait_ge(rope_done, n + 1)
                if n >= 2:
                    pe.wait_ge(rope_t, n - 1)
                else:
                    pe.wait_ge(q_t, 5)
                for h in range(HD):
                    q = pe.transpose(PS[:, 5 + n % 2, h * P:(h + 1) * P], DQK[:, n % 2, h * P:(h + 1) * P], ident)
                q.then_inc(rope_tr, 1)

            def gate_transposes():
                pe.wait_ge(g_free, NT)
                for c in range(2):
                    for t in range(NT):
                        dst = PS[0:HM, 5 + c, t * P:(t + 1) * P] if t < NTP else PS[0:HM, 7, c * P:(c + 1) * P]
                        q = pe.transpose(dst, MQG[:, t, 256 + 4 * c:260 + 4 * c], ident)
                q.then_inc(gates_tr, 1)

            def qk_transposes(n):
                pe.wait_ge(g_free, 2 * NT)
                pe.wait_ge(gates_row, 4)
                if n >= 3:
                    pe.wait_ge(q_t, n - 2)
                for t in range(NTP):
                    src, j, tile = ((MQG, MK)[n // 2], n % 2, t) if n < 4 else ((MQG, MK)[t // 2], t % 2, NTP)
                    q = pe.transpose(PS[:, 5 + n % 3, t * P:(t + 1) * P], src[:, tile, j * P:(j + 1) * P], ident)
                q.then_inc(q_tr, 1)

            def column_transposes():
                pe.wait_ge(q_t, 3)
                pe.wait_ge(rows_ready, 1)
                for k, row in enumerate((ROWA, ROWI, ROWR, ROWB)):
                    for t in range(NT):
                        q = pe.transpose(PS[:, 7, (k * NT + t) * HM:(k * NT + t + 1) * HM], row[:, t * P:(t + 1) * P], ident[0:HM, 0:HM])
                q.then_inc(cols_tr, 1)

            def segment_weights():
                pe.wait_ge(cols_exp, 2)
                pe.wait_ge(seg_exp, 1)
                pe.wait_ge(seg_d, 1)
                for j in range(2):
                    mm(PS[:, 7, 4 * j:4 * j + 4], CON[0:HM, CPAIR + j * P:CPAIR + (j + 1) * P], WSR[:, 36:40])
                mm(PS[:, 7, 8:40], CON[0:HM, CONE:CONE + P], WSR[:, 48:80])
                pe.transpose(PS[0:DB, 7, 40:44], WSR[:, 40:48], ident[0:HM, 0:HM]).then_inc(seg_mm, 1)

            def scaled_queries(j):
                pe.wait_ge(seg_bc, 2)
                pe.wait_ge(qs_ready, 1)
                if j:
                    pe.wait_ge(qs_t, 1)
                for t in range(1, NTP):
                    q = pe.transpose(PS[:, 7, t * P:(t + 1) * P], MQG[:, t, j * P:(j + 1) * P], ident)
                q.then_inc(qs_tr, 1)

            preparation = {(1, 0): [gate_transposes], (2, 1): [lambda: qk_transposes(0), lambda: qk_transposes(1), lambda: qk_transposes(2)],
                           (3, 0): [lambda: qk_transposes(3), lambda: qk_transposes(4)], (3, 1): [column_transposes],
                           (4, 1): [segment_weights], (5, 0): [lambda: scaled_queries(0)], (6, 0): [lambda: scaled_queries(1)]}
            for g in range(7):
                for s in range(2):
                    for t in range(NT):
                        if g == 0 and t < NTP:
                            continue
                        q = project(g, s, t)
                        if s == 1:
                            q.then_inc(g_bank, 1)
                        elif t == NT - 1:
                            q.then_inc(g_half, 1)
                        if g in (4, 5) and s == 1 and t >= 1:
                            rope_transposes(NT * (g - 4) + t - 1)
                        if g in (5, 6) and s == 0 and t == 0:
                            rope_transposes(NT * (g - 5) + 4)
                    for step in preparation.get((g, s), ()):
                        step()

            pe.wait_ge(rope_t, 2 * NT)
            pe.wait_ge(g_free, 7 * NT)
            pe.wait_ge(qs_t, 2)

            def state_transposes(pr):
                pe.wait_ge(mst_landed, 16 * 7)
                if pr:
                    pe.wait_ge(st_t, pr)
                for h in range(HM):
                    q = pe.transpose(PS[:, 7, h * DV:(h + 1) * DV], SC[:, h, 2 * pr:2 * pr + 2, :], ident)
                q.then_inc(st_tr, 1)

            def half(h):
                return slice(64 * (h % 2), 64 * (h % 2) + 64)

            def m_score(c):
                tok = slice(c * P, (c + 1) * P)
                if c >= 2:
                    pe.wait_ge(m_s, c - 1)
                    pe.wait_ge(m_arg, c - 1)
                for h in (0, 2):
                    q = mm(PS[:, c % 2, h * P:(h + 1) * P], MKT[half(h), h // 2, tok], MQT[half(h), h // 2, tok])
                q.then_inc(m_even, 1)
                for h in range(HM):
                    q = mm(PS[:, 2 + c % 2, h * P:(h + 1) * P], CON[0:HM, CHEAD + h * P:CHEAD + (h + 1) * P], ROWM[:, tok])
                q.then_inc(m_scores, 1)
                pe.wait_ge(m_even, c + 1)
                for h in (1, 3):
                    q = mm(PS[:, c % 2, h * P:(h + 1) * P], MKT[half(h), h // 2, tok], MQT[half(h), h // 2, tok])
                q.then_inc(m_scores, 1)

            def m_state_part(c):
                pe.wait_ge(m_kw, c + 1)
                if c:
                    pe.wait_ge(m_state, c)
                for h in range(HM):
                    o_ = 129 * (h // 2)
                    q = mm(PS[half(h), 6, o_:o_ + DV + 1], KW[:, h, :], MVX[:, c, h, :])
                q.then_inc(m_cu, 1)

            def m_out(c, h):
                return PS[:, 4 + h % 2, 129 * (h // 2):129 * (h // 2) + DV + 1]

            m_score(0)
            for c in range(NTP):
                m_score(c + 1)
                m_state_part(c)
                if c in (2, 3):
                    state_transposes(c - 2)
                pe.wait_ge(m_s, c + 1)
                if c:
                    pe.wait_ge(m_state, c)
                    pe.wait_ge(m_head, 2 * c)
                for h in range(HM):
                    q = mm(m_out(c, h), ST[:, h, :], MVX[:, c, h, :], True, c == 0)
                    if c:
                        q = mm(m_out(c, h), QST[half(h), h // 2, c * P:(c + 1) * P], CTX[half(h), h // 2, :], False, True)
                    if h >= 2:
                        q.then_inc(m_hn, 1)

            for pr in (2, 3):
                state_transposes(pr)
            pe.wait_ge(st_t, 4)
            pe.transpose(PS[:, 7, 0:32], NROW[:, :], ident[0:32, 0:32]).then_inc(st_tr, 1)
            pe.wait_ge(st_n, 2)
            pe.wait_ge(m_state, NTP)

            def query_transposes(h):
                pe.wait_ge(qb_ready, h + 1)
                if h >= 2:
                    pe.wait_ge(qb_t, h - 1)
                for r in range(DB // 2):
                    q = pe.transpose(PS[:, 6 + h % 2, r * P:(r + 1) * P], QB[:, 2 * r:2 * r + 2, :], ident)
                q.then_inc(qb_tr, 1)

            query_transposes(0)
            pe.wait_ge(m_s, NT)
            pe.wait_ge(m_head, 2 * NTP)
            for h in range(HM):
                if h + 1 < HM:
                    query_transposes(h + 1)
                mm(m_out(NTP, h), ST[:, h, :], MVX[:, NTP, h, :], True, False)
                pe.wait_ge(qb_t, h + 1)
                for r in range(DB // 2):
                    q = mm(m_out(NTP, h), QBT[h % 2][:, r, :], SCT[:, r, h, :], False, r == DB // 2 - 1)
                q.then_inc(m_hn if h >= 2 else qb_mm, 1)
            for h in range(HM):
                pe.wait_ge(kb_ready, h + 1)
                if h >= 2:
                    pe.wait_ge(c_new, h - 1)
                else:
                    pe.wait_ge(qb_t, HM)
                mm(PS[:, 6 + h % 2, :], MVX[:, NTP, h, 0:DV], KBM[h % 2][:, :, :]).then_inc(cu_s, 1)
            pe.wait_ge(m_arg, NT)
            pe.wait_ge(qs_ready, 2)
            for h in range(HM):
                q = mm(PS[0:DB, 3, h * DQ:(h + 1) * DQ], WB[:, h, :], MK[:, NTP, h * DQ:(h + 1) * DQ])
            q.then_inc(n_mm, 1)
            for j in range(2):
                q = pe.transpose(PS[:, 2, j * P:(j + 1) * P], CTX[:, j, 0:DV], ident)
            q.then_inc(fin_tr, 1)

            pe.wait_ge(fin_c, 1)
            pe.wait_ge(m_s, NT)
            pe.wait_ge(m_head, 2 * NT)
            pe.wait_ge(c_new, HM)
            pe.wait_ge(c_new, HM + 1)

            def p_score(n):
                t, h = n // HD, n % HD
                if n >= 2:
                    pe.wait_ge(p_exp, 2 * (n - 1))
                for c in range(2):
                    q = mm(PS[:, 2 * (n % 2) + c, 0:P * (t + 1)], DQT[half(c), h, t * P:(t + 1) * P], DKT[half(c), h, 0:P * (t + 1)])
                q.then_inc(p_scores, 1)

            def p_transpose(n):
                pe.wait_ge(p_comb, n + 1)
                if n >= 2:
                    pe.wait_ge(p_t, n - 1)
                for k in range(n // HD + 1):
                    q = pe.transpose(PS[:, 4 + n % 2, k * P:(k + 1) * P], PR[:, n % 2, 0, k * P:(k + 1) * P], ident)
                q.then_inc(p_tr, 1)

            def p_out(n):
                t, h = n // HD, n % HD
                pe.wait_ge(p_t, n + 1)
                if t >= 2 and h == 0:
                    pe.wait_ge(p_copied, t - 1)
                for k in range(t + 1):
                    q = mm(PS[:, 6 + t % 2, h * DV:(h + 1) * DV], PTT[:, n % 2, k * P:(k + 1) * P], DVT[:, k, h * DV:(h + 1) * DV], k == 0, k == t)
                q.then_inc(p_o, 1)

            last_n = NTP * HD
            p_score(0)
            for n in range(last_n):
                if n + 1 < last_n:
                    p_score(n + 1)
                if n:
                    p_out(n - 1)
                p_transpose(n)
            p_out(last_n - 1)

            pe.wait_ge(p_exp, 2 * last_n)
            pe.wait_ge(p_copied, NTP)
            pe.wait_ge(qbd_ready, 1)

            def s_key_transposes(b):
                pe.wait_ge(kc_landed[b % 3], 16 * (b // 3 + 1))
                if b >= 2:
                    pe.wait_ge(s_kta, b - 1)
                    pe.wait_ge(s_ktd, b - 1)
                for k in range(2):
                    for h in range(HD):
                        q = pe.transpose(PS[:, 6 * (b % 2) + k, h * P:(h + 1) * P], KC[b % 3][:, k, h * P:(h + 1) * P], ident)
                    q.then_inc(s_ktr, 1)

            def s_score(b):
                pe.wait_ge(s_kta, b + 1)
                pe.wait_ge(s_ktd, b + 1)
                if b >= 2:
                    pe.wait_ge(s_exp, b - 1)
                for h in range(HD):
                    rows = slice(32 * h, 32 * h + 32)
                    mm(PS[rows, 2 + b % 2, 0:PAST], QBD[:, b, h, :], KCT[b % 2][:, h, :])
                    q = mm(PS[rows, 2 + b % 2, PAST:PAST + DS], QBD[:, b, h, :], DKT[:, h, SEQ + b * DS:SEQ + (b + 1) * DS])
                q.then_inc(s_scores, 1)

            def s_combine(b):
                pe.wait_ge(s_mr, b + 1)
                if b:
                    pe.wait_ge(s_pt, 2 * b)
                for k in range(3):
                    n = P if k < 2 else DS
                    q = mm(PS[0:n, 4, k * P:(k + 1) * P], PS_[:, b % 2, k * P:k * P + n], MR[:, :])
                q.then_inc(s_ptr, 1)

            def s_out(b):
                pe.wait_ge(s_pt, 2 * (b + 1))
                pe.wait_ge(vc_landed[b % 3], 32 * (b // 3 + 1))
                if b:
                    pe.wait_ge(s_ob, b)
                mm(PS[:, 5, :], PTS[:, 0, :], VC[b % 3][:, 0, :], True, False)
                mm(PS[:, 5, :], PTS[:, 1, :], VC[b % 3][:, 1, :], False, False)
                mm(PS[:, 5, :], PTS[0:DS, 2, :], VN[b % 3][:, :], False, True).then_inc(s_o, 1)

            s_key_transposes(0)
            for b in range(DB + 2):
                if b < DB:
                    s_score(b)
                if b + 1 < DB:
                    s_key_transposes(b + 1)
                if b >= 2:
                    s_out(b - 2)
                if 1 <= b <= DB:
                    s_combine(b - 1)
            def output_block(k):
                half, n = k // 4, GROUPS[7][2]
                if k % 4 == 0:
                    pe.wait_ge(g_hi[half], 8)
                    pe.wait_ge(g_lo[half], 8)
                wh, wl = grp_view(WH, half, n), grp_view(WL, half, n)
                for t in range(NT):
                    th, tl = (T[:, k, t * P:(t + 1) * P] for T in (HTH, HTL))
                    mm(PS[:, t, 0:n], th, wh[:, k % 4, :], k == 0, False)
                    mm(PS[:, t, 0:n], th, wl[:, k % 4, :], False, False)
                    q = mm(PS[:, t, 0:n], tl, wh[:, k % 4, :], False, k == KT - 1)
                    if k == KT - 1:
                        q.then_inc(g_bank, 1)
                        if t == 0:
                            gate_mms(1, [3])
                if k == 3:
                    q.then_inc(g_half, 1)

            pe.wait_ge(s_ob, DB)
            for k in range(KT + 2):
                if k >= 2:
                    pe.wait_ge(hh_hi, k - 1)
                    pe.wait_ge(hh_lo, k - 1)
                if k == 0:
                    pe.wait_ge(heads, NT)
                elif k == 4:
                    pe.wait_ge(heads, NT + NTP)
                    pe.wait_ge(heads_s, 1)
                if k < KT:
                    src = HHM if k < 4 else HDF
                    if k % 4 == 0:
                        for j in range(4):
                            pe.transpose(PS[:, 7, j * P:(j + 1) * P], src[:, NTP, j * P:(j + 1) * P], ident)
                    for t in range(NTP):
                        q = pe.transpose(PS[:, 5 + k % 2, t * P:(t + 1) * P], src[:, t, (k % 4) * P:(k % 4 + 1) * P], ident)
                    q.then_inc(hh_tr, 1)
                if k == KT + 1:
                    gate_mms(1, range(3))
                if k >= 2:
                    output_block(k - 2)
            for s in range(2):
                for t in range(NT):
                    if s == 0:
                        pe.wait_ge(y_copied, 2 * NT + t + 1)
                    q = project(8, s, t)
                    if s == 1:
                        q.then_inc(g_bank, 1)
                if s == 0:
                    q.then_inc(g_half, 1)
            pe.wait_ge(y_copied, 4 * NT)
            pe.wait_ge(f_silu, FT)
            norm(2, ffn_first(FT))
            ffn_mm(1, FT)
            with pe.Fori(FT + 1, 2 * FT) as n:
                ffn_mm(0, n)
                ffn_mm(1, n)
            ffn_out(1)
        @block.vector
        def _(dve):
            link = chain(dve, dvec)
            dve.wait_ge(c_tr, 2)
            dve.wait_ge(c_silu, 2)
            dve.tensor_tensor(CT[:, :, NB:2 * NB], PS[:, 7, 0:KT * NB].rearrange("p (k b) -> p k b", k=KT),
                              CT[:, :, 0:NB].bitcast(F32), ALU.subtract).then_inc(c_ready, 1)
            dve.tensor_copy(BT[:, :], PS[:, 6, 0:NADA * KT]).then_inc(c_ready, 1)
            dve.tensor_copy(GT[:, :], PS[:, 6, P:P + 6 * KT]).then_inc(c_ready, 1)
            dve.wait_ge(c_ready, 3)

            def split_lo(dst, raw, hi):
                return dve.tensor_tensor(dst, raw, hi.bitcast(F32), ALU.subtract)

            def inverse_mean(col, squares, count, done):
                dve.wait_ge(squares, count)
                if col:
                    link(dve.tensor_tensor(SS[:, 1, :], SS[:, 1, :], SS[:, 2, :], ALU.add))
                link(dve.tensor_scalar(SS[:, col, :], SS[:, col, :], 1.0 / D, EPS, ALU.mult, ALU.add))
                dve.reciprocal(SS[:, col, :], SS[:, col, :]).then_inc(done, 1)

            def norm_rows(p):
                inverse_mean(0, x_sq, NT * (p + 1), x_ms)
                dve.wait_ge(x_rstd, p + 1)
                for t in range(NT - 2):
                    dve.tensor_scalar(XN[:, t, :], X[:, t, :], RS[:, 0, t:t + 1], None, ALU.mult).then_inc(x_norm, 1)

            norm_rows(0)

            def ada_lo(s, n):
                dve.wait_ge(a_hi[s], n + 1)
                split_lo(WL[:, s, :], RAW[:, s, :], WH[:, s, :]).then_inc(a_lo[s], 1)

            def ada_mod(s, unit, n):
                dve.wait_ge(a_tr[s], n + 1)
                dve.tensor_tensor(MODT[:, bass.ds(2 * unit, 2), :], PS[:, 6 + s, 0:2 * NB].rearrange("p (j b) -> p j b", j=2),
                                  BT[:, bass.ds(2 * unit, 2)].rearrange("p (j b) -> p j b", b=1).to_broadcast([P, 2, NB]), ALU.add).then_inc(a_mod[s], 1)

            for unit in range(2 * ADA_FIRST + 3):
                if unit < 2 * ADA_FIRST:
                    dve.wait_ge(a_hi[unit % 2], unit // 2 + 1)
                    split_lo(start_lo(unit), RAW_START[:, unit % START_SLOTS, :], start_hi(unit)).then_inc(a_lo[unit % 2], 1)
                if unit >= 3:
                    ada_mod((unit - 3) % 2, unit - 3, (unit - 3) // 2)

            def gain(g):
                return GT[:, g * KT:(g + 1) * KT].rearrange("p (k b) -> p k b", b=1).to_broadcast([P, KT, NB])

            def mod(j):
                return MODT[:, j * KT:(j + 1) * KT, :]

            def mods_known(units0, units1):
                dve.wait_ge(a_mod[0], units0)
                dve.wait_ge(a_mod[1], units1)

            def norm(p, between=None):
                dve.scalar_tensor_tensor(SCA[:, :, :], mod(3 * p + 1), 1.0, gain(2 * p), ALU.add, ALU.mult).then_inc(sca_ready, 1)
                dve.wait_ge(sca_ready, p + 1)

                def lo(k):
                    dve.wait_ge(h_hi, KT * p + k + 1)
                    split_lo(HTL[:, k, :], V[:, k % 4, :], HTH[:, k, :]).then_inc(h_lo, 1)

                for k in range(KT):
                    dve.wait_ge(x_tr, KT * p + k + 1)
                    v = V[:, k % 4, SEQ:TOK].rearrange("p (b s) -> p b s", b=DB)
                    tr = PS[:, 6 + k % 2, 0:P].rearrange("p (b s) -> p b s", b=DB)
                    sc = SCA[:, k, 1:NB].rearrange("p (b s) -> p b s", s=1).to_broadcast([P, DB, DS])
                    sh = mod(3 * p)[:, k, 1:NB].rearrange("p (b s) -> p b s", s=1).to_broadcast([P, DB, DS])
                    if k >= 4:
                        dve.wait_ge(h_lo, KT * p + k - 3)
                    link(dve.tensor_tensor(v, tr, sc, ALU.mult))
                    dve.tensor_tensor(v, v, sh, ALU.add).then_inc(v_s, 1)
                    if between:
                        between(k)
                    if k >= 1:
                        lo(k - 1)
                lo(KT - 1)

            def ffn_lo(s, n):
                dve.wait_ge(f_hi[s], n + 1)
                w = slice(s * 1024, (s + 1) * 1024)
                split_lo(WL[:, 0, w], RAW[:, 0, w], WH[:, 0, w]).then_inc(f_lo[s], 1)

            def ffn_act(m, n):
                dve.wait_ge(f_mm[1], n + 1)
                dve.wait_ge(f_silu, n + 1)
                dve.tensor_tensor(ACTT[:, bass.ds(m, 1), :].rearrange("p m (a n) -> p (m a) n", a=2), SIL[:, :].rearrange("p (a n) -> p a n", a=2),
                                  PS[:, 2:4, 0:HALF], ALU.mult).then_inc(f_act, 1)

            def out_lo(s, t, n):
                dve.wait_ge(k_hi[s], 2 * n + 1)
                w = slice(s * 1024, s * 1024 + 512)
                split_lo(WL[:, 0, w], RAW[:, 0, w], WH[:, 0, w]).then_inc(k_lo[s], 1)
                dve.wait_ge(k_hi[s], 2 * n + 2)
                split_lo(ASTL[:, s, :], ACTT[:, bass.ds(2 * t + s, 1), :].rearrange("p a n -> p (a n)"), ASTH[:, s, :]).then_inc(k_lo[s], 1)

            def y_gated(r, half):
                for t in range(NT):
                    dve.wait_ge(y_sq, 2 * NT * r + NT * half + t + 1)
                    if t == 0 and half == 0:
                        dve.wait_ge(gate_rows, 4 * (r + 1))
                    cols = slice(half * 512, (half + 1) * 512)
                    dve.tensor_tensor(Y[:, t, cols], PS[:, t, :], GATE_BUF[r][2][:, t // NTP, cols], ALU.mult).then_inc(y_copied, 1)

            def gate(r):
                w = 1.0 if r == 1 else 0.5
                dve.scalar_tensor_tensor(GATE[:, :, :], mod(3 * r + 2), w, gain(2 * r + 1), ALU.mult, ALU.mult).then_inc(gate_t, 1)

            def ffn_out(f):
                n0 = 2 * f * OUT_TURNS
                def turn(t, ada=False):
                    if not (isinstance(t, int) and t == 0):
                        out_lo(0, t, n0 + t)
                    if ada:
                        ada_lo(1, ADA_FIRST + FT + t)
                        ada_mod(1, 2 * ADA_FIRST + FT - 1 + t, ADA_FIRST + FT - 1 + t)
                    out_lo(1, t, n0 + t)
                from_zero(dve, ADA_OUT, lambda t: turn(t, f == 0))
                turn(ADA_OUT)
                if f == 0:
                    ada_mod(1, ADA_UNITS - 1, ADA_FIRST + FT + ADA_OUT - 1)
                with dve.Fori(ADA_OUT + 1, OUT_TURNS) as t:
                    turn(t)

                n0 += OUT_TURNS
                out_lo(0, 0, n0)
                y_gated(2 * f, 0)
                out_lo(1, 0, n0)
                with dve.Fori(1, OUT_TURNS) as t:
                    for s in range(2):
                        out_lo(s, t, n0 + t)
                y_gated(2 * f, 1)

            def residual(r):
                inverse_mean(1, y_sq, 2 * NT * (r + 1), y_ms)
                dve.wait_ge(y_rstd, r + 1)
                dve.wait_ge(y_copied, 2 * NT * (r + 1))
                for t in range(NT):
                    dve.scalar_tensor_tensor(X[:, t, :], Y[:, t, :], RS[:, 1, t:t + 1], X[:, t, :], ALU.mult, ALU.add).then_inc(x_new, 1)

            mods_known(ADA_FIRST, ADA_FIRST)
            norm(0, lambda k: ffn_lo(k - 1, 0) if k in (1, 2) else None)
            ada_lo(1, ADA_FIRST)
            ffn_lo(0, 1)
            with dve.Fori(1, FT - 1) as m:
                ffn_act(m - 1, m - 1)
                ffn_lo(1, m)
                ada_lo(1, ADA_FIRST + m)
                ada_mod(1, 2 * ADA_FIRST - 1 + m, ADA_FIRST - 1 + m)
                ffn_lo(0, m + 1)
            ffn_act(FT - 2, FT - 2)
            ffn_lo(1, FT - 1)
            ada_lo(1, ADA_FIRST + FT - 1)
            ada_mod(1, 2 * ADA_FIRST + FT - 2, ADA_FIRST + FT - 2)
            out_lo(0, 0, 0)
            ffn_act(FT - 1, FT - 1)
            mods_known(ADA_FIRST, ADA_FIRST + FT - 1)
            gate(0)
            ffn_out(0)
            mods_known(ADA_FIRST, ADA_FIRST + FT + ADA_OUT)
            residual(0)
            norm_rows(1)

            def grp_lo(g, s):
                n = 4 * GROUPS[g][2]
                dve.wait_ge(g_hi[s], g + 1)
                split_lo(WL[:, s, 0:n], RAW[:, s, 0:n], WH[:, s, 0:n]).then_inc(g_lo[s], 1)

            norm(1, lambda k: grp_lo(0, k - 1) if k in (1, 2) else None)

            def rope(n):
                t = n % NT
                dve.wait_ge(g_free, NT * (4 + n // NT) + t + 1)
                x = DQK[:, n % 2, :].rearrange("p (h a j) -> p h a j", h=2 * HD, j=8)
                tab = CON[:, CROPE + 24 * t:CROPE + 24 * t + 24].rearrange("p (x a j) -> p x a j", x=1, j=8)
                cos, nsin, sin = (tab[:, :, a, :].to_broadcast([P, 2 * HD, 8]) for a in range(3))
                dve.tensor_tensor(R1[:, n % 2, :, 0, :], x[:, :, 0, :], cos, ALU.mult)
                dve.tensor_tensor(R1[:, n % 2, :, 1, :], x[:, :, 1, :], cos, ALU.mult)
                dve.tensor_tensor(R2[:, n % 2, :, 0, :], x[:, :, 1, :], nsin, ALU.mult)
                link(dve.tensor_tensor(R2[:, n % 2, :, 1, :], x[:, :, 0, :], sin, ALU.mult))
                dve.tensor_tensor(x[:, :, 0:2, :], R1[:, n % 2, :, :, :], R2[:, n % 2, :, :, :], ALU.add).then_inc(rope_done, 1)

            def rope_copy(n):
                dve.wait_ge(rope_tr, n + 1)
                dst = DKT if n >= NT else DQT
                t = n % NT
                dve.tensor_copy(dst[:, :, t * P:(t + 1) * P], PS[:, 5 + n % 2, :].rearrange("p (h t) -> p h t", h=HD)).then_inc(rope_t, 1)

            bmask = CON[:, CBM:CBM + DB]

            def per_head(a, t):
                return COLE[:, a, t, :].rearrange("p (h d) -> p h d", d=1).to_broadcast([P, HM, DQ])

            def gate_rows_in():
                dve.wait_ge(gates_tr, 1)
                dve.wait_ge(gb_landed, 16 * 3)
                dve.tensor_scalar(ROWA[:, 0:SEQ], PS[0:HM, 5, :], WSR[:, 8:9], None, ALU.add).then_inc(gates_row, 1)
                dve.tensor_scalar(ROWA[:, SEQ:TOK], PS[0:HM, 7, 0:P], WSR[:, 8:9], None, ALU.add).then_inc(gates_row, 1)
                dve.tensor_scalar(ROWB[:, 0:SEQ], PS[0:HM, 6, :], WSR[:, 9:10], None, ALU.add).then_inc(gates_row, 1)
                dve.tensor_scalar(ROWB[:, SEQ:TOK], PS[0:HM, 7, P:2 * P], WSR[:, 9:10], None, ALU.add).then_inc(gates_row, 1)

            def row_chain():
                dve.wait_ge(ln_f, 1)
                dve.wait_ge(gates_row, 4)
                link(dve.scalar_tensor_tensor(ROWB[:, :], ROWB[:, :], 0.0, ROWR[:, :], ALU.min, ALU.subtract))

                def pseg(T):
                    return T[:, 0:SEQ].rearrange("h (c s) -> h c s", c=NTP)

                def sseg(T):
                    return T[:, SEQ:TOK].rearrange("h (b s) -> h b s", b=DB)

                def col(a, n):
                    return WSR[:, a:a + n].rearrange("h (c s) -> h c s", s=1)

                link(dve.memset(ROWM[:, :], 1.0))
                link(dve.memset(pseg(ROWM)[:, :, 0:1], 0.0))
                link(dve.memset(sseg(ROWM)[:, :, 0:1], 0.0))
                link(dve.tensor_tensor_scan(ROWI[:, :], ROWM[:, :], ROWB[:, :], 0.0, ALU.mult, ALU.add))
                link(dve.tensor_tensor(ROWA[:, :], ROWA[:, :], ROWI[:, :], ALU.subtract))
                link(dve.memset(ROWR[:, :], 0.0))
                link(dve.memset(sseg(ROWR)[:, :, 0:1], BIG))
                link(dve.tensor_copy(ROWB[:, SEQ:TOK], ROWA[:, SEQ:TOK]))
                link(dve.tensor_tensor(sseg(ROWB)[:, :, 0:1], sseg(ROWA)[:, :, 0:1], col(0, DB), ALU.max))
                link(dve.memset(WSR[:, 10:11], 0.0))
                for c in range(NTP):
                    w, e = slice(c * P, (c + 1) * P), (c + 1) * P - 1
                    link(dve.tensor_tensor_scan(ROWM[:, w], ROWR[:, w], ROWA[:, w], WSR[:, 10 + c:11 + c], ALU.add, ALU.max))
                    link(dve.tensor_tensor(WSR[:, 11 + c:12 + c], ROWI[:, e:e + 1], ROWM[:, e:e + 1], ALU.add))
                link(dve.tensor_tensor_scan(ROWM[:, SEQ:TOK], ROWR[:, SEQ:TOK], ROWB[:, SEQ:TOK], 0.0, ALU.add, ALU.max))
                link(dve.tensor_tensor(col(16, DB), sseg(ROWI)[:, :, DS - 1:DS], sseg(ROWM)[:, :, DS - 1:DS], ALU.add))
                dve.tensor_tensor(col(24, NTP), col(10, NTP), pseg(ROWM)[:, :, P - 1:P], ALU.subtract)
                dve.tensor_tensor(col(28, DB), col(0, DB), sseg(ROWM)[:, :, DS - 1:DS], ALU.subtract).then_inc(seg_arg, 1)
                dve.tensor_tensor(pseg(ROWB), pseg(ROWA), pseg(ROWM)[:, :, P - 1:P].to_broadcast([HM, NTP, P]), ALU.subtract)
                dve.tensor_tensor(sseg(ROWB), sseg(ROWA), sseg(ROWM)[:, :, DS - 1:DS].to_broadcast([HM, DB, DS]), ALU.subtract)
                link(dve.scalar_tensor_tensor(ROWR[:, :], ROWI[:, :], -1.0, ROWM[:, :], ALU.mult, ALU.subtract))
                dve.tensor_tensor(pseg(ROWI), col(10, NTP).to_broadcast([HM, NTP, P]), pseg(ROWM), ALU.subtract)
                dve.tensor_tensor(sseg(ROWI), col(0, DB).to_broadcast([HM, DB, DS]), sseg(ROWM), ALU.subtract).then_inc(rows_ready, 1)

            def qk_copy(a):
                dve.wait_ge(q_tr, a + 1)
                bank = PS[:, 5 + a % 3, :]
                if a < 4:
                    dve.tensor_copy((MQT, MKT)[a // 2][:, a % 2, 0:SEQ], bank).then_inc(q_t, 1)
                else:
                    dve.tensor_copy(MQT[:, :, SEQ:TOK], bank[:, 0:2 * P].rearrange("p (j t) -> p j t", j=2))
                    dve.tensor_copy(MKT[:, :, SEQ:TOK], bank[:, 2 * P:4 * P].rearrange("p (j t) -> p j t", j=2)).then_inc(q_t, 1)

            def segment_rows():
                dve.wait_ge(seg_exp, 1)
                dve.tensor_tensor(WSR[:, 48:80].rearrange("p (h b) -> p h b", h=HM), CON[0:HM, CDELTA:CDELTA + HM * DB].rearrange("p (h b) -> p h b", h=HM),
                                  WSR[:, 40:48].rearrange("p (h b) -> p h b", h=1).to_broadcast([HM, HM, DB]), ALU.mult).then_inc(seg_d, 1)

            def segment_copy():
                dve.wait_ge(seg_mm, 1)
                dve.tensor_copy(WSB[:, :], PS[:, 7, 0:40]).then_inc(seg_bc, 1)
                dve.tensor_copy(WS8[:, :], PS[0:DB, 7, 40:44]).then_inc(seg_bc, 1)

            def scale_queries():
                dve.wait_ge(cols_exp, 2)
                dve.wait_ge(q_tr, 5)

                for t in range(NT):
                    q4 = MQG[:, t, 0:256].rearrange("p (h d) -> p h d", h=HM)
                    q = dve.tensor_tensor(q4, q4, per_head(0, t), ALU.mult)
                q.then_inc(qs_ready, 1)
                dve.tensor_tensor(WB[:, :, :], bmask.rearrange("p (h b) -> p h b", h=1).to_broadcast([P, HM, DB]),
                                  COLE[:, 2, NTP, :].rearrange("p (h b) -> p h b", b=1).to_broadcast([P, HM, DB]), ALU.mult).then_inc(qs_ready, 1)

            def lambda_sums():
                dve.wait_ge(g_lam_landed, 16)
                dve.tensor_tensor(LAM[:, 0, :], LAM[:, 0, :], LAM[:, 1, :], ALU.mult)
                link(dve.tensor_tensor(LAM[:, 2, :], LAM[:, 2, :], LAM[:, 3, :], ALU.mult))
                dve.reduce_sum(LS[:, 0:1], LAM[:, 0, :], AXX)
                dve.reduce_sum(LS[:, 1:2], LAM[:, 2, :], AXX).then_inc(lam_s, 1)

            def lambda_row():
                dve.wait_ge(lam_e, 1)
                link(dve.scalar_tensor_tensor(LS[:, 4:5], LS[:, 3:4], -LAM_INIT, LS[:, 2:3], ALU.add, ALU.subtract))
                link(dve.scalar_tensor_tensor(LS[:, 5:6], CON[:, CSIGN + 1:CSIGN + 2], LS[:, 4:5], CON[:, CSIGN:CSIGN + 1], ALU.mult, ALU.add))

            def scaled_copy(j):
                dve.wait_ge(qs_tr, j + 1)
                dve.tensor_copy(QST[:, j, P:SEQ], PS[:, 7, P:SEQ]).then_inc(qs_t, 1)

            dve.wait_ge(g_bank, 1)
            dve.memset(MVX[:, :, :, DV:DV + 1], 1.0)
            for g in range(7):
                if g == 3:
                    for a in range(3):
                        qk_copy(a)
                if g < 6:
                    grp_lo(g + 1, 0)
                if g == 0:
                    lambda_sums()
                elif g == 1:
                    gate_rows_in()
                elif g == 2:
                    row_chain()
                elif g == 3:
                    qk_copy(3)
                    qk_copy(4)
                elif g == 4:
                    segment_rows()
                elif g == 6:
                    lambda_row()
                if g in (5, 6):
                    rope_copy(NT * (g - 4) - 1)
                if g in (4, 5):
                    for t in range(NT):
                        rope(NT * (g - 4) + t)
                        if t:
                            rope_copy(NT * (g - 4) + t - 1)
                if g == 4:
                    segment_copy()
                    scale_queries()
                elif g in (5, 6):
                    scaled_copy(g - 5)
                if g < 6:
                    grp_lo(g + 1, 1)
            dve.wait_ge(k_sent[0], 16 * 2)
            dve.wait_ge(k_sent[1], 16 * 3)

            def m_arguments(c):
                dve.wait_ge(m_scores, 2 * (c + 1))
                if c >= 2:
                    dve.wait_ge(m_s, c - 1)
                mask = CON[:, (CMS if c == NTP else CMP):(CMS if c == NTP else CMP) + P]
                for h in range(HM):
                    q = dve.scalar_tensor_tensor(ARG[c % 2][:, h, :], PS[:, 2 + c % 2, h * P:(h + 1) * P], COLA[:, c, h:h + 1], mask, ALU.add, ALU.add)
                q.then_inc(m_arg, 1)

            def m_keys(c):
                if c:
                    dve.wait_ge(m_cu, c)
                dve.tensor_tensor(KW[:, :, :], MK[:, c, :].rearrange("p (h d) -> p h d", h=HM), per_head(2, c), ALU.mult).then_inc(m_kw, 1)

            m_arguments(0)
            m_keys(0)
            for c in range(NT):
                dve.wait_ge(m_exp, c + 1)
                if c:
                    dve.wait_ge(m_hn, 2 * c)
                dve.tensor_tensor(ST[:, :, :], ARG[c % 2][:, :, :], PS[:, c % 2, :].rearrange("p (h t) -> p h t", h=HM), ALU.mult).then_inc(m_s, 1)
                if c < NTP:
                    m_arguments(c + 1)
                    m_keys(c + 1)
                    dve.wait_ge(m_cu, c + 1)
                    dve.wait_ge(m_hn, 2 * (c + 1))
                    for j in range(2):
                        cu = PS[:, 6, 129 * j:129 * j + DV + 1]
                        if c == 0:
                            q = dve.tensor_copy(CTX[:, j, :], cu)
                        else:
                            q = dve.scalar_tensor_tensor(CTX[:, j, :], CTX[:, j, :], WSB[:, 4 * j + c:4 * j + c + 1], cu, ALU.mult, ALU.add)
                    q.then_inc(m_state, 1)
                else:
                    dve.wait_ge(st_tr, 5)
                    for a in range(2):
                        r = slice(64 * a, 64 * a + 64)
                        dve.tensor_copy(SCT[r, :, :, DV:DV + 1], PS[r, 7, 0:32].rearrange("p (r i h w) -> p i r h w", i=2, h=HM, w=1)[:, a, :, :, :]).then_inc(st_n, 1)
                    for h in range(HM):
                        if h:
                            dve.wait_ge(qb_tr, h)
                        dve.tensor_tensor(QB[:, :, :], MQG[:, c, h * DQ:(h + 1) * DQ].rearrange("p (b d) -> p b d", b=1).to_broadcast([P, DB, DQ]),
                                          bmask.rearrange("p (b d) -> p b d", d=1).to_broadcast([P, DB, DQ]), ALU.mult).then_inc(qb_ready, 1)
                for a in range(2):
                    dve.wait_ge(m_hn, 2 * c + a + 1)
                    hn = PS[:, 4 + a, 0:258].rearrange("p (h v) -> p h v", h=2)
                    den = DEN[:, c, a:HM:2].rearrange("p (h v) -> p h v", v=1)
                    link(dve.scalar_tensor_tensor(den, hn[:, :, DV:DV + 1], -1.0, COLE[:, 1, c, a:HM:2].rearrange("p (h v) -> p h v", v=1), ALU.mult, ALU.max))
                    link(dve.tensor_tensor(den, den, hn[:, :, DV:DV + 1], ALU.max))
                    link(dve.reciprocal(den, den))
                    dve.tensor_tensor(HHM[:, c, :].rearrange("p (h v) -> p h v", h=HM)[:, a:HM:2, :], hn[:, :, 0:DV],
                                      den.to_broadcast([P, 2, DV]), ALU.mult).then_inc(m_head, 1)
            def keys_by_batch(h):
                dve.wait_ge(m_s, NT)
                dve.wait_ge(m_kw, NT)
                if h >= 2:
                    dve.wait_ge(cu_s, h - 1)
                dve.tensor_tensor(KBM[h % 2][:, :, :], KW[:, h, :].rearrange("p (b d) -> p b d", b=1).to_broadcast([P, DB, DQ]),
                                  bmask.rearrange("p (b d) -> p b d", d=1).to_broadcast([P, DB, DQ]), ALU.mult).then_inc(kb_ready, 1)

            keys_by_batch(0)
            dve.wait_ge(st_tr, 5)
            link(dve.tensor_tensor(SC[:, :, :, :], SC[:, :, :, :],
                                   WSB[:, 8:40].rearrange("p (h b d) -> p h b d", h=HM, d=1).to_broadcast([P, HM, DB, DQ]), ALU.mult))
            link(dve.tensor_tensor(NNAT[:, :, :], NNAT[:, :, :], WS8[:, :].rearrange("p (h d) -> p h d", d=1).to_broadcast([DB, HM, DQ]), ALU.mult))
            for h in range(HM):
                if h + 1 < HM:
                    keys_by_batch(h + 1)
                dve.wait_ge(cu_s, h + 1)
                dve.tensor_tensor(SC[:, h, :, :], SC[:, h, :, :], PS[:, 6 + h % 2, :].rearrange("p (b d) -> p b d", b=DB), ALU.add).then_inc(c_new, 1)
            dve.wait_ge(n_mm, 1)
            dve.tensor_tensor(NNAT[:, :, :], NNAT[:, :, :], PS[0:DB, 3, 0:256].rearrange("p (h d) -> p h d", h=HM), ALU.add).then_inc(c_new, 1)

            def p_maxima(n):
                nk, m = P * (n // HD + 1), 8 * (n % 2)
                dve.wait_ge(p_scores, n + 1)
                ps = PS[:, 2 * (n % 2):2 * (n % 2) + 2, 0:nk]
                link(dve.memset(ps[0:64, :, nk - 64:nk], BIG))
                if n >= 2:
                    dve.wait_ge(p_exp, 2 * (n - 1))
                link(dve.reduce_max(MX[:, m:m + 2], ps, AXX))
                dve.tensor_scalar(MX[:, m + 2:m + 4], MX[:, m:m + 2], -SCALE, None, ALU.mult).then_inc(p_max, 1)

            def p_combine(n):
                nk, m = P * (n // HD + 1), 8 * (n % 2)
                dve.wait_ge(p_exp, 2 * (n + 1))
                link(dve.reciprocal(MX[:, m + 6:m + 8], MX[:, m + 4:m + 6]))
                link(dve.tensor_tensor(MX[:, m + 7:m + 8], MX[:, m + 7:m + 8], LS[:, 4:5], ALU.mult))
                p0, p1 = PR[:, n % 2, 0, 0:nk], PR[:, n % 2, 1, 0:nk]
                link(dve.tensor_scalar(p0, p0, MX[:, m + 6:m + 7], None, ALU.mult))
                dve.scalar_tensor_tensor(p0, p1, MX[:, m + 7:m + 8], p0, ALU.mult, ALU.add).then_inc(p_comb, 1)

            last_n = NTP * HD
            p_maxima(0)
            for n in range(last_n):
                p_combine(n)
                if n + 1 < last_n:
                    p_maxima(n + 1)
                if n in (4, 6):
                    grp_lo(7, (n - 4) // 2)

            def heads_ms(hr, count):
                dve.wait_ge(hd_sq, count)
                link(dve.tensor_scalar(hr, hr, 1.0 / DV, EPS, ALU.mult, ALU.add))
                dve.reciprocal(hr, hr).then_inc(hd_ms, 1)

            def keys_t(b):
                dve.wait_ge(s_ktr, 2 * b + 2)
                if b >= 2:
                    dve.wait_ge(s_scores, b - 1)
                dve.tensor_copy(KCT[b % 2][:, :, P:2 * P], PS[:, 6 * (b % 2) + 1, :].rearrange("p (h t) -> p h t", h=HD)).then_inc(s_ktd, 1)

            keys_t(0)
            for b in range(DB):
                dve.wait_ge(s_scores, b + 1)
                m = 16 + 4 * (b % 2)
                if b >= 2:
                    dve.wait_ge(s_exp, b - 1)
                link(dve.reduce_max(MX[:, m:m + 1], PS[:, 2 + b % 2, 0:PAST + DS], AXX))
                dve.tensor_scalar(MX[:, m + 1:m + 2], MX[:, m:m + 1], -SCALE, None, ALU.mult).then_inc(s_max, 1)
                if b + 1 < DB:
                    keys_t(b + 1)
                dve.wait_ge(s_exp, b + 1)
                link(dve.reciprocal(MX[:, m + 3:m + 4], MX[:, m + 2:m + 3]))
                if b:
                    dve.wait_ge(s_ptr, b)
                dve.tensor_scalar(MR[:, :], CON[:, CSEL:CSEL + P], MX[:, m + 3:m + 4], LS[:, 5:6], ALU.mult, ALU.mult).then_inc(s_mr, 1)
                if b == NTP:
                    heads_ms(HR[:, :, :, :].rearrange("p a t h -> p (a t h)")[:, 0:(NT + NTP) * HM], NT + NTP)
                if b == 1:
                    dve.wait_ge(gate_bc, 2)
                    gate(1)
            for k in range(KT):
                if k == 2:
                    heads_ms(HR[:, 1, NTP, :], 2 * NT)
                    dve.wait_ge(hd_rstd, 3)
                    for h in range(HD):
                        cols = slice(h * DV, (h + 1) * DV)
                        q = dve.scalar_tensor_tensor(HDF[:, NTP, cols], HDF[:, NTP, cols], HR[:, 1, NTP, h:h + 1], GH[:, 512 + h * DV:512 + (h + 1) * DV], ALU.mult, ALU.mult)
                    q.then_inc(heads_s, 1)
                dve.wait_ge(hh_hi, k + 1)
                if k % 4 == 0:
                    dve.tensor_tensor(HTL[:, k:k + 4, SEQ:TOK], PS[:, 7, :].rearrange("p (j t) -> p j t", j=4), HTH[:, k:k + 4, SEQ:TOK].bitcast(F32), ALU.subtract)
                dve.tensor_tensor(HTL[:, k, 0:SEQ], PS[:, 5 + k % 2, :], HTH[:, k, 0:SEQ].bitcast(F32), ALU.subtract).then_inc(hh_lo, 1)

            grp_lo(8, 0)
            y_gated(1, 0)
            grp_lo(8, 1)
            y_gated(1, 1)
            residual(1)
            norm_rows(2)
            norm(2, lambda k: ffn_lo(k - 1, FT) if k in (1, 2) else None)
            ffn_lo(0, FT + 1)
            with dve.Fori(1, FT - 1) as m:
                ffn_act(m - 1, FT + m - 1)
                ffn_lo(1, FT + m)
                ffn_lo(0, FT + m + 1)
            ffn_act(FT - 2, 2 * FT - 2)
            ffn_lo(1, 2 * FT - 1)
            out_lo(0, 0, 2 * OUT_TURNS)
            ffn_act(FT - 1, 2 * FT - 1)
            dve.wait_ge(gate_bc, 4)
            gate(2)
            ffn_out(1)
            residual(2)
        @block.gpsimd
        def _(pool):
            def gate_broadcast(r):
                gp, gs, _ = GATE_BUF[r]
                pool.wait_ge(gate_t, r + 1)
                pool.tensor_copy(gp[:, :, :], GATE[:, :, 0:1].to_broadcast([P, KT, P])).then_inc(gate_bc, 1)
                for k in range(KT):
                    q = pool.tensor_copy(gs[:, k, :].rearrange("p (b s) -> p b s", b=DB),
                                         GATE[:, k, 1:NB].rearrange("p (b s) -> p b s", s=1).to_broadcast([P, DB, DS]))
                q.then_inc(gate_bc, 1)

            gate_broadcast(0)
            k_out = [o["k_prompt"].rearrange("l b (t p) h d -> p (l b t) (h d)", p=P)[:, t, :] for t in range(NTP)]
            k_out.append(o["k_sample"].rearrange("l b s h d -> (l b s) (h d)"))
            v_out = [o["v_prompt"].rearrange("l b (t p) h d -> p (l b t) (h d)", p=P)[:, t, :] for t in range(NTP)]
            v_out.append(o["v_sample"].rearrange("l b s h d -> (l b s) (h d)"))
            for t in range(NT):
                pool.wait_ge(rope_done, NT + t + 1)
                pool.dma_start(k_out[t], DQK[:, (NT + t) % 2, :]).then_inc(k_sent[(NT + t) % 2], 16)
            for t in range(NT):
                pool.wait_ge(g_free, 6 * NT + t + 1)
                pool.dma_start(v_out[t], DVT[:, t, :]).then_inc(kv_out, 16)
            pool.wait_ge(seg_arg, 1)
            with nc.allow_non_contiguous_dma(reason="a few numbers"):
                pool.dma_start(o["m_prompt"].rearrange("l b h -> (l h) b"), WSR[:, 14:15]).then_inc(st_out, 16)
                pool.dma_start(o["m_sample"].rearrange("l b h -> (l h) b"), WSR[:, 16:24]).then_inc(st_out, 16)
            pool.wait_ge(fin_c, 1)
            for a in range(2):
                pool.dma_start(o["C_prompt"].rearrange("l b (j i) v d -> i v (l b j) d", i=2)[a],
                               ST[:, 0:2, 64 * a:64 * a + 64]).then_inc(st_out, 16)
            with nc.allow_non_contiguous_dma(reason="one column"):
                for j in range(2):
                    pool.dma_start(o["n_prompt"].rearrange("l b (j i) d -> j (l b i d)", i=2)[j].rearrange("(a b) -> a b", b=1), CTX[:, j, DV:DV + 1]).then_inc(st_out, 16)
            pool.wait_ge(c_new, HM)
            for h in range(HM):
                pool.dma_start(o["C_sample"].rearrange("l b h v d -> h v (l b) d")[h], SC[:, h, :, :]).then_inc(st_out, 16)
            pool.wait_ge(c_new, HM + 1)
            pool.dma_start(o["n_sample"].rearrange("l b h d -> (l b) (h d)"), NNAT[:, :, :].rearrange("b h d -> b (h d)")).then_inc(st_out, 16)
            pool.wait_ge(st_out, 16 * 11)
            pool.wait_ge(c_new, HM)
            link = chain(pool, poold)
            link(pool.memset(QBD[:, :, :, :], 0.0))
            for h in range(HD):
                for c in range(2):
                    r = slice(64 * c, 64 * c + 64)
                    q = pool.tensor_copy(QBD[r, :, h, 16 * c:16 * c + 16], DQT[r, h, SEQ:TOK].rearrange("p (b q) -> p b q", b=DB))
            q.then_inc(qbd_ready, 1)
            pool.wait_ge(qbd_ready, 1)
            pool.wait_ge(g_lam_landed, 16 * 3)
            for t in range(NT):
                q = pool.tensor_tensor(OG[:, t, :], OG[:, t, :], GH[:, 0:512], ALU.mult)
            link(q)
            for t in range(NT):
                pool.wait_ge(hd_sq, t + 1)
                q = pool.tensor_tensor(HHM[:, t, :], HHM[:, t, :], OG[:, t, :], ALU.mult)
            link(q)
            for t in range(NTP):
                pool.wait_ge(hd_sq, NT + t + 1)
                q = pool.tensor_tensor(HDF[:, t, :], HDF[:, t, :], GH[:, 512:1024], ALU.mult)
            link(q)
            pool.wait_ge(hd_rstd, 2)
            for a, T in enumerate((HHM, HDF)):
                for t in range(NT if a == 0 else NTP):
                    heads4 = T[:, t, :].rearrange("p (h v) -> p h v", h=HM)
                    pool.tensor_tensor(heads4, heads4, HR[:, a, t, :].rearrange("p (h v) -> p h v", v=1).to_broadcast([P, HM, DV]), ALU.mult).then_inc(heads, 1)
            pool.wait_ge(s_scores, DB)
            gate_broadcast(1)
            gate_broadcast(2)
            pool.wait_ge(k_sent[0], 16 * 2)
            pool.wait_ge(k_sent[1], 16 * 3)
            pool.wait_ge(kv_out, 16 * NT)


_INS = ["x_prompt", "x_sample", "cache_k", "cache_v", "state_C", "state_n", "state_m", "c_prompt", "c_sample",
        "w_ada", "b_ada", "g_norm", "w_ffn1_in", "w_ffn1_out", "w_in", "b_igate", "b_fgate", "g_mlstm", "g_diff",
        "lambda_qk", "w_out", "w_ffn2_in", "w_ffn2_out"]
_OUTS = [("y_prompt", (1, SEQ, D)), ("y_sample", (DB, DS, D)),
         ("k_prompt", (1, 1, SEQ, HD, 2 * DQ)), ("v_prompt", (1, 1, SEQ, HD, DV)),
         ("C_prompt", (1, 1, HM, DV, DQ)), ("n_prompt", (1, 1, HM, DQ)), ("m_prompt", (1, 1, HM)),
         ("k_sample", (1, DB, DS, HD, 2 * DQ)), ("v_sample", (1, DB, DS, HD, DV)),
         ("C_sample", (1, DB, HM, DV, DQ)), ("n_sample", (1, DB, HM, DQ)), ("m_sample", (1, DB, HM))]


def kernel(**inputs):
    import numpy as np
    import concourse.bacc as bacc
    from concourse.bass_utils import run_bass_kernel_spmd

    nc = bacc.Bacc("TRN2", target_bir_lowering=False, num_devices=1)
    arrays, ins, outs = {}, {}, {}
    for name in _INS:
        a = np.ascontiguousarray(inputs[name])
        arrays[f"in_{name}"] = a
        ins[name] = nc.dram_tensor(f"in_{name}", a.shape, mybir.dt.from_np(a.dtype), kind="ExternalInput").ap()
    arrays["in_const"] = constants()
    ins["const"] = nc.dram_tensor("in_const", (P, CW), F32, kind="ExternalInput").ap()
    for name, shape in _OUTS:
        outs[name] = nc.dram_tensor(f"out_{name}", shape, F32, kind="ExternalOutput").ap()
    build(nc, ins, outs)
    r = run_bass_kernel_spmd(nc, [arrays], core_ids=[0])
    return tuple(r.results[0][f"out_{name}"] for name, _ in _OUTS)
```
